# Optimizing a Trainium2 kernel written in Bass

```python
import math
import jax
import jax.numpy as jnp
from jax import lax
import numpy as np
import jax, jax.numpy as jnp

D_MODEL = 1024
BATCH = 1
SEQ = 512
DEPTH = 2

GRID_W = 64
CTX_LEN = 256
N_MIXERS = 2
N_HEADS = 8
HEAD_DIM = D_MODEL // N_HEADS
CHUNK = 64
N_GROUPS = 4
EXPERTS_PER_GROUP = 8
N_EXPERTS = N_GROUPS * EXPERTS_PER_GROUP
TOP_K = 2
D_EXPERT = D_MODEL // 2
MOE_BLOCK = 128
N_MOD = 6
EPS = 1e-6


def rmsnorm(x, g):
    xf = x.astype(jnp.float32)
    y = xf * lax.rsqrt(jnp.mean(xf * xf, axis=-1, keepdims=True) + EPS)
    return (y * g.astype(jnp.float32)).astype(x.dtype)

def modulate(x, g, shift, scale):
    return rmsnorm(x, g) * (1 + scale) + shift

def ada_params(cond, w, b):
    m = jax.nn.silu(cond) @ w + b
    return jnp.split(m[..., None, :], N_MOD, axis=-1)

def conv3_seq(x, w):
    xp = jnp.pad(x, ((0, 0), (1, 1), (0, 0)))
    return xp[:, :-2] * w[0] + xp[:, 1:-1] * w[1] + xp[:, 2:] * w[2]

def conv3_grid(x, w, rows):
    b, s, ch = x.shape
    half = ch // 2
    g = x.reshape(b, rows, GRID_W, ch)
    wh, wv = w[:, :half], w[:, half:]
    ph = jnp.pad(g[..., :half], ((0, 0), (0, 0), (1, 1), (0, 0)))
    yh = ph[:, :, :-2] * wh[0] + ph[:, :, 1:-1] * wh[1] + ph[:, :, 2:] * wh[2]
    pv = jnp.pad(g[..., half:], ((0, 0), (1, 1), (0, 0), (0, 0)))
    yv = pv[:, :-2] * wv[0] + pv[:, 1:-1] * wv[1] + pv[:, 2:] * wv[2]
    return jnp.concatenate([yh, yv], axis=-1).reshape(b, s, ch)

def l2norm(t):
    return t * lax.rsqrt(jnp.sum(t * t, axis=-1, keepdims=True) + EPS)

def to_chunks(t):
    b, l, h = t.shape[:3]
    t = t.reshape(b, l // CHUNK, CHUNK, h, *t.shape[3:])
    return jnp.moveaxis(t, (1, 3), (0, 2))

def from_chunks(t):
    t = jnp.moveaxis(t, (0, 2), (1, 3))
    b, n, c, h, d = t.shape
    return t.reshape(b, n * c, h, d)

def gated_delta_scan(q, k, v, g, beta, s0, with_output):
    qc, kc, vc = to_chunks(q), to_chunks(k), to_chunks(v)
    gc = jnp.cumsum(to_chunks(g), axis=-1)
    bc = to_chunks(beta)
    pos = jnp.arange(CHUNK)
    incl = pos[:, None] >= pos[None, :]
    decay = jnp.exp(jnp.where(incl, gc[..., :, None] - gc[..., None, :], -jnp.inf))
    kb = kc * bc[..., None]
    lmat = jnp.where(pos[:, None] > pos[None, :],
                     jnp.einsum('nbhid,nbhjd->nbhij', kb, kc) * decay, 0.0)
    rhs = jnp.concatenate([vc * bc[..., None], kb * jnp.exp(gc)[..., None]], axis=-1)
    sol = lax.linalg.triangular_solve(lmat, rhs, left_side=True, lower=True, unit_diagonal=True)
    dv = vc.shape[-1]
    u, w = sol[..., :dv], sol[..., dv:]
    k_dec = kc * jnp.exp(gc[..., -1:] - gc)[..., None]
    g_last = jnp.exp(gc[..., -1])
    xs = (u, w, k_dec, g_last)
    if with_output:
        xs = xs + (qc * jnp.exp(gc)[..., None], jnp.einsum('nbhid,nbhjd->nbhij', qc, kc) * decay)

    def step(s, inp):
        u_i, w_i, kd_i, gl_i = inp[:4]
        v_new = u_i - jnp.einsum('bhcd,bhde->bhce', w_i, s)
        s_next = s * gl_i[..., None, None] + jnp.einsum('bhcd,bhce->bhde', kd_i, v_new)
        if with_output:
            qd_i, qk_i = inp[4:]
            o = jnp.einsum('bhcd,bhde->bhce', qd_i, s) + jnp.einsum('bhij,bhje->bhie', qk_i, v_new)
            return s_next, o
        return s_next, None

    s_final, o = lax.scan(step, s0, xs)
    return s_final, (from_chunks(o) if with_output else None)

def deltanet_mixer(h_lat, h_ctx, w_in, conv_w, a_log, dt_bias, onorm, w_out, ctx_out):
    d, nh, f32 = D_MODEL, N_HEADS, jnp.float32

    def project(h):
        b, l, _ = h.shape
        p = h @ w_in
        qkv = jax.nn.silu(conv3_seq(p[..., :3 * d], conv_w))
        q, k, v = (t.reshape(b, l, nh, HEAD_DIM).astype(f32) for t in jnp.split(qkv, 3, axis=-1))
        q = l2norm(q) * HEAD_DIM ** -0.5
        k = l2norm(k)
        z = p[..., 3 * d:4 * d]
        beta = jax.nn.sigmoid(p[..., 4 * d:4 * d + 2 * nh].astype(f32)).reshape(b, l, 2, nh)
        a_in = p[..., 4 * d + 2 * nh:].astype(f32).reshape(b, l, 2, nh)
        g = -jnp.exp(a_log.astype(f32)) * jax.nn.softplus(a_in + dt_bias.astype(f32))
        return q, k, v, z, beta, g

    def bidir(q, k, v, beta, g, s_f, s_b, with_output):
        flip = lambda t: t[:, ::-1]
        rf = gated_delta_scan(q, k, v, g[:, :, 0], beta[:, :, 0], s_f, with_output)
        rb = gated_delta_scan(flip(q), flip(k), flip(v), flip(g[:, :, 1]), flip(beta[:, :, 1]),
                              s_b, with_output)
        return rf, rb

    def finish(o, z):
        b, l = z.shape[:2]
        o = o * lax.rsqrt(jnp.mean(o * o, axis=-1, keepdims=True) + EPS) * onorm.astype(f32)
        y = o.astype(z.dtype) * jax.nn.silu(z).reshape(b, l, nh, HEAD_DIM)
        return y.reshape(b, l, d) @ w_out

    qc, kc, vc, zc, bc, gc = project(h_ctx)
    s_zero = jnp.zeros((h_ctx.shape[0], nh, HEAD_DIM, HEAD_DIM), f32)
    (sf, ocf), (sb, ocb) = bidir(qc, kc, vc, bc, gc, s_zero, s_zero, ctx_out)
    y_ctx = finish(ocf + ocb[:, ::-1], zc) if ctx_out else None
    ql, kl, vl, zl, bl, gl = project(h_lat)
    (_, olf), (_, olb) = bidir(ql, kl, vl, bl, gl, sf, sb, True)
    y_lat = finish(olf + olb[:, ::-1], zl)
    return y_lat, y_ctx

def shortconv_mixer(h, w_in, conv_w, w_out, rows):
    gate_b, gate_c, hx = jnp.split(h @ w_in, 3, axis=-1)
    u = gate_c * hx
    y = conv3_grid(u, conv_w, rows) if rows is not None else conv3_seq(u, conv_w)
    return (gate_b * y) @ w_out

def hier_moe(h, router_g, router_e, w1, w3, w2):
    f32 = jnp.float32
    t, d = h.shape
    hf = h.astype(f32)
    pg = jax.nn.softmax(hf @ router_g.astype(f32), axis=-1)
    gi = jnp.argmax(pg, axis=-1).astype(jnp.int32)
    pg_sel = jnp.take_along_axis(pg, gi[:, None], axis=-1)
    le = (hf @ router_e.astype(f32)).reshape(t, N_GROUPS, EXPERTS_PER_GROUP)
    le_sel = jnp.take_along_axis(le, gi[:, None, None], axis=1)[:, 0]
    pk, ik = lax.top_k(jax.nn.softmax(le_sel, axis=-1), TOP_K)
    wts = pg_sel * pk / jnp.sum(pk, axis=-1, keepdims=True)
    eid = gi[:, None] * EXPERTS_PER_GROUP + ik.astype(jnp.int32)

    n = t * TOP_K
    n_blocks = -(-n // MOE_BLOCK) + N_EXPERTS
    cap = n_blocks * MOE_BLOCK
    flat_e = eid.reshape(-1)
    flat_tok = jnp.repeat(jnp.arange(t, dtype=jnp.int32), TOP_K)
    flat_w = wts.reshape(-1)
    order = jnp.argsort(flat_e)
    se = flat_e[order]
    counts = jnp.zeros((N_EXPERTS,), jnp.int32).at[flat_e].add(1)
    padded = (counts + MOE_BLOCK - 1) // MOE_BLOCK * MOE_BLOCK
    ends_pad = jnp.cumsum(padded)
    start_pad = ends_pad - padded
    start_raw = jnp.cumsum(counts) - counts
    dest = start_pad[se] + jnp.arange(n, dtype=jnp.int32) - start_raw[se]
    buf_tok = jnp.full((cap,), t, jnp.int32).at[dest].set(flat_tok[order])
    buf_w = jnp.zeros((cap,), f32).at[dest].set(flat_w[order])
    block_e = jnp.minimum(
        jnp.searchsorted(ends_pad, jnp.arange(n_blocks, dtype=jnp.int32) * MOE_BLOCK, side='right'),
        N_EXPERTS - 1).astype(jnp.int32)
    h_pad = jnp.concatenate([h, jnp.zeros((1, d), h.dtype)], axis=0)
    xb = h_pad[buf_tok].reshape(n_blocks, MOE_BLOCK, d)

    def expert_block(args):
        xi, e = args
        return (jax.nn.silu(xi @ w1[e]) * (xi @ w3[e])) @ w2[e]

    yb = lax.map(expert_block, (xb, block_e)).reshape(cap, d)
    y = jax.ops.segment_sum(yb * buf_w[:, None].astype(yb.dtype), buf_tok, num_segments=t + 1)
    return y[:t]

def first_inputs(seed: int = 0) -> dict:
    key = jax.random.key(seed)
    ks = jax.random.split(key, 24)
    d, nh, f32 = D_MODEL, N_HEADS, jnp.float32
    n_a = (DEPTH + N_MIXERS - 1) // N_MIXERS
    n_b = DEPTH // N_MIXERS

    def nrm(k, shape, scale):
        return jax.random.normal(k, shape, f32) * scale

    dt = jnp.exp(jax.random.uniform(ks[10], (n_a, 2, nh), f32, math.log(1e-3), math.log(1e-1)))
    return {
        'x': nrm(ks[0], (BATCH, SEQ, d), 1.0),
        'c': nrm(ks[1], (BATCH, d), 1.0),
        'ctx': nrm(ks[2], (BATCH, CTX_LEN, d), 1.0),
        'c_ctx': nrm(ks[3], (d,), 1.0),
        'ada_w': nrm(ks[4], (DEPTH, d, N_MOD * d), 0.5 * d ** -0.5),
        'ada_b': nrm(ks[5], (DEPTH, N_MOD * d), 0.02),
        'norm_mix': 1.0 + nrm(ks[6], (DEPTH, d), 0.05),
        'norm_ffn': 1.0 + nrm(ks[7], (DEPTH, d), 0.05),
        'w_in_a': nrm(ks[8], (n_a, d, 4 * d + 4 * nh), d ** -0.5),
        'conv_a': nrm(ks[9], (n_a, 3, 3 * d), 3 ** -0.5),
        'a_log_a': jnp.log(jax.random.uniform(ks[11], (n_a, 2, nh), f32, 1.0, 16.0)),
        'dt_bias_a': dt + jnp.log(-jnp.expm1(-dt)),
        'onorm_a': 1.0 + nrm(ks[12], (n_a, HEAD_DIM), 0.05),
        'w_out_a': nrm(ks[13], (n_a, d, d), d ** -0.5),
        'w_in_b': nrm(ks[14], (n_b, d, 3 * d), d ** -0.5),
        'conv_b': nrm(ks[15], (n_b, 3, d), 3 ** -0.5),
        'w_out_b': nrm(ks[16], (n_b, d, d), d ** -0.5),
        'router_g': nrm(ks[17], (DEPTH, d, N_GROUPS), d ** -0.5),
        'router_e': nrm(ks[18], (DEPTH, d, N_EXPERTS), d ** -0.5),
        'w1': nrm(ks[19], (DEPTH, N_EXPERTS, d, D_EXPERT), d ** -0.5),
        'w3': nrm(ks[20], (DEPTH, N_EXPERTS, d, D_EXPERT), d ** -0.5),
        'w2': nrm(ks[21], (DEPTH, N_EXPERTS, D_EXPERT, d), D_EXPERT ** -0.5),
        'final_norm': 1.0 + nrm(ks[22], (d,), 0.05),
    }

def first_block(x, c, ctx, c_ctx, ada_w, ada_b, norm_mix, norm_ffn,
              w_in_a, conv_a, a_log_a, dt_bias_a, onorm_a, w_out_a,
              w_in_b, conv_b, w_out_b, router_g, router_e, w1, w3, w2, final_norm):
    b, s, d = x.shape
    rows = s // GRID_W
    kinds = [i % N_MIXERS for i in range(DEPTH)]
    for i in range(DEPTH):
        kind, j = kinds[i], i // N_MIXERS
        ctx_live = 0 in kinds[i + 1:]
        sh_m, sc_m, gt_m, sh_f, sc_f, gt_f = ada_params(c, ada_w[i], ada_b[i])
        if kind == 0 or ctx_live:
            csh_m, csc_m, cgt_m, csh_f, csc_f, cgt_f = ada_params(c_ctx, ada_w[i], ada_b[i])
            hc = modulate(ctx, norm_mix[i], csh_m, csc_m)
        h = modulate(x, norm_mix[i], sh_m, sc_m)
        if kind == 0:
            y, yc = deltanet_mixer(h, hc, w_in_a[j], conv_a[j], a_log_a[j], dt_bias_a[j],
                                   onorm_a[j], w_out_a[j], ctx_live)
        else:
            y = shortconv_mixer(h, w_in_b[j], conv_b[j], w_out_b[j], rows)
            yc = shortconv_mixer(hc, w_in_b[j], conv_b[j], w_out_b[j], None) if ctx_live else None
        x = x + gt_m * y
        hf = modulate(x, norm_ffn[i], sh_f, sc_f).reshape(b * s, d)
        if ctx_live:
            ctx = ctx + cgt_m * yc
            hcf = modulate(ctx, norm_ffn[i], csh_f, csc_f).reshape(-1, d)
            out = hier_moe(jnp.concatenate([hf, hcf], axis=0), router_g[i], router_e[i],
                           w1[i], w3[i], w2[i])
            x = x + gt_f * out[:b * s].reshape(b, s, d)
            ctx = ctx + cgt_f * out[b * s:].reshape(ctx.shape)
        else:
            x = x + gt_f * hier_moe(hf, router_g[i], router_e[i], w1[i], w3[i], w2[i]).reshape(b, s, d)
    return rmsnorm(x, final_norm)


DEPTH_2 = 1

D_MIX = D_MODEL
HG_HEADS = 4
HG_DK = 128
HG_DV = 128
HG_WIDTH = HG_HEADS * HG_DV
HG_CHUNK = 64
NSA_HEADS = 8
NSA_KV_GROUPS = 2
NSA_HD = 64
NSA_WIDTH = NSA_HEADS * NSA_HD
NSA_KV = NSA_KV_GROUPS * NSA_HD
CMP_BLOCK = 32
CMP_STRIDE = 16
CMP_HIDDEN = 256
SEL_BLOCK = 64
N_SEL = 16
WINDOW = 512
Q_BLOCK = 128
ROPE_THETA = 10000.0
N_EXPERTS_2 = 64
TOP_K_2 = 8
N_GROUPS_2 = 8
TOPK_GROUPS = 4
EXPERT_HIDDEN = 256
SHARED_HIDDEN = 256
ROUTED_SCALE = 2.5
EXPERT_BLOCK = 128
IN_SPLITS = (HG_WIDTH,) * 4 + (NSA_WIDTH,) + (NSA_KV,) * 6 + (3 * NSA_HEADS,)
IN_COLS = 4 * HG_WIDTH + NSA_WIDTH + 6 * NSA_KV + 3 * NSA_HEADS


def rmsnorm_2(x, g):
    xf = x.astype(jnp.float32)
    y = xf * lax.rsqrt(jnp.mean(xf * xf, axis=-1, keepdims=True) + EPS)
    return (y * g.astype(jnp.float32)).astype(x.dtype)

def rope(t, pos):
    half = t.shape[-1] // 2
    inv = ROPE_THETA ** (-jnp.arange(half, dtype=jnp.float32) / half)
    ang = pos.astype(jnp.float32)[:, None] * inv[None, :]
    cos, sin = jnp.cos(ang), jnp.sin(ang)
    t1 = t[..., :half].astype(jnp.float32)
    t2 = t[..., half:].astype(jnp.float32)
    return jnp.concatenate([t1 * cos - t2 * sin, t2 * cos + t1 * sin], axis=-1).astype(t.dtype)

def swiglu(t, w_gu, w_dn):
    g, u = jnp.split(t @ w_gu, 2, axis=-1)
    return (jax.nn.silu(g) * u) @ w_dn

def hgrn2_mixer(q, f_logit, i, gate, lb, norm_g):
    B, S, _ = q.shape
    f32 = jnp.float32
    f = lb + (1.0 - lb) * jax.nn.sigmoid(f_logit.astype(f32))
    log_f = jnp.log(f)
    k = 1.0 - f
    n_ch = S // HG_CHUNK

    def to_chunks(t, d):
        return t.reshape(B, n_ch, HG_CHUNK, HG_HEADS, d).transpose(1, 0, 3, 2, 4)

    qc = to_chunks(q.astype(f32) * HG_DK ** -0.5, HG_DK)
    kc = to_chunks(k, HG_DK)
    vc = to_chunks(i.astype(f32), HG_DV)
    bc = jnp.cumsum(to_chunks(log_f, HG_DK), axis=3)
    causal = jnp.tril(jnp.ones((HG_CHUNK, HG_CHUNK), bool))

    def step(state, inp):
        q_, k_, v_, b_ = inp
        diff = jnp.where(causal[:, :, None], b_[:, :, :, None, :] - b_[:, :, None, :, :], -jnp.inf)
        a = jnp.einsum('bhtd,bhtsd,bhsd->bhts', q_, jnp.exp(diff), k_)
        o = a @ v_ + jnp.einsum('bhtd,bhde->bhte', q_ * jnp.exp(b_), state)
        b_last = b_[:, :, -1]
        state = jnp.exp(b_last)[..., None] * state + jnp.einsum(
            'bhsd,bhse->bhde', k_ * jnp.exp(b_last[:, :, None, :] - b_), v_)
        return state, o

    s0 = jnp.zeros((B, HG_HEADS, HG_DK, HG_DV), f32)
    _, o = lax.scan(step, s0, (qc, kc, vc, bc))
    o = o.transpose(1, 0, 3, 2, 4).reshape(B, S, HG_HEADS, HG_DV)
    o = o * lax.rsqrt(jnp.mean(o * o, axis=-1, keepdims=True) + EPS) * norm_g.astype(f32).reshape(HG_HEADS, HG_DV)
    o = o.reshape(B, S, HG_WIDTH) * jax.nn.silu(gate.astype(f32))
    return o.astype(q.dtype)

def nsa_mixer(q, kc, vc, ks, vs, kw, vw, gate_logit,
              pos_k, w1_k, b1_k, w2_k, pos_v, w1_v, b1_v, w2_v):
    B, S, _ = q.shape
    G, HG, HD = NSA_KV_GROUPS, NSA_HEADS // NSA_KV_GROUPS, NSA_HD
    f32 = jnp.float32
    pos = jnp.arange(S)
    scale = HD ** -0.5
    qh = q.reshape(B, S, G, HG, HD).transpose(0, 2, 3, 1, 4)
    q_rot = rope(qh, pos)

    def kv_heads(t):
        return t.reshape(B, S, G, HD).transpose(0, 2, 1, 3)

    n_cmp = (S - CMP_BLOCK) // CMP_STRIDE + 1
    tok_idx = jnp.arange(n_cmp)[:, None] * CMP_STRIDE + jnp.arange(CMP_BLOCK)[None, :]

    def compress(t, pe, w1, b1, w2):
        blocks = kv_heads(t)[:, :, tok_idx] + pe
        hdn = jax.nn.gelu(blocks.reshape(B, G, n_cmp, CMP_BLOCK * HD) @ w1 + b1)
        return hdn @ w2

    k_cmp = compress(kc, pos_k, w1_k, b1_k, w2_k)
    v_cmp = compress(vc, pos_v, w1_v, b1_v, w2_v)
    s_cmp = jnp.einsum('bghsd,bgcd->bghsc', qh, k_cmp).astype(f32) * scale
    c_start = jnp.arange(n_cmp) * CMP_STRIDE
    cmp_mask = (c_start + CMP_BLOCK - 1)[None, :] <= pos[:, None]
    p_cmp = jax.nn.softmax(jnp.where(cmp_mask, s_cmp, -1e30), axis=-1) * cmp_mask
    o_cmp = jnp.einsum('bghsc,bgcd->bghsd', p_cmp, v_cmp.astype(f32))

    n_sb = S // SEL_BLOCK
    n_sel = min(N_SEL, n_sb)
    s_start = jnp.arange(n_sb) * SEL_BLOCK
    overlap = jnp.clip(jnp.minimum(c_start[:, None] + CMP_BLOCK, s_start[None, :] + SEL_BLOCK)
                       - jnp.maximum(c_start[:, None], s_start[None, :]), 0, None).astype(f32) / CMP_BLOCK
    p_slc = jnp.einsum('bghsc,cj->bgsj', p_cmp, overlap)
    cur = pos // SEL_BLOCK
    blk = jnp.arange(n_sb)
    available = blk[None, :] <= cur[:, None]
    forced = (blk[None, :] == 0) | (blk[None, :] == cur[:, None]) | (blk[None, :] == cur[:, None] - 1)
    sel_score = jnp.where(forced, 1e30, jnp.where(available, p_slc, -1e30))
    top_val, top_idx = lax.top_k(sel_score, n_sel)
    top_valid = top_val > -1e29

    n_qb = S // Q_BLOCK
    k_blocks = rope(kv_heads(ks), pos).reshape(B, G, n_sb, SEL_BLOCK * HD)
    v_blocks = kv_heads(vs).reshape(B, G, n_sb, SEL_BLOCK * HD)
    bi = jnp.arange(B)[:, None, None]
    gi = jnp.arange(G)[None, :, None]

    def by_qblock(t, axis):
        shape = t.shape[:axis] + (n_qb, Q_BLOCK) + t.shape[axis + 1:]
        return jnp.moveaxis(t.reshape(shape), axis, 0)

    def slc_block(args):
        qb, idx, valid, qpos = args
        flat = idx.reshape(B, G, Q_BLOCK * n_sel)
        kg = k_blocks[bi, gi, flat].reshape(B, G, Q_BLOCK, n_sel, SEL_BLOCK, HD)
        vg = v_blocks[bi, gi, flat].reshape(B, G, Q_BLOCK, n_sel, SEL_BLOCK, HD)
        s = jnp.einsum('bghqd,bgqnld->bghqnl', qb, kg).astype(f32) * scale
        kpos = idx[..., None] * SEL_BLOCK + jnp.arange(SEL_BLOCK)
        ok = valid[..., None] & (kpos <= qpos[:, None, None])
        s = jnp.where(ok[:, :, None], s, -1e30).reshape(B, G, HG, Q_BLOCK, n_sel * SEL_BLOCK)
        p = jax.nn.softmax(s, axis=-1).reshape(B, G, HG, Q_BLOCK, n_sel, SEL_BLOCK)
        return jnp.einsum('bghqnl,bgqnld->bghqd', p, vg.astype(f32))

    o_slc = lax.map(slc_block, (by_qblock(q_rot, 3), by_qblock(top_idx, 2),
                                by_qblock(top_valid, 2), pos.reshape(n_qb, Q_BLOCK)))
    o_slc = jnp.moveaxis(o_slc, 0, 3).reshape(B, G, HG, S, HD)

    n_back = WINDOW // Q_BLOCK

    def banded(t):
        tp = jnp.pad(t, ((0, 0), (0, 0), (WINDOW, 0), (0, 0))).reshape(B, G, n_qb + n_back, Q_BLOCK, HD)
        return jnp.concatenate([tp[:, :, o:o + n_qb] for o in range(n_back + 1)], axis=3)

    kwb = banded(rope(kv_heads(kw), pos))
    vwb = banded(kv_heads(vw))
    qw = q_rot.reshape(B, G, HG, n_qb, Q_BLOCK, HD)
    s_w = jnp.einsum('bghnqd,bgnkd->bghnqk', qw, kwb).astype(f32) * scale
    qpos = pos.reshape(n_qb, Q_BLOCK)
    kpos = (jnp.arange(n_qb)[:, None] - n_back) * Q_BLOCK + jnp.arange((n_back + 1) * Q_BLOCK)[None, :]
    d = qpos[:, :, None] - kpos[:, None, :]
    ok_w = (d >= 0) & (d < WINDOW) & (kpos[:, None, :] >= 0)
    p_w = jax.nn.softmax(jnp.where(ok_w, s_w, -1e30), axis=-1)
    o_win = jnp.einsum('bghnqk,bgnkd->bghnqd', p_w, vwb.astype(f32)).reshape(B, G, HG, S, HD)

    gates = jax.nn.sigmoid(gate_logit.astype(f32)).reshape(B, S, G, HG, 3).transpose(0, 2, 3, 1, 4)
    o = gates[..., 0:1] * o_cmp + gates[..., 1:2] * o_slc + gates[..., 2:3] * o_win
    return o.transpose(0, 3, 1, 2, 4).reshape(B, S, NSA_WIDTH).astype(q.dtype)

def routed_experts(t, top_i, top_w, w_gu, w_dn):
    T, D = t.shape
    A = T * TOP_K_2
    e_flat = top_i.reshape(A).astype(jnp.int32)
    w_flat = top_w.reshape(A).astype(jnp.float32)
    order = jnp.argsort(e_flat)
    e_sorted = e_flat[order]
    tok_sorted = (order // TOP_K_2).astype(jnp.int32)
    counts = jnp.bincount(e_flat, length=N_EXPERTS_2)
    start = jnp.cumsum(counts) - counts
    padded = (counts + EXPERT_BLOCK - 1) // EXPERT_BLOCK * EXPERT_BLOCK
    pad_end = jnp.cumsum(padded)
    pad_start = pad_end - padded
    dest = pad_start[e_sorted] + jnp.arange(A) - start[e_sorted]
    n_blk = -(-A // EXPERT_BLOCK) + N_EXPERTS_2
    P = n_blk * EXPERT_BLOCK
    rows = jnp.full((P,), T, jnp.int32).at[dest].set(tok_sorted)
    wts = jnp.zeros((P,), jnp.float32).at[dest].set(w_flat[order])
    blk_expert = jnp.minimum(jnp.searchsorted(pad_end, jnp.arange(n_blk) * EXPERT_BLOCK, side='right'),
                             N_EXPERTS_2 - 1)
    t_pad = jnp.concatenate([t, jnp.zeros((1, D), t.dtype)], axis=0)

    def one_block(args):
        rb, e = args
        return swiglu(t_pad[rb], w_gu[e], w_dn[e]).astype(jnp.float32)

    ys = lax.map(one_block, (rows.reshape(n_blk, EXPERT_BLOCK), blk_expert)).reshape(P, D)
    out = jnp.zeros((T + 1, D), jnp.float32).at[rows].add(ys * wts[:, None])
    return out[:T]

def moe_ffn(h, router_w, router_bias, w_gu, w_dn, w_sh_gu, w_sh_dn):
    B, S, D = h.shape
    t = h.reshape(B * S, D)
    scores = jax.nn.sigmoid((t @ router_w).astype(jnp.float32))
    choice = scores + router_bias.astype(jnp.float32)
    grp = choice.reshape(B * S, N_GROUPS_2, N_EXPERTS_2 // N_GROUPS_2)
    grp_score = lax.top_k(grp, 2)[0].sum(-1)
    top_g = lax.top_k(grp_score, TOPK_GROUPS)[1]
    gmask = jnp.any(top_g[..., None] == jnp.arange(N_GROUPS_2), axis=-2)
    emask = jnp.repeat(gmask, N_EXPERTS_2 // N_GROUPS_2, axis=-1)
    top_i = lax.top_k(jnp.where(emask, choice, -jnp.inf), TOP_K_2)[1]
    top_w = jnp.take_along_axis(scores, top_i, axis=-1)
    top_w = top_w / jnp.sum(top_w, axis=-1, keepdims=True) * ROUTED_SCALE
    routed = routed_experts(t, top_i, top_w, w_gu, w_dn)
    shared = swiglu(t, w_sh_gu, w_sh_dn).astype(jnp.float32)
    return (routed + shared).reshape(B, S, D).astype(h.dtype)

def second_inputs(seed: int = 0) -> dict:
    key = jax.random.key(seed)
    ks = jax.random.split(key, 26)
    L = DEPTH_2

    def nrm(k, shape, s):
        return jax.random.normal(k, shape, jnp.float32) * s

    return {
        "x": nrm(ks[0], (BATCH, SEQ, D_MODEL), 1.0),
        "c": nrm(ks[1], (BATCH, D_MODEL), 1.0),
        "w_ada": nrm(ks[2], (L, D_MODEL, 6 * D_MODEL), 0.5 * D_MODEL ** -0.5),
        "b_ada": nrm(ks[3], (L, 6 * D_MODEL), 0.02),
        "norm1_g": 1.0 + nrm(ks[4], (L, D_MODEL), 0.02),
        "w_in": nrm(ks[5], (L, D_MODEL, IN_COLS), D_MODEL ** -0.5),
        "hg_lb_logits": nrm(ks[6], (L + 1, HG_WIDTH), 0.5),
        "hg_norm_g": 1.0 + nrm(ks[7], (L, HG_WIDTH), 0.02),
        "cmp_pos_k": nrm(ks[8], (L, CMP_BLOCK, NSA_HD), 0.1),
        "cmp_w1_k": nrm(ks[9], (L, CMP_BLOCK * NSA_HD, CMP_HIDDEN), (CMP_BLOCK * NSA_HD) ** -0.5),
        "cmp_b1_k": nrm(ks[10], (L, CMP_HIDDEN), 0.02),
        "cmp_w2_k": nrm(ks[11], (L, CMP_HIDDEN, NSA_HD), CMP_HIDDEN ** -0.5),
        "cmp_pos_v": nrm(ks[12], (L, CMP_BLOCK, NSA_HD), 0.1),
        "cmp_w1_v": nrm(ks[13], (L, CMP_BLOCK * NSA_HD, CMP_HIDDEN), (CMP_BLOCK * NSA_HD) ** -0.5),
        "cmp_b1_v": nrm(ks[14], (L, CMP_HIDDEN), 0.02),
        "cmp_w2_v": nrm(ks[15], (L, CMP_HIDDEN, NSA_HD), CMP_HIDDEN ** -0.5),
        "w_out": nrm(ks[16], (L, D_MIX, D_MODEL), D_MIX ** -0.5),
        "norm2_g": 1.0 + nrm(ks[17], (L, D_MODEL), 0.02),
        "router_w": nrm(ks[18], (L, D_MODEL, N_EXPERTS_2), D_MODEL ** -0.5),
        "router_bias": nrm(ks[19], (L, N_EXPERTS_2), 0.01),
        "w_exp_gu": nrm(ks[20], (L, N_EXPERTS_2, D_MODEL, 2 * EXPERT_HIDDEN), D_MODEL ** -0.5),
        "w_exp_dn": nrm(ks[21], (L, N_EXPERTS_2, EXPERT_HIDDEN, D_MODEL), EXPERT_HIDDEN ** -0.5),
        "w_sh_gu": nrm(ks[22], (L, D_MODEL, 2 * SHARED_HIDDEN), D_MODEL ** -0.5),
        "w_sh_dn": nrm(ks[23], (L, SHARED_HIDDEN, D_MODEL), SHARED_HIDDEN ** -0.5),
        "final_g": 1.0 + nrm(ks[24], (D_MODEL,), 0.02),
    }

def second_block(x, c, w_ada, b_ada, norm1_g, w_in, hg_lb_logits, hg_norm_g,
              cmp_pos_k, cmp_w1_k, cmp_b1_k, cmp_w2_k, cmp_pos_v, cmp_w1_v, cmp_b1_v, cmp_w2_v,
              w_out, norm2_g, router_w, router_bias, w_exp_gu, w_exp_dn, w_sh_gu, w_sh_dn, final_g):
    offsets = np.cumsum(IN_SPLITS)[:-1].tolist()
    lb_all = jnp.cumsum(jax.nn.softmax(hg_lb_logits.astype(jnp.float32), axis=0), axis=0)
    c_act = jax.nn.silu(c)
    for l in range(DEPTH_2):
        mod = (c_act @ w_ada[l] + b_ada[l])[:, None, :]
        sh1, sc1, g1, sh2, sc2, g2 = jnp.split(mod, 6, axis=-1)
        h = rmsnorm_2(x, norm1_g[l]) * (1.0 + sc1) + sh1
        hq, hf, hi, hgt, nq, kc, vc, ksl, vsl, kwn, vwn, ngate = jnp.split(h @ w_in[l], offsets, axis=-1)
        o_hg = hgrn2_mixer(hq, hf, hi, hgt, lb_all[l], hg_norm_g[l])
        o_nsa = nsa_mixer(nq, kc, vc, ksl, vsl, kwn, vwn, ngate,
                          cmp_pos_k[l], cmp_w1_k[l], cmp_b1_k[l], cmp_w2_k[l],
                          cmp_pos_v[l], cmp_w1_v[l], cmp_b1_v[l], cmp_w2_v[l])
        x = x + g1 * (jnp.concatenate([o_hg, o_nsa], axis=-1) @ w_out[l])
        h = rmsnorm_2(x, norm2_g[l]) * (1.0 + sc2) + sh2
        x = x + g2 * moe_ffn(h, router_w[l], router_bias[l], w_exp_gu[l], w_exp_dn[l], w_sh_gu[l], w_sh_dn[l])
    return rmsnorm_2(x, final_g)


def setup_inputs(seed=0):
    out = dict(first_inputs(seed))
    for name, value in second_inputs(seed + 1).items():
        if name != "x":
            out[name + "_2"] = value
    return out


def reference(
    x, c, ctx, c_ctx, ada_w, ada_b, norm_mix, norm_ffn, w_in_a, conv_a, a_log_a, dt_bias_a,
    onorm_a, w_out_a, w_in_b, conv_b, w_out_b, router_g, router_e, w1, w3, w2, final_norm, c_2,
    w_ada_2, b_ada_2, norm1_g_2, w_in_2, hg_lb_logits_2, hg_norm_g_2, cmp_pos_k_2, cmp_w1_k_2,
    cmp_b1_k_2, cmp_w2_k_2, cmp_pos_v_2, cmp_w1_v_2, cmp_b1_v_2, cmp_w2_v_2, w_out_2, norm2_g_2,
    router_w_2, router_bias_2, w_exp_gu_2, w_exp_dn_2, w_sh_gu_2, w_sh_dn_2, final_g_2,
):
    x = first_block(
        x, c, ctx, c_ctx, ada_w, ada_b, norm_mix, norm_ffn, w_in_a, conv_a, a_log_a, dt_bias_a,
        onorm_a, w_out_a, w_in_b, conv_b, w_out_b, router_g, router_e, w1, w3, w2, final_norm,
    )
    return second_block(
        x, c_2, w_ada_2, b_ada_2, norm1_g_2, w_in_2, hg_lb_logits_2, hg_norm_g_2, cmp_pos_k_2,
        cmp_w1_k_2, cmp_b1_k_2, cmp_w2_k_2, cmp_pos_v_2, cmp_w1_v_2, cmp_b1_v_2, cmp_w2_v_2,
        w_out_2, norm2_g_2, router_w_2, router_bias_2, w_exp_gu_2, w_exp_dn_2, w_sh_gu_2,
        w_sh_dn_2, final_g_2,
    )


_drawn_inputs = setup_inputs


def setup_inputs(seed=0):
    import zlib

    import numpy as np

    out = dict(_drawn_inputs(seed))
    spreads = {}
    factors = {'norm1_g_2': 3.087,
     'hg_norm_g_2': 12.138,
     'cmp_pos_k_2': 8.0,
     'cmp_b1_k_2': 43.41,
     'cmp_pos_v_2': 10.797,
     'cmp_b1_v_2': 46.333,
     'final_g_2': 7.933,
     'norm2_g_2': 3.84,
     'router_bias_2': 2.84}
    for name, (base, spread) in spreads.items():
        noise = np.random.default_rng([zlib.crc32(name.encode()), seed]).standard_normal(out[name].shape)
        drawn = base * np.exp(spread * noise) if base else spread * noise
        out[name] = jnp.asarray(drawn.astype(out[name].dtype))
    for name, factor in factors.items():
        out[name] = (out[name] * factor).astype(out[name].dtype)
    return out
```

```python
from contextlib import ExitStack
from collections import namedtuple

import numpy as np
import concourse.bass as bass
from concourse import mybir

ALU = mybir.AluOpType
ACT = mybir.ActivationFunctionType
F32 = mybir.dt.float32
U32 = mybir.dt.uint32
AX_X = mybir.AxisListType.X

P = 128
D = 1024
KD = D // P
T = 512
NT = T // P
CT = 256
NCT = CT // P
EPS = 1e-6
NEG = -1e30
SLOTS = 3
SLOT = KD * 512
HEADS = 8
E1, F1 = 32, 512
E2, F2 = 64, 256
W_IN2 = 3352


def base_masks():
    i = np.arange(P)
    return np.stack([np.eye(P), np.ones((P, P))], 1).astype(np.float32)


def delta_masks():
    r, c = np.arange(P)[:, None], np.arange(P)[None, :]
    out = [r <= c, r >= c]
    neg = [np.where(ok, 0.0, NEG) for ok in (c < r, c > r, c >= r, c <= r)]
    levels = []
    for n in (1, 2, 4, 8, 16, 32, 64):
        levels.append((r // (2 * n) == c // (2 * n)) & (r % (2 * n) >= n) & (c % (2 * n) < n))
    levels += [m.T for m in levels]
    return np.stack([np.asarray(m, np.float32) for m in out + neg + levels], 1)


def mix_masks():
    p = np.arange(P)
    r, c = p[:, None], p[None, :]
    half = 32
    inv = 10000.0 ** (-np.arange(half, dtype=np.float32) / half)
    ang = np.arange(T, dtype=np.float32)[None, :] * inv.astype(np.float32)[p % half][:, None]
    cos, sin = np.cos(ang), np.sin(ang)
    rot = np.where(c % 64 < half, -(r == c + half).astype(np.float32), (r == c - half).astype(np.float32))
    dup = [(r == g * 64 + c % 64) for g in range(2)]
    block = np.arange(31)
    pos = np.arange(T).reshape(NT, P).T
    ok = (block[None, None, :] * 16 + 31) <= pos[:, :, None]
    local = np.arange(16)
    shift = (p[:, None, None] % 16 - local[None, None, :]) == local[None, :, None]
    chunk = (p[:, None] // 16) == np.arange(8)[None, :]
    spread = np.repeat(chunk, 16, axis=1)
    notstart = np.tile(np.arange(16) != 0, (P, 1))
    start = np.tile(np.arange(16) == 0, (P, 1))
    notend = np.tile(np.arange(16) != 15, (P, 1))
    parts = [("cos", cos), ("sin", sin), ("rot", rot), ("dup0", dup[0]), ("dup1", dup[1]),
             ("causal", np.where(c <= r, 0.0, NEG)),
             ("cneg", np.where(ok, 0.0, NEG).reshape(P, -1)), ("cok", ok.reshape(P, -1)),
             ("shift", shift.reshape(P, -1)), ("chunk", chunk), ("spread", spread),
             ("notstart", notstart), ("start", start), ("notend", notend)]
    where, at = {}, 0
    for name, a in parts:
        where[name] = (at, a.shape[1])
        at += a.shape[1]
    return np.concatenate([np.asarray(a, np.float32) for _, a in parts], 1), where


def column(ap, n, width):
    return ap.unsqueeze(2).to_broadcast([ap.shape[0], n, width])


def across(ap, n):
    return ap.unsqueeze(1).to_broadcast([ap.shape[0], n, ap.shape[1]])


def flat(ap):
    return ap.rearrange("p a b -> p (a b)")


class Bag:
    pass


class Linked:

    def __init__(self, eng, sem):
        self.eng, self.sem, self.n = eng, sem, 0

    def __call__(self, ins):
        ins.then_inc(self.sem, 1)
        self.n += 1
        self.eng.wait_ge(self.sem, self.n)


class WeightRing:

    def __init__(self, nc, ctx):
        self.buf = ctx.enter_context(nc.sbuf_tensor("weight_ring", [P, SLOTS, SLOT], F32))
        self.loaded = [ctx.enter_context(nc.semaphore(f"weights_loaded{i}")) for i in range(SLOTS)]
        self.freed = [ctx.enter_context(nc.semaphore(f"weights_used{i}")) for i in range(SLOTS)]
        self.tiles = []
        self.sent = 0

    def add(self, dmas):
        self.tiles.append(dmas)
        return len(self.tiles) - 1

    def slot(self, n):
        return self.buf[:, n % SLOTS, :]

    def loads(self, n):
        return 16 * sum(len(self.tiles[i]) for i in range(n % SLOTS, n + 1, SLOTS))

    def uses(self, n):
        return n // SLOTS

    def stream(self, sp, upto):
        while self.sent < min(upto, len(self.tiles)):
            n = self.sent
            if n >= SLOTS:
                sp.wait_ge(self.freed[n % SLOTS], self.uses(n))
            for dst, src in self.tiles[n]:
                sp.dma_start(dst(self.slot(n)), src).then_inc(self.loaded[n % SLOTS], 16)
            self.sent += 1

    def wait(self, pe, n):
        pe.wait_ge(self.loaded[n % SLOTS], self.loads(n))


class Stage:

    def __init__(self, m, name):
        self.m, self.nc, self.name = m, m.nc, name
        self.ctx = ExitStack()
        self.sems = []

    def sb(self, name, shape, dt=F32):
        return self.ctx.enter_context(self.nc.sbuf_tensor(f"{self.name}_{name}", shape, dt))

    def sem(self, names, mark=""):
        new = [self.nc.alloc_semaphore(f"{self.name}{mark}_{n}") for n in names.split()]
        self.sems += new
        return namedtuple("Semaphores", names)(*new)

    def block(self):
        return self.nc.Block()

    def clear(self):
        self.nc.clear_and_free_semaphores(self.sems)
        self.nc.all_engine_barrier()
        self.sems = []

    def close(self):
        self.clear()
        self.ctx.close()


def whole(k, n):
    return lambda s: s[:, 0:k * n].rearrange("p (k n) -> p k n", k=k)


def rows_of(w, c0, n):
    return w[:, c0:c0 + n].rearrange("(k p) n -> p k n", p=P)


def modulation_stage(m, tag, conds, first, bias, after):
    nc, ring = m.nc, m.ring
    st = Stage(m, f"mod{tag}")
    nv = len(conds)
    craw = st.sb("craw", [P, nv, KD])
    csil = st.sb("csil", [P, nv, KD])
    wide = st.sb("wide", [P, nv, KD, P])
    s = st.sem("vector_in bias_in silu wide product added")
    units = [(n, v) for n in range(6 * D // 512) for v in range(nv) if n < conds[v][2]]
    with st.block() as block:
        @block.sync
        def _(sp):
            for v, (c, _, _) in enumerate(conds):
                sp.dma_start(craw[:, v, :], c.rearrange("(k p) -> p k", p=P),
                             allow_slow_non_contiguous=True).then_inc(s.vector_in, 16)
            ring.stream(sp, first + 1)
            for v, (_, dst, blocks) in enumerate(conds):
                sp.dma_start(dst[:, 0:blocks * 512],
                             bias[0:blocks * 512].partition_broadcast(P)).then_inc(s.bias_in, 16)
            ring.stream(sp, after)

        @block.scalar
        def _(act):
            act.wait_ge(s.vector_in, 16 * nv)
            nc.scalar.activation(csil[:], craw[:], ACT.Silu).then_inc(s.silu, 1)

        @block.vector
        def _(dve):
            dve.wait_ge(s.silu, 1)
            nc.vector.tensor_copy(wide[:].rearrange("p v k c -> p (v k) c"),
                                  column(flat(csil[:]), nv * KD, P)).then_inc(s.wide, 1)
            dve.wait_ge(s.bias_in, 16 * nv)
            for u, (n, v) in enumerate(units):
                dst = conds[v][1][:, n * 512:(n + 1) * 512]
                dve.wait_ge(s.product, u + 1)
                nc.vector.tensor_tensor(dst, m.ps[:, u % 4, :], dst, ALU.add).then_inc(s.added, 1)

        @block.tensor
        def _(pe):
            pe.wait_ge(s.wide, 1)
            for u, (n, v) in enumerate(units):
                ring.wait(pe, first + n)
                w = whole(KD, 512)(ring.slot(first + n))
                if u >= 4:
                    pe.wait_ge(s.added, u - 3)
                for k in range(KD):
                    last = nc.tensor.matmul(m.ps[:, u % 4, :], wide[:, v, k, :], w[:, k, :],
                                            start=(k == 0), stop=(k == KD - 1))
                last.then_inc(s.product, 1)
                if u + 1 == len(units) or units[u + 1][0] != n:
                    pe.wait_ge(s.product, u + 1)
                    pe.sem_inc(ring.freed[(first + n) % SLOTS], 1)
    st.close()


def prepare_stage(m, tag, groups, gain, after):
    nc = m.nc
    st = Stage(m, f"prep{tag}")
    tiles = [(x, g, i) for g, grp in enumerate(groups) for i, x in enumerate(grp[0])]
    n = len(tiles)
    gbc = st.sb("gain", [P, D])
    xn = st.sb("xn", [P, 2, D])
    junk = st.sb("junk", [P, D])
    ss = st.sb("ss", [P, 3, n])
    s = st.sem("gain_in square v root rstd chain ready turned evac kept")
    with st.block() as block:
        @block.sync
        def _(sp):
            sp.dma_start(gbc[:], gain.partition_broadcast(P)).then_inc(s.gain_in, 16)
            for u, (_, g, i) in enumerate(tiles):
                keep = groups[g][5]
                if keep is not None:
                    sp.wait_ge(s.ready, u + 1)
                    sp.dma_start(keep[i * P:(i + 1) * P, :], xn[:, u % 2, :]).then_inc(s.kept, 16)
            m.ring.stream(sp, after)
            if any(grp[5] is not None for grp in groups):
                sp.wait_ge(s.kept, 16 * n)

        @block.vector
        def _(dve):
            link = Linked(dve, s.chain)
            for u, (x, _, _) in enumerate(tiles):
                link(nc.vector.tensor_tensor_reduce(out=junk[:], in0=x, in1=x, scale=1.0, scalar=0.0,
                                                    op0=ALU.mult, op1=ALU.add, accum_out=ss[:, 0, u:u + 1]))
            link(nc.vector.tensor_scalar(ss[:, 1, :], ss[:, 0, :], 1.0 / D, EPS, ALU.mult, ALU.add))
            nc.vector.tensor_copy(ss[:, 1, :], ss[:, 1, :]).then_inc(s.v, 1)
            dve.wait_ge(s.gain_in, 16)
            for g, (_, _, scale, _, _, _) in enumerate(groups):
                link(nc.vector.scalar_tensor_tensor(out=scale, in0=scale, scalar=1.0, in1=gbc[:],
                                                    op0=ALU.add, op1=ALU.mult))
            dve.wait_ge(s.root, 1)
            r, v, a = ss[:, 2, :], ss[:, 1, :], ss[:, 0, :]
            link(nc.vector.reciprocal(r, r))
            link(nc.vector.tensor_tensor(a, r, r, ALU.mult))
            link(nc.vector.tensor_tensor(a, a, v, ALU.mult))
            link(nc.vector.tensor_scalar(a, a, -0.5, 1.5, ALU.mult, ALU.add))
            link(nc.vector.tensor_tensor(r, r, a, ALU.mult))
            for u, (x, g, i) in enumerate(tiles):
                _, shift, scale, _, _, keep = groups[g]
                if u >= 2:
                    dve.wait_ge(s.turned, u - 1)
                    if keep is not None:
                        dve.wait_ge(s.kept, 16 * (u - 1))
                link(nc.vector.scalar_tensor_tensor(out=xn[:, u % 2, :], in0=x, scalar=r[:, u:u + 1],
                                                    in1=scale, op0=ALU.mult, op1=ALU.mult))
                nc.vector.tensor_tensor(xn[:, u % 2, :], xn[:, u % 2, :], shift, ALU.add).then_inc(s.ready, 1)

        @block.scalar
        def _(act):
            act.wait_ge(s.v, 1)
            nc.scalar.activation(ss[:, 2, :], ss[:, 1, :], ACT.Sqrt).then_inc(s.root, 1)
            for u, (_, g, i) in enumerate(tiles):
                _, _, _, dst, c0, _ = groups[g]
                act.wait_ge(s.turned, u + 1)
                for h in range(2):
                    last = nc.scalar.activation(
                        dst[:, 4 * h:4 * h + 4, c0 + i * P:c0 + (i + 1) * P],
                        m.ps[:, (u % 2) * 2 + h, :].rearrange("p (k t) -> p k t", k=4), ACT.Copy)
                last.then_inc(s.evac, 1)

        @block.tensor
        def _(pe):
            for u in range(n):
                pe.wait_ge(s.ready, u + 1)
                if u >= 2:
                    pe.wait_ge(s.evac, u - 1)
                for k in range(KD):
                    last = nc.tensor.transpose(m.ps[:, (u % 2) * 2 + k // 4, (k % 4) * P:(k % 4 + 1) * P],
                                               xn[:, u % 2, k * P:(k + 1) * P], m.ident)
                last.then_inc(s.turned, 1)
    st.close()


def project_stage(m, tag, aT, first, gate, after):
    nc, ring = m.nc, m.ring
    st = Stage(m, f"out{tag}")
    tmp = st.sb("tmp", [P, 2, 512])
    s = st.sem("product gated added")
    units = [(h, t) for h in range(2) for t in range(NT)]
    with st.block() as block:
        @block.sync
        def _(sp):
            ring.stream(sp, after)

        @block.tensor
        def _(pe):
            for u, (h, t) in enumerate(units):
                ring.wait(pe, first + h)
                w = whole(KD, 512)(ring.slot(first + h))
                if u >= 4:
                    pe.wait_ge(s.gated, u - 3)
                for k in range(KD):
                    last = nc.tensor.matmul(m.ps[:, u % 4, :], aT[:, k, t * P:(t + 1) * P], w[:, k, :],
                                            start=(k == 0), stop=(k == KD - 1))
                last.then_inc(s.product, 1)
                if t == NT - 1:
                    pe.wait_ge(s.product, u + 1)
                    pe.sem_inc(ring.freed[(first + h) % SLOTS], 1)

        @block.vector
        def _(dve):
            for u, (h, t) in enumerate(units):
                cols = slice(h * 512, (h + 1) * 512)
                dve.wait_ge(s.product, u + 1)
                nc.vector.tensor_tensor(tmp[:, u % 2, :], m.ps[:, u % 4, :], gate[:, cols],
                                        ALU.mult).then_inc(s.gated, 1)
                dve.wait_ge(s.gated, u + 1)
                nc.vector.tensor_tensor(m.x[:, t, cols], m.x[:, t, cols], tmp[:, u % 2, :],
                                        ALU.add).then_inc(s.added, 1)
                dve.wait_ge(s.added, u + 1)
    st.close()


LAT = CT + 2
SPAN = LAT + T
DK = 128


def delta_gates(m, hx, p, w_small, a_log, dt_bias):
    nc = m.nc
    st = Stage(m, "gates")
    n = NCT + NT
    ws = st.sb("w", [P, KD, 32])
    al = st.sb("alog", [P, 16])
    dt = st.sb("dt", [P, 16])
    raw = st.sb("raw", [P, n, 32])
    b = st.sb("b", [P, 6, n, 16])
    s = st.sem("small_in sum_in logits raw_there beta expA expB decay chain sums exps")
    with st.block() as block:
        @block.sync
        def _(sp):
            sp.dma_start(ws[:], w_small.rearrange("(k p) n -> p k n", p=P)).then_inc(s.small_in, 16)
            sp.dma_start(al[:], a_log.partition_broadcast(P)).then_inc(s.sum_in, 16)
            sp.dma_start(dt[:], dt_bias.partition_broadcast(P)).then_inc(s.sum_in, 16)

        @block.tensor
        def _(pe):
            pe.wait_ge(s.small_in, 16)
            for t in range(n):
                for k in range(KD):
                    last = nc.tensor.matmul(m.ps[:, 0, t * 32:(t + 1) * 32], hx[:, k, t * P:(t + 1) * P],
                                            ws[:, k, :], start=(k == 0), stop=(k == KD - 1))
            last.then_inc(s.logits, 1)
            pe.wait_ge(s.decay, 1)
            for d in range(2):
                g = b[:, 5, :, 8 * d:8 * d + 8]
                nc.tensor.matmul(m.ps[:, 1 + d, 0:8 * n].rearrange("p (t h) -> p t h", h=8),
                                 p.masks[:, d, :], g, start=True, stop=True)
                last = nc.tensor.matmul(m.ps[:, 3 + d, 0:8 * n].rearrange("p (t h) -> p t h", h=8),
                                        m.ones, g, start=True, stop=True)
            last.then_inc(s.sums, 1)

        @block.scalar
        def _(act):
            act.wait_ge(s.raw_there, 1)
            nc.scalar.activation(p.beta[:], raw[:, :, 0:16], ACT.Sigmoid).then_inc(s.beta, 1)
            act.wait_ge(s.sum_in, 32)
            nc.scalar.activation(al[:], al[:], ACT.Exp).then_inc(s.expA, 1)
            act.wait_ge(s.chain, 3)
            nc.scalar.activation(b[:, 2, :, :], b[:, 1, :, :], ACT.Exp).then_inc(s.expB, 1)
            act.wait_ge(s.chain, 4)
            nc.scalar.activation(b[:, 3, :, :], b[:, 2, :, :], ACT.Ln).then_inc(s.expB, 1)
            act.wait_ge(s.chain, 8)
            nc.scalar.activation(p.egc[:], p.cum[:], ACT.Exp).then_inc(s.exps, 1)
            nc.scalar.activation(p.ekd[:], b[:, 0, :, :], ACT.Exp).then_inc(s.exps, 1)
            nc.scalar.activation(p.egl[:], p.egl[:], ACT.Exp).then_inc(s.exps, 1)

        @block.vector
        def _(dve):
            link = Linked(dve, s.chain)
            dve.wait_ge(s.logits, 1)
            nc.vector.tensor_copy(raw[:], m.ps[:, 0, 0:n * 32].rearrange("p (t c) -> p t c", c=32)
                                  ).then_inc(s.raw_there, 1)
            dve.wait_ge(s.raw_there, 1)
            dve.wait_ge(s.sum_in, 32)
            link(nc.vector.tensor_tensor(b[:, 0, :, :], raw[:, :, 16:32], across(dt[:], n), ALU.add))
            link(nc.vector.tensor_scalar(b[:, 4, :, :], b[:, 0, :, :], -1.0, None, ALU.mult))
            link(nc.vector.tensor_tensor(b[:, 1, :, :], b[:, 0, :, :], b[:, 4, :, :], ALU.min))
            dve.wait_ge(s.expB, 1)
            link(nc.vector.tensor_scalar(b[:, 2, :, :], b[:, 2, :, :], 1.0, None, ALU.add))
            dve.wait_ge(s.expB, 2)
            link(nc.vector.scalar_tensor_tensor(out=b[:, 4, :, :], in0=b[:, 0, :, :], scalar=0.0,
                                                in1=b[:, 3, :, :], op0=ALU.max, op1=ALU.add))
            dve.wait_ge(s.expA, 1)
            nc.vector.scalar_tensor_tensor(out=b[:, 5, :, :], in0=b[:, 4, :, :], scalar=-1.0,
                                           in1=across(al[:], n), op0=ALU.mult, op1=ALU.mult
                                           ).then_inc(s.decay, 1)
            dve.wait_ge(s.sums, 1)
            for d in range(2):
                hs = slice(8 * d, 8 * d + 8)
                nc.vector.tensor_copy(p.cum[:, :, hs],
                                      m.ps[:, 1 + d, 0:8 * n].rearrange("p (t h) -> p t h", h=8))
                nc.vector.tensor_copy(p.egl[:, :, hs],
                                      m.ps[:, 3 + d, 0:8 * n].rearrange("p (t h) -> p t h", h=8))
            nc.vector.tensor_copy(p.g[:], b[:, 5, :, :])
            link(nc.vector.tensor_copy(b[:, 4, :, 0:1], b[:, 4, :, 0:1]))
            link(nc.vector.tensor_scalar(p.ncum[:], p.cum[:], -1.0, None, ALU.mult))
            link(nc.vector.tensor_tensor(b[:, 0, :, :], p.egl[:], p.cum[:], ALU.subtract))
            dve.wait_ge(s.exps, 3)
            dve.wait_ge(s.beta, 1)
            link(nc.vector.tensor_tensor(p.bege[:], p.beta[:], p.egc[:], ALU.mult))
    st.close()


def delta_heads(m, hg, hx, p, first, after):
    nc, ring = m.nc, m.ring
    st = Stage(m, f"heads{hg}")
    raw = st.sb("raw", [P, 2, SPAN + 2])
    acc = st.sb("acc", [P, 2, SPAN])
    xw = m.x[:].rearrange("p t d -> p (t d)")
    y = xw[:, 0:2 * SPAN].rearrange("p (b c) -> p b c", b=2)
    sq = xw[:, 2 * SPAN:4 * SPAN].rearrange("p (b c) -> p b c", b=2)
    s = st.sem("product copied zeroed chain tapped silu squared summed root turned moved done")
    kinds = [(0, h) for h in range(4)] + [(1, h) for h in range(4)] + [(2, h) for h in range(4)]
    with st.block() as block:
        @block.sync
        def _(sp):
            ring.stream(sp, after)

        @block.gpsimd
        def _(pool):
            nc.gpsimd.memset(raw[:], 0.0).then_inc(s.zeroed, 1)

        @block.tensor
        def _(pe):
            def project(u):
                kind, h = kinds[u]
                n = first + kind
                if h == 0:
                    ring.wait(pe, n)
                w = whole(KD, 512)(ring.slot(n))
                if u >= 2:
                    pe.wait_ge(s.copied, u - 1)
                b = (u % 2) * 2
                for k in range(KD):
                    last = nc.tensor.matmul(m.ps[:, b, :], w[:, k, h * P:(h + 1) * P], hx[:, k, CT:CT + T],
                                            start=(k == 0), stop=(k == KD - 1))
                if kind > 0:
                    for k in range(KD):
                        last = nc.tensor.matmul(m.ps[:, b + 1, 0:CT], w[:, k, h * P:(h + 1) * P],
                                                hx[:, k, 0:CT], start=(k == 0), stop=(k == KD - 1))
                last.then_inc(s.product, 1)
                if h == 3:
                    pe.wait_ge(s.product, u + 1)
                    pe.sem_inc(ring.freed[n % SLOTS], 1)

            def norm_or_turn(u):
                kind, h = kinds[u]
                if kind < 2:
                    pe.wait_ge(s.squared, u + 1)
                    if u >= 1:
                        pe.wait_ge(s.root, u)
                    last = nc.tensor.matmul(m.ps[:, 4, :], m.ones, sq[:, u % 2, LAT:SPAN], start=True, stop=True)
                    if kind == 1:
                        last = nc.tensor.matmul(m.ps[:, 5, 0:CT], m.ones, sq[:, u % 2, 0:CT],
                                                start=True, stop=True)
                    last.then_inc(s.summed, 1)

            def turn(u):
                kind, h = kinds[u]
                if kind == 0:
                    return
                i = u - 4
                pe.wait_ge(s.silu, u + 1)
                if kind == 1:
                    pe.wait_ge(s.done, u + 1)
                if i >= 1:
                    pe.wait_ge(s.moved, 2 * i)
                src = p.kT[:, h, :] if kind == 1 else y[:, u % 2, :]
                for t in range(NCT + NT):
                    c = t * P if t < NCT else LAT + (t - NCT) * P
                    last = nc.tensor.transpose(m.ps[:, 6 + t // 4, (t % 4) * P:(t % 4 + 1) * P],
                                               src[:, c:c + P], m.ident)
                last.then_inc(s.turned, 1)

            for u in range(len(kinds) + 1):
                if u < len(kinds):
                    project(u)
                if u >= 1:
                    norm_or_turn(u - 1)
                    turn(u - 1)

        @block.scalar
        def _(act):
            act.wait_ge(s.zeroed, 1)
            for u, (kind, h) in enumerate(kinds):
                b = (u % 2) * 2
                act.wait_ge(s.product, u + 1)
                if u >= 2:
                    act.wait_ge(s.tapped, u - 1)
                last = nc.scalar.activation(raw[:, u % 2, 1 + LAT:1 + SPAN], m.ps[:, b, :], ACT.Copy)
                if kind > 0:
                    last = nc.scalar.activation(raw[:, u % 2, 1:1 + CT], m.ps[:, b + 1, 0:CT], ACT.Copy)
                last.then_inc(s.copied, 1)
                act.wait_ge(s.tapped, u + 1)
                if u >= 2:
                    act.wait_ge(s.done, min(u - 1, 8))
                    if u - 2 >= 8:
                        act.wait_ge(s.turned, u - 2 - 4 + 1)
                nc.scalar.activation(y[:, u % 2, :], acc[:, u % 2, :], ACT.Silu).then_inc(s.silu, 1)
                if kind < 2:
                    act.wait_ge(s.silu, u + 1)
                    nc.scalar.activation(sq[:, u % 2, :], y[:, u % 2, :], ACT.Square).then_inc(s.squared, 1)
                    act.wait_ge(s.summed, u + 1)
                    if kind == 0:
                        nc.scalar.activation(sq[:, u % 2, LAT:SPAN], m.ps[:, 4, :], ACT.Sqrt,
                                             bias=m.eps[:]).then_inc(s.root, 1)
                    else:
                        nc.scalar.activation(sq[:, u % 2, LAT:SPAN], m.ps[:, 4, :], ACT.Sqrt, bias=m.eps[:])
                        nc.scalar.activation(sq[:, u % 2, 0:CT], m.ps[:, 5, 0:CT], ACT.Sqrt,
                                             bias=m.eps[:]).then_inc(s.root, 1)
                if kind > 0:
                    i = u - 4
                    dst = p.k if kind == 1 else p.v
                    act.wait_ge(s.turned, i + 1)
                    nc.scalar.activation(dst[:, 0:4, h * P:(h + 1) * P],
                                         m.ps[:, 6, :].rearrange("p (t c) -> p t c", c=P),
                                         ACT.Copy).then_inc(s.moved, 1)
                    nc.scalar.activation(dst[:, 4:6, h * P:(h + 1) * P],
                                         m.ps[:, 7, 0:2 * P].rearrange("p (t c) -> p t c", c=P),
                                         ACT.Copy).then_inc(s.moved, 1)

        @block.vector
        def _(dve):
            link = Linked(dve, s.chain)
            for u, (kind, h) in enumerate(kinds):
                taps = [p.conv[:, j, kind * 8 + hg * 4 + h:kind * 8 + hg * 4 + h + 1] for j in range(3)]
                dve.wait_ge(s.copied, u + 1)
                if u >= 2:
                    dve.wait_ge(s.silu, u - 1)
                link(nc.vector.tensor_scalar(acc[:, u % 2, :], raw[:, u % 2, 0:SPAN], taps[0], None, ALU.mult))
                link(nc.vector.scalar_tensor_tensor(out=acc[:, u % 2, :], in0=raw[:, u % 2, 1:1 + SPAN],
                                                    scalar=taps[1], in1=acc[:, u % 2, :],
                                                    op0=ALU.mult, op1=ALU.add))
                nc.vector.scalar_tensor_tensor(out=acc[:, u % 2, :], in0=raw[:, u % 2, 2:2 + SPAN],
                                               scalar=taps[2], in1=acc[:, u % 2, :],
                                               op0=ALU.mult, op1=ALU.add).then_inc(s.tapped, 1)
                if kind < 2:
                    dve.wait_ge(s.root, u + 1)
                    lo = LAT if kind == 0 else 0
                    link(nc.vector.reciprocal(sq[:, u % 2, lo:SPAN], sq[:, u % 2, lo:SPAN]))
                    if kind == 0:
                        nc.vector.scalar_tensor_tensor(out=p.qT[:, h, :], in0=y[:, u % 2, LAT:SPAN],
                                                       scalar=DK ** -0.5, in1=sq[:, u % 2, LAT:SPAN],
                                                       op0=ALU.mult, op1=ALU.mult).then_inc(s.done, 1)
                    else:
                        nc.vector.tensor_tensor(p.kT[:, h, :], y[:, u % 2, :], sq[:, u % 2, :],
                                                ALU.mult).then_inc(s.done, 1)
    st.close()


def delta_scan(m, hg, p):
    nc = m.nc
    st = Stage(m, f"scan{hg}")
    W4 = 4 * P
    names = ["L", "Tm", "A", "X", "XT", "Z", "bV", "bK", "kd", "S"]
    spare = [m.x[:, i // 2, (i % 2) * 512:(i % 2) * 512 + 512] for i in range(8)] + \
            [m.mod[:, i * 512:(i + 1) * 512] for i in range(4)]
    extra = st.sb("extra", [P, 8, 512])
    spare += [extra[:, i, :] for i in range(8)]
    B = [{nm: spare[d * 10 + i] for i, nm in enumerate(names)} for d in range(2)]
    ev = ("gcb kk qk argA argB expA expB lower attn bv bk kdec lm inv0 turned0 xt0 z zcopied pq xt xx "
          "w wcopied vps vnew q_s o_s o_add a_v o_done s_ps s_scaled state zero")
    S2 = [st.sem(ev, "f"), st.sem(ev, "b")]
    order = [[0, 1, 2, 3, 4, 5], [1, 0, 5, 4, 3, 2]]
    steps = 6
    LV = 6

    def cols(t):
        return t * P if t < NCT else LAT + (t - NCT) * P

    def lat_count(i):
        return max(0, i - NCT)

    def bank(d, b):
        return m.ps[:, 4 * d + b, :]

    def h3(ap):
        return ap.rearrange("p (h c) -> p h c", h=4)

    def hd(ap, h):
        return ap[:, h * P:(h + 1) * P]

    def gate(buf, t, d):
        return buf[:, t, 8 * d + 4 * hg:8 * d + 4 * hg + 4]

    with st.block() as block:
        @block.tensor
        def _(pe):
            def scores(i, d):
                e, b, t = S2[d], B[d], order[d][i]
                c = cols(t)
                if i >= 1:
                    pe.wait_ge(e.xx, LV * i)
                for h in range(4):
                    g = p.g[:, t, 8 * d + 4 * hg + h:8 * d + 4 * hg + h + 1]
                    if i >= NCT + 1 and h == 0:
                        pe.wait_ge(e.o_done, lat_count(i))
                    last = nc.tensor.matmul(hd(bank(d, 2), h), g.to_broadcast([P, P]), p.masks[:, d, :],
                                            start=True, stop=True)
                last.then_inc(e.gcb, 1)
                if i >= 1:
                    pe.wait_ge(e.vnew, i)
                for h in range(4):
                    kt = p.kT[:, h, c:c + P]
                    last = nc.tensor.matmul(hd(bank(d, 0), h), kt, kt, start=True, stop=True)
                last.then_inc(e.kk, 1)
                if t >= NCT:
                    if i >= NCT + 1:
                        pe.wait_ge(e.o_s, lat_count(i))
                    for h in range(4):
                        last = nc.tensor.matmul(hd(bank(d, 1), h), p.kT[:, h, c:c + P],
                                                p.qT[:, h, (t - NCT) * P:(t - NCT + 1) * P],
                                                start=True, stop=True)
                    last.then_inc(e.qk, 1)

            def first_level(i, d):
                e, b = S2[d], B[d]
                pe.wait_ge(e.lm, (LV + 1) * i + 1)
                pe.wait_ge(e.lower, i + 1)
                for h in range(4):
                    last = nc.tensor.transpose(hd(bank(d, 0), h), hd(b["Tm"], h), m.ident)
                last.then_inc(e.turned0, 1)

            def level_z(i, l, d):
                e, b = S2[d], B[d]
                pe.wait_ge(e.lm, (LV + 1) * i + l + 2)
                pe.wait_ge(e.xt0, i + 1)
                pe.wait_ge(e.xt, LV * i + l)
                for h in range(4):
                    last = nc.tensor.matmul(hd(bank(d, 0), h), hd(b["Tm"], h), hd(b["XT"], h),
                                            start=True, stop=True)
                last.then_inc(e.z, 1)

            def level_pq(i, l, d):
                e, b = S2[d], B[d]
                pe.wait_ge(e.zcopied, LV * i + l + 1)
                pe.wait_ge(e.inv0, i + 1)
                pe.wait_ge(e.xx, LV * i + l)
                if order[d][i] >= NCT:
                    pe.wait_ge(e.attn, lat_count(i) + 1)
                for h in range(4):
                    nc.tensor.matmul(hd(bank(d, 1), h), hd(b["X"], h), hd(b["Z"], h), start=True, stop=True)
                for h in range(4):
                    last = nc.tensor.matmul(hd(bank(d, 2), h), hd(b["Z"], h), hd(b["X"], h),
                                            start=True, stop=True)
                last.then_inc(e.pq, 1)

            def make_w(i, d):
                e, b = S2[d], B[d]
                pe.wait_ge(e.xt, LV * (i + 1))
                pe.wait_ge(e.bk, i + 1)
                pe.wait_ge(e.state, i)
                for h in range(4):
                    last = nc.tensor.matmul(hd(bank(d, 3), h), hd(b["bK"], h), hd(b["XT"], h),
                                            start=True, stop=True)
                last.then_inc(e.w, 1)

            def chain(i, d):
                e, b, t = S2[d], B[d], order[d][i]
                pe.wait_ge(e.wcopied, i + 1)
                pe.wait_ge(e.bv, i + 1)
                pe.wait_ge(e.zero, 1)
                for h in range(4):
                    nc.tensor.matmul(hd(bank(d, 0), h), hd(b["XT"], h), hd(b["bV"], h), start=True, stop=False)
                    last = nc.tensor.matmul(hd(bank(d, 0), h), hd(b["Z"], h), hd(b["S"], h),
                                            start=False, stop=True)
                last.then_inc(e.vps, 1)
                if t >= NCT:
                    q0 = (t - NCT) * P
                    for h in range(4):
                        last = nc.tensor.matmul(hd(bank(d, 1), h), p.qT[:, h, q0:q0 + P], hd(b["S"], h),
                                                start=True, stop=True)
                    last.then_inc(e.q_s, 1)
                pe.wait_ge(e.vnew, i + 1)
                pe.wait_ge(e.kdec, i + 1)
                if i < steps - 1:
                    for h in range(4):
                        last = nc.tensor.matmul(hd(bank(d, 3), h), hd(b["kd"], h), hd(b["bK"], h),
                                                start=True, stop=True)
                    last.then_inc(e.s_ps, 1)
                if t >= NCT:
                    pe.wait_ge(e.xx, LV * (i + 1))
                    for h in range(4):
                        last = nc.tensor.matmul(hd(bank(d, 2), h), hd(b["A"], h), hd(b["bK"], h),
                                                start=True, stop=True)
                    last.then_inc(e.a_v, 1)

            for i in range(steps):
                for d in range(2):
                    scores(i, d)
                for d in range(2):
                    first_level(i, d)
                for l in range(LV):
                    for d in range(2):
                        level_z(i, l, d)
                    for d in range(2):
                        level_pq(i, l, d)
                for d in range(2):
                    make_w(i, d)
                for d in range(2):
                    chain(i, d)

        @block.scalar
        def _(act):
            for i in range(steps):
                for d in range(2):
                    e, b, t = S2[d], B[d], order[d][i]
                    act.wait_ge(e.argA, i + 1)
                    for h in range(4):
                        j = 8 * d + 4 * hg + h
                        last = nc.scalar.activation(hd(b["L"], h), hd(b["L"], h), ACT.Exp,
                                                    bias=p.cum[:, t, j:j + 1])
                    last.then_inc(e.expA, 1)
                    if t >= NCT:
                        act.wait_ge(e.argB, lat_count(i) + 1)
                        for h in range(4):
                            j = 8 * d + 4 * hg + h
                            last = nc.scalar.activation(hd(b["A"], h), hd(b["A"], h), ACT.Exp,
                                                        bias=p.ncum[:, t, j:j + 1])
                        last.then_inc(e.expB, 1)
                for l in range(LV):
                    for d in range(2):
                        e, b = S2[d], B[d]
                        act.wait_ge(e.z, LV * i + l + 1)
                        if l >= 1:
                            act.wait_ge(e.pq, LV * i + l)
                        elif i >= 1:
                            act.wait_ge(e.vps, i)
                        nc.scalar.activation(b["Z"], bank(d, 0), ACT.Copy).then_inc(e.zcopied, 1)
                for d in range(2):
                    e, b = S2[d], B[d]
                    act.wait_ge(e.w, i + 1)
                    act.wait_ge(e.pq, LV * (i + 1))
                    nc.scalar.mul(b["Z"], bank(d, 3), -1.0).then_inc(e.wcopied, 1)

        @block.gpsimd
        def _(pool):
            for d in range(2):
                nc.gpsimd.memset(B[d]["S"], 0.0).then_inc(S2[d].zero, 1)
            for i in range(steps):
                for d in range(2):
                    e, b, t = S2[d], B[d], order[d][i]
                    if i >= 1:
                        pool.wait_ge(e.vps, i)
                        if i < steps:
                            pool.wait_ge(e.s_ps, i)
                        if lat_count(i):
                            pool.wait_ge(e.a_v, lat_count(i))
                    nc.gpsimd.tensor_tensor(h3(b["bV"]), h3(p.v[:, t, :]), column(gate(p.beta, t, d), 4, P),
                                            ALU.mult).then_inc(e.bv, 1)
                    nc.gpsimd.tensor_tensor(h3(b["bK"]), h3(p.k[:, t, :]), column(gate(p.bege, t, d), 4, P),
                                            ALU.mult).then_inc(e.bk, 1)
                    nc.gpsimd.tensor_tensor(h3(b["kd"]), h3(p.k[:, t, :]), column(gate(p.ekd, t, d), 4, P),
                                            ALU.mult).then_inc(e.kdec, 1)
                for l in range(LV + 1):
                    for d in range(2):
                        e, b = S2[d], B[d]
                        pool.wait_ge(e.lower, i + 1)
                        if l == 1:
                            pool.wait_ge(e.inv0, i + 1)
                            pool.wait_ge(e.turned0, i + 1)
                        if l >= 2:
                            pool.wait_ge(e.z, LV * i + l - 1)
                        if l == 0 and i >= 1:
                            pool.wait_ge(e.z, LV * i)
                        nc.gpsimd.tensor_tensor(h3(b["Tm"]), h3(b["L"]), across(p.masks[:, 6 + 7 * d + l, :], 4),
                                                ALU.mult).then_inc(e.lm, 1)
                if i < steps - 1:
                    for d in range(2):
                        e, b, t = S2[d], B[d], order[d][i]
                        pool.wait_ge(e.vps, i + 1)
                        if t >= NCT:
                            pool.wait_ge(e.q_s, lat_count(i) + 1)
                        if i >= 1:
                            pool.wait_ge(e.state, i)
                        nc.gpsimd.tensor_tensor(h3(b["S"]), h3(b["S"]), column(gate(p.egl, t, d), 4, P),
                                                ALU.mult).then_inc(e.s_scaled, 1)

        @block.vector
        def _(dve):
            for i in range(steps):
                for d in range(2):
                    e, b, t = S2[d], B[d], order[d][i]
                    dve.wait_ge(e.gcb, i + 1)
                    if i >= 1:
                        dve.wait_ge(e.lm, (LV + 1) * i)
                    nc.vector.scalar_tensor_tensor(out=h3(b["L"]), in0=h3(bank(d, 2)), scalar=-1.0,
                                                   in1=across(p.masks[:, 2 + d, :], 4),
                                                   op0=ALU.mult, op1=ALU.add).then_inc(e.argA, 1)
                    if t >= NCT:
                        if i > NCT:
                            dve.wait_ge(e.a_v, lat_count(i))
                        nc.vector.tensor_tensor(h3(b["A"]), h3(bank(d, 2)), across(p.masks[:, 4 + d, :], 4),
                                                ALU.add).then_inc(e.argB, 1)
                for d in range(2):
                    e, b, t = S2[d], B[d], order[d][i]
                    dve.wait_ge(e.expA, i + 1)
                    dve.wait_ge(e.kk, i + 1)
                    for h in range(4):
                        j = 8 * d + 4 * hg + h
                        last = nc.vector.scalar_tensor_tensor(out=hd(b["L"], h), in0=hd(b["L"], h),
                                                              scalar=p.beta[:, t, j:j + 1],
                                                              in1=hd(bank(d, 0), h),
                                                              op0=ALU.mult, op1=ALU.mult)
                    last.then_inc(e.lower, 1)
                    if t >= NCT:
                        dve.wait_ge(e.expB, lat_count(i) + 1)
                        dve.wait_ge(e.qk, lat_count(i) + 1)
                        nc.vector.tensor_tensor(b["A"], b["A"], bank(d, 1), ALU.mult).then_inc(e.attn, 1)
                for d in range(2):
                    e, b = S2[d], B[d]
                    dve.wait_ge(e.lm, (LV + 1) * i + 1)
                    nc.vector.scalar_tensor_tensor(out=h3(b["X"]), in0=h3(b["Tm"]), scalar=-1.0,
                                                   in1=across(m.ident, 4), op0=ALU.mult,
                                                   op1=ALU.add).then_inc(e.inv0, 1)
                    dve.wait_ge(e.turned0, i + 1)
                    nc.vector.scalar_tensor_tensor(out=h3(b["XT"]), in0=h3(bank(d, 0)), scalar=-1.0,
                                                   in1=across(m.ident, 4), op0=ALU.mult,
                                                   op1=ALU.add).then_inc(e.xt0, 1)
                for l in range(LV):
                    for d in range(2):
                        e, b = S2[d], B[d]
                        dve.wait_ge(e.pq, LV * i + l + 1)
                        dve.wait_ge(e.xt0, i + 1)
                        if l:
                            dve.wait_ge(e.xx, LV * i + l)
                        nc.vector.tensor_tensor(b["XT"], b["XT"], bank(d, 1), ALU.subtract).then_inc(e.xt, 1)
                        nc.vector.tensor_tensor(b["X"], b["X"], bank(d, 2), ALU.subtract).then_inc(e.xx, 1)
                for d in range(2):
                    e, b, t = S2[d], B[d], order[d][i]
                    dve.wait_ge(e.vps, i + 1)
                    nc.vector.tensor_copy(b["bK"], bank(d, 0)).then_inc(e.vnew, 1)
                    if i < steps - 1:
                        dve.wait_ge(e.s_ps, i + 1)
                        dve.wait_ge(e.s_scaled, i + 1)
                        nc.vector.tensor_tensor(b["S"], b["S"], bank(d, 3), ALU.add).then_inc(e.state, 1)
                    if t >= NCT:
                        n = lat_count(i) + 1
                        dve.wait_ge(e.q_s, n)
                        dve.wait_ge(e.xx, LV * (i + 1))
                        nc.vector.tensor_tensor(h3(b["X"]), h3(bank(d, 1)), column(gate(p.egc, t, d), 4, P),
                                                ALU.mult).then_inc(e.o_s, 1)
                        o = p.o[:, t - NCT, hg * 512:(hg + 1) * 512]
                        dve.wait_ge(e.o_s, n)
                        if i > NCT:
                            dve.wait_ge(S2[1 - d].o_done, lat_count(i) if d == 0 else n)
                            dve.wait_ge(e.o_done, n - 1)
                        elif d == 1:
                            dve.wait_ge(S2[0].o_done, 1)
                        nc.vector.tensor_tensor(o, o, b["X"], ALU.add).then_inc(e.o_add, 1)
                        dve.wait_ge(e.o_add, n)
                        dve.wait_ge(e.a_v, n)
                        nc.vector.tensor_tensor(o, o, bank(d, 2), ALU.add).then_inc(e.o_done, 1)
    st.close()


def delta_finish(m, hx, p, first, after):
    nc, ring = m.nc, m.ring
    st = Stage(m, "ofin")
    zs = st.sb("z", [P, 2, NT, 512])
    sq = st.sb("sq", [P, 512])
    on = st.sb("onorm", [P, DK])
    r = st.sb("r", [P, 3, NT * HEADS])
    s = st.sem("norm_in product silu chain root ready turned evac v")
    units = [(h, t) for h in range(2) for t in range(NT)]
    with st.block() as block:
        @block.sync
        def _(sp):
            sp.dma_start(on[:], p.onorm.partition_broadcast(P)).then_inc(s.norm_in, 16)
            ring.stream(sp, after)

        @block.tensor
        def _(pe):
            for u, (h, t) in enumerate(units):
                ring.wait(pe, first + h)
                w = whole(KD, 512)(ring.slot(first + h))
                if u >= 2:
                    pe.wait_ge(s.silu, u - 1)
                for k in range(KD):
                    last = nc.tensor.matmul(m.ps[:, u % 2, :], hx[:, k, CT + t * P:CT + (t + 1) * P], w[:, k, :],
                                            start=(k == 0), stop=(k == KD - 1))
                last.then_inc(s.product, 1)
                if t == NT - 1:
                    pe.wait_ge(s.product, u + 1)
                    pe.sem_inc(ring.freed[(first + h) % SLOTS], 1)
            for t in range(NT):
                pe.wait_ge(s.ready, t + 1)
                if t >= 1:
                    pe.wait_ge(s.evac, t)
                for k in range(KD):
                    last = nc.tensor.transpose(m.ps[:, 4 + k // 4, (k % 4) * P:(k % 4 + 1) * P],
                                               p.o[:, t, k * P:(k + 1) * P], m.ident)
                last.then_inc(s.turned, 1)

        @block.scalar
        def _(act):
            for u, (h, t) in enumerate(units):
                act.wait_ge(s.product, u + 1)
                nc.scalar.activation(zs[:, h, t, :], m.ps[:, u % 2, :], ACT.Silu).then_inc(s.silu, 1)
            act.wait_ge(s.v, 1)
            nc.scalar.activation(r[:, 2, :], r[:, 1, :], ACT.Sqrt).then_inc(s.root, 1)
            for t in range(NT):
                act.wait_ge(s.turned, t + 1)
                for h in range(2):
                    last = nc.scalar.activation(p.oT[:, 4 * h:4 * h + 4, t * P:(t + 1) * P],
                                                m.ps[:, 4 + h, :].rearrange("p (k t) -> p k t", k=4), ACT.Copy)
                last.then_inc(s.evac, 1)

        @block.vector
        def _(dve):
            link = Linked(dve, s.chain)
            for t in range(NT):
                for h in range(HEADS):
                    link(nc.vector.tensor_tensor_reduce(
                        out=sq[:, 0:P], in0=p.o[:, t, h * P:(h + 1) * P], in1=p.o[:, t, h * P:(h + 1) * P],
                        scale=1.0, scalar=0.0, op0=ALU.mult, op1=ALU.add,
                        accum_out=r[:, 0, t * HEADS + h:t * HEADS + h + 1]))
            nc.vector.tensor_scalar(r[:, 1, :], r[:, 0, :], 1.0 / DK, EPS, ALU.mult, ALU.add).then_inc(s.v, 1)
            dve.wait_ge(s.root, 1)
            link(nc.vector.reciprocal(r[:, 2, :], r[:, 2, :]))
            dve.wait_ge(s.norm_in, 16)
            for t in range(NT):
                o = p.o[:, t, :].rearrange("p (h c) -> p h c", h=HEADS)
                link(nc.vector.tensor_tensor(o, o, column(r[:, 2, t * HEADS:(t + 1) * HEADS], HEADS, P), ALU.mult))
                link(nc.vector.tensor_tensor(o, o, across(on[:], HEADS), ALU.mult))
                dve.wait_ge(s.silu, NT + t + 1)
                o2 = p.o[:, t, :].rearrange("p (h c) -> p h c", h=2)
                nc.vector.tensor_tensor(o2, o2, zs[:, :, t, :], ALU.mult).then_inc(s.ready, 1)
    st.close()


def rank_in_eights(nc, link, src, gt, eq, before, rank):
    n = src.shape[1]
    other, own = src.unsqueeze(2).to_broadcast([P, n, 8, 8]), src.unsqueeze(3).to_broadcast([P, n, 8, 8])
    earlier = before.rearrange("p (i j) -> p i j", i=8).unsqueeze(1).to_broadcast([P, n, 8, 8])
    link(nc.vector.tensor_tensor(gt, other, own, ALU.is_gt))
    link(nc.vector.tensor_tensor(eq, other, own, ALU.is_equal))
    link(nc.vector.tensor_tensor(eq, eq, earlier, ALU.mult))
    link(nc.vector.tensor_tensor(gt, gt, eq, ALU.add))
    link(nc.vector.tensor_reduce(rank, gt, AX_X, ALU.add))


def route_groups_stage(m, tag, hT, router_g, router_e, wt, after):
    nc = m.nc
    st = Stage(m, f"route{tag}")
    rw = st.sb("w", [P, KD, 36])
    lg = st.sb("group_logits", [P, NT, 8])
    le = st.sb("expert_logits", [P, NT, 32])
    gt = st.sb("gt", [P, NT * 4, 8, 8])
    eq = st.sb("eq", [P, NT * 4, 8, 8])
    rk = st.sb("rank", [P, NT * 4, 8])
    ge = st.sb("group_rank", [P, NT, 8])
    c = st.sb("cols", [P, 6, NT])
    s = st.sem("in_ logits chain groups_shifted groups_exp shifted exp")
    with st.block() as block:
        @block.sync
        def _(sp):
            sp.dma_start(rw[:, :, 0:4], router_g.rearrange("(k p) n -> p k n", p=P)).then_inc(s.in_, 16)
            sp.dma_start(rw[:, :, 4:36], router_e.rearrange("(k p) n -> p k n", p=P)).then_inc(s.in_, 16)
            m.ring.stream(sp, after)

        @block.tensor
        def _(pe):
            pe.wait_ge(s.in_, 32)
            for t in range(NT):
                for k in range(KD):
                    last = nc.tensor.matmul(m.ps[:, 0, t * 36:(t + 1) * 36], hT[:, k, t * P:(t + 1) * P],
                                            rw[:, k, :], start=(k == 0), stop=(k == KD - 1))
            last.then_inc(s.logits, 1)

        @block.scalar
        def _(act):
            act.wait_ge(s.groups_shifted, 1)
            nc.scalar.activation(ge[:, :, 0:4], ge[:, :, 0:4], ACT.Exp).then_inc(s.groups_exp, 1)
            act.wait_ge(s.shifted, 1)
            nc.scalar.activation(wt, wt, ACT.Exp).then_inc(s.exp, 1)

        @block.vector
        def _(dve):
            link = Linked(dve, s.chain)
            link(nc.vector.memset(lg[:, :, 4:8], NEG))
            dve.wait_ge(s.logits, 1)
            src = m.ps[:, 0, 0:NT * 36].rearrange("p (t c) -> p t c", c=36)
            link(nc.vector.tensor_copy(lg[:, :, 0:4], src[:, :, 0:4]))
            link(nc.vector.tensor_copy(le[:], src[:, :, 4:36]))
            link(nc.vector.tensor_reduce(c[:, 0, :], lg[:], AX_X, ALU.max))
            nc.vector.tensor_tensor(ge[:, :, 0:4], lg[:, :, 0:4], column(c[:, 0, :], NT, 4),
                                    ALU.subtract).then_inc(s.groups_shifted, 1)
            dve.wait_ge(s.groups_exp, 1)
            link(nc.vector.tensor_reduce(c[:, 1, :], ge[:, :, 0:4], AX_X, ALU.add))
            link(nc.vector.reciprocal(c[:, 1, :], c[:, 1, :]))
            rank_in_eights(nc, link, lg[:], gt[:, 0:NT], eq[:, 0:NT], m.before, ge[:])
            link(nc.vector.tensor_scalar(ge[:], ge[:], 0.5, NEG, ALU.is_gt, ALU.mult))
            le8 = le[:].rearrange("p t (g e) -> p t g e", g=4)
            wt8 = wt.rearrange("p t (g e) -> p t g e", g=4)
            link(nc.vector.tensor_tensor(wt8, le8, ge[:, :, 0:4].unsqueeze(3).to_broadcast([P, NT, 4, 8]), ALU.add))
            link(nc.vector.tensor_reduce(c[:, 2, :], wt, AX_X, ALU.max))
            nc.vector.tensor_tensor(wt, wt, column(c[:, 2, :], NT, 32), ALU.subtract).then_inc(s.shifted, 1)
            rank_in_eights(nc, link, le[:].rearrange("p t (g e) -> p (t g) e", e=8), gt[:], eq[:], m.before, rk[:])
            link(nc.vector.tensor_scalar(rk[:], rk[:], 1.5, None, ALU.is_lt))
            dve.wait_ge(s.exp, 1)
            link(nc.vector.tensor_tensor(wt, wt, rk[:].rearrange("p (t g) e -> p t (g e)", t=NT), ALU.mult))
            link(nc.vector.tensor_reduce(c[:, 3, :], wt, AX_X, ALU.add))
            link(nc.vector.reciprocal(c[:, 3, :], c[:, 3, :]))
            link(nc.vector.tensor_tensor(c[:, 4, :], c[:, 3, :], c[:, 1, :], ALU.mult))
            link(nc.vector.tensor_tensor(wt, wt, column(c[:, 4, :], NT, 32), ALU.mult))
    st.close()


def route_sigmoid_stage(m, tag, hT, router, bias, wt, after):
    nc = m.nc
    st = Stage(m, f"route{tag}")
    rw = st.sb("w", [P, KD, E2])
    bb = st.sb("bias", [P, E2])
    sc = st.sb("scores", [P, NT, E2])
    ch = st.sb("choice", [P, NT, E2])
    gt = st.sb("gt", [P, NT * 8, 8, 8])
    eq = st.sb("eq", [P, NT * 8, 8, 8])
    rk = st.sb("rank", [P, NT * 8, 8])
    gs = st.sb("group", [P, NT, 8])
    gr = st.sb("group_rank", [P, NT, 8])
    top = st.sb("top", [P, NT, 8])
    c = st.sb("cols", [P, NT])
    s = st.sem("in_ logits chain scores")
    with st.block() as block:
        @block.sync
        def _(sp):
            sp.dma_start(rw[:], router.rearrange("(k p) n -> p k n", p=P)).then_inc(s.in_, 16)
            sp.dma_start(bb[:], bias.partition_broadcast(P)).then_inc(s.in_, 16)
            m.ring.stream(sp, after)

        @block.tensor
        def _(pe):
            pe.wait_ge(s.in_, 32)
            for t in range(NT):
                for k in range(KD):
                    last = nc.tensor.matmul(m.ps[:, 0, t * E2:(t + 1) * E2], hT[:, k, t * P:(t + 1) * P],
                                            rw[:, k, :], start=(k == 0), stop=(k == KD - 1))
            last.then_inc(s.logits, 1)

        @block.scalar
        def _(act):
            act.wait_ge(s.logits, 1)
            nc.scalar.activation(sc[:], m.ps[:, 0, 0:NT * E2].rearrange("p (t e) -> p t e", t=NT),
                                 ACT.Sigmoid).then_inc(s.scores, 1)

        @block.vector
        def _(dve):
            link = Linked(dve, s.chain)
            dve.wait_ge(s.in_, 32)
            dve.wait_ge(s.scores, 1)
            link(nc.vector.tensor_tensor(ch[:], sc[:], across(bb[:], NT), ALU.add))
            ch8 = ch[:].rearrange("p t (g e) -> p (t g) e", e=8)
            rank_in_eights(nc, link, ch8, gt[:], eq[:], m.before, rk[:])
            link(nc.vector.scalar_tensor_tensor(out=rk[:], in0=rk[:], scalar=1.5, in1=ch8,
                                                op0=ALU.is_lt, op1=ALU.mult))
            link(nc.vector.tensor_reduce(gs[:].rearrange("p t g -> p (t g)"), rk[:], AX_X, ALU.add))
            rank_in_eights(nc, link, gs[:], gt[:, 0:NT], eq[:, 0:NT], m.before, gr[:])
            link(nc.vector.tensor_scalar(gr[:], gr[:], 3.5, NEG, ALU.is_gt, ALU.mult))
            c8 = ch[:].rearrange("p t (g e) -> p t g e", e=8)
            link(nc.vector.tensor_tensor(c8, c8, gr[:].unsqueeze(3).to_broadcast([P, NT, 8, 8]), ALU.add))
            for t in range(NT):
                link(nc.vector.max(top[:, t, :], ch[:, t, :]))
                link(nc.vector.match_replace(wt[:, t, :], top[:, t, :], ch[:, t, :], -3e38))
            link(nc.vector.tensor_tensor(wt, wt, ch[:], ALU.not_equal))
            link(nc.vector.tensor_tensor(wt, wt, sc[:], ALU.mult))
            link(nc.vector.tensor_reduce(c[:], wt, AX_X, ALU.add))
            link(nc.vector.reciprocal(c[:], c[:]))
            link(nc.vector.tensor_scalar(c[:], c[:], 2.5, None, ALU.mult))
            link(nc.vector.tensor_tensor(wt, wt, column(c[:], NT, E2), ALU.mult))
    st.close()


def experts_stage(m, tag, hT, wt, y, first, weights, n_exp, after):
    nc, ring = m.nc, m.ring
    st = Stage(m, f"moe{tag}")
    w1, w3, w2 = weights
    aT = st.sb("aT", [P, 4, T])
    sg = st.sb("sg", [P, 2, T])
    wc = st.sb("wc", [P, NT])
    s = st.sem("gu silu act_done y_ps y_done col")
    slot = [(first + j) % SLOTS for j in range(3)]
    v1, v3, v2 = (whole(KD, 512)(ring.slot(first)), whole(KD, 512)(ring.slot(first + 1)),
                  whole(4, D)(ring.slot(first + 2)))
    with st.block() as block:
        @block.sync
        def _(sp):
            ring.stream(sp, first + 3)
            with sp.Fori(1, n_exp) as e:
                for j, (w, v) in enumerate(((w1, v1), (w3, v3), (w2, v2))):
                    sp.wait_ge(ring.freed[slot[j]], ring.uses(first + j) + e)
                    src = w[bass.ds(e, 1), :, :].rearrange("o (k p) n -> p (o k) n", p=P)
                    sp.dma_start(v, src).then_inc(ring.loaded[slot[j]], 16)
            ring.sent = first + 3 * n_exp
            ring.stream(sp, after)

        @block.tensor
        def _(pe):
            with pe.Fori(0, n_exp) as e:
                for f in range(4):
                    if f == 0:
                        pe.wait_ge(ring.loaded[slot[0]], ring.loads(first) + 16 * e)
                        pe.wait_ge(ring.loaded[slot[1]], ring.loads(first + 1) + 16 * e)
                    pe.wait_ge(s.act_done, 1 + 4 * e + max(f - 1, 0))
                    for w, b in ((v1, 0), (v3, 1)):
                        for k in range(KD):
                            last = nc.tensor.matmul(m.ps[:, 2 * (f % 2) + b, :], w[:, k, f * P:(f + 1) * P],
                                                    hT[:, k, :], start=(k == 0), stop=(k == KD - 1))
                    last.then_inc(s.gu, 1)
                pe.wait_ge(s.gu, 4 * e + 4)
                pe.sem_inc(ring.freed[slot[0]], 1)
                pe.sem_inc(ring.freed[slot[1]], 1)
                pe.wait_ge(ring.loaded[slot[2]], ring.loads(first + 2) + 16 * e)
                pe.wait_ge(s.act_done, 1 + 4 * e + 4)
                for j in range(2 * NT):
                    t, h = j // 2, j % 2
                    pe.wait_ge(s.y_done, 1 + 8 * e + max(j - 3, 0))
                    for f in range(4):
                        last = nc.tensor.matmul(m.ps[:, 4 + j % 4, :], aT[:, f, t * P:(t + 1) * P],
                                                v2[:, f, h * 512:(h + 1) * 512], start=(f == 0), stop=(f == 3))
                    last.then_inc(s.y_ps, 1)
                pe.wait_ge(s.y_ps, 8 * e + 8)
                pe.sem_inc(ring.freed[slot[2]], 1)

        @block.scalar
        def _(act):
            with act.Fori(0, n_exp) as e:
                for f in range(4):
                    act.wait_ge(s.gu, 4 * e + f + 1)
                    act.wait_ge(s.act_done, 1 + 4 * e + max(f - 1, 0))
                    nc.scalar.activation(sg[:, f % 2, :], m.ps[:, 2 * (f % 2), :], ACT.Silu).then_inc(s.silu, 1)

        @block.vector
        def _(dve):
            dve.sem_inc(s.act_done, 1)
            dve.sem_inc(s.y_done, 1)
            with dve.Fori(0, n_exp) as e:
                nc.vector.tensor_copy(wc[:].unsqueeze(2), wt[:, :, bass.ds(e, 1)]).then_inc(s.col, 1)
                for f in range(4):
                    dve.wait_ge(s.silu, 4 * e + f + 1)
                    nc.vector.tensor_tensor(aT[:, f, :], sg[:, f % 2, :], m.ps[:, 2 * (f % 2) + 1, :],
                                            ALU.mult).then_inc(s.act_done, 1)
                dve.wait_ge(s.col, e + 1)
                for j in range(2 * NT):
                    t, h = j // 2, j % 2
                    cols = slice(h * 512, (h + 1) * 512)
                    dve.wait_ge(s.y_ps, 8 * e + j + 1)
                    dve.wait_ge(s.y_done, 1 + 8 * e + max(j - 7, 0))
                    nc.vector.scalar_tensor_tensor(out=y[:, t, cols], in0=m.ps[:, 4 + j % 4, :],
                                                   scalar=wc[:, t:t + 1], in1=y[:, t, cols],
                                                   op0=ALU.mult, op1=ALU.add).then_inc(s.y_done, 1)
                dve.wait_ge(s.y_done, 1 + 8 * e + 8)
    st.close()


def pair_experts_stage(m, tag, hT, wt, y, first, shared, w_gu, w_dn, n_exp, after):
    nc, ring = m.nc, m.ring
    st = Stage(m, f"moe{tag}")
    aT = st.sb("aT", [P, 4, T])
    sg = st.sb("sg", [P, 2, T])
    wc = st.sb("wc", [P, NT, 2])
    s = st.sem("gu silu act_done y_ps y_done col")
    pairs = n_exp // 2
    slot = [(first + 2 + j) % SLOTS for j in range(3)]
    va, vb, vd = (whole(KD, 512)(ring.slot(first + 2)), whole(KD, 512)(ring.slot(first + 3)),
                  whole(4, D)(ring.slot(first + 4)))

    def units_gu(pe, gu, f, b):
        for c0, bk in ((f * P, 0), (256 + f * P, 1)):
            for k in range(KD):
                last = nc.tensor.matmul(m.ps[:, 2 * b + bk, :], gu[:, k, c0:c0 + P], hT[:, k, :],
                                        start=(k == 0), stop=(k == KD - 1))
        return last

    with st.block() as block:
        @block.sync
        def _(sp):
            ring.stream(sp, first + 5)
            with sp.Fori(1, pairs) as e:
                for j in range(2):
                    sp.wait_ge(ring.freed[slot[j]], ring.uses(first + 2 + j) + e)
                    src = w_gu[bass.ds(2 * e + j, 1), :, :].rearrange("o (k p) n -> p (o k) n", p=P)
                    sp.dma_start((va, vb)[j], src).then_inc(ring.loaded[slot[j]], 16)
                sp.wait_ge(ring.freed[slot[2]], ring.uses(first + 4) + e)
                src = w_dn[bass.ds(2 * e, 2), :, :].rearrange("o (k p) n -> p (o k) n", p=P)
                sp.dma_start(vd, src).then_inc(ring.loaded[slot[2]], 16)
            ring.sent = first + 2 + 3 * pairs
            ring.stream(sp, after)

        @block.tensor
        def _(pe):
            sgu = whole(KD, 512)(ring.slot(first))
            sdn = whole(2, D)(ring.slot(first + 1))
            ring.wait(pe, first)
            for f in range(2):
                units_gu(pe, sgu, f, f).then_inc(s.gu, 1)
            pe.wait_ge(s.gu, 2)
            pe.sem_inc(ring.freed[first % SLOTS], 1)
            ring.wait(pe, first + 1)
            pe.wait_ge(s.act_done, 1 + 2)
            for j in range(2 * NT):
                t, h = j // 2, j % 2
                if j >= 4:
                    pe.wait_ge(s.y_done, 1 + j - 3)
                for f in range(2):
                    last = nc.tensor.matmul(m.ps[:, 4 + j % 4, :], aT[:, f, t * P:(t + 1) * P],
                                            sdn[:, f, h * 512:(h + 1) * 512], start=(f == 0), stop=(f == 1))
                last.then_inc(s.y_ps, 1)
            pe.wait_ge(s.y_ps, 8)
            pe.sem_inc(ring.freed[(first + 1) % SLOTS], 1)
            with pe.Fori(0, pairs) as e:
                for x, gu in enumerate((va, vb)):
                    pe.wait_ge(ring.loaded[slot[x]], ring.loads(first + 2 + x) + 16 * e)
                    for f in range(2):
                        pe.wait_ge(s.act_done, 1 + 2 + 4 * e + max(2 * x + f - 1, 0))
                        units_gu(pe, gu, f, f).then_inc(s.gu, 1)
                    pe.wait_ge(s.gu, 4 * e + 2 * x + 4)
                    pe.sem_inc(ring.freed[slot[x]], 1)
                pe.wait_ge(ring.loaded[slot[2]], ring.loads(first + 4) + 16 * e)
                pe.wait_ge(s.act_done, 1 + 4 * e + 6)
                for j in range(4 * NT):
                    x, t, h = j // 8, (j % 8) // 2, j % 2
                    pe.wait_ge(s.y_done, 1 + 8 + 16 * e + max(j - 3, 0))
                    for f in range(2):
                        last = nc.tensor.matmul(m.ps[:, 4 + j % 4, :], aT[:, 2 * x + f, t * P:(t + 1) * P],
                                                vd[:, 2 * x + f, h * 512:(h + 1) * 512],
                                                start=(f == 0), stop=(f == 1))
                    last.then_inc(s.y_ps, 1)
                pe.wait_ge(s.y_ps, 16 * e + 24)
                pe.sem_inc(ring.freed[slot[2]], 1)

        @block.scalar
        def _(act):
            for f in range(2):
                act.wait_ge(s.gu, f + 1)
                nc.scalar.activation(sg[:, f, :], m.ps[:, 2 * f, :], ACT.Silu).then_inc(s.silu, 1)
            with act.Fori(0, pairs) as e:
                for f in range(4):
                    act.wait_ge(s.gu, 2 + 4 * e + f + 1)
                    act.wait_ge(s.act_done, 1 + 2 + 4 * e + max(f - 1, 0))
                    nc.scalar.activation(sg[:, f % 2, :], m.ps[:, 2 * (f % 2), :], ACT.Silu).then_inc(s.silu, 1)

        @block.vector
        def _(dve):
            dve.sem_inc(s.act_done, 1)
            dve.sem_inc(s.y_done, 1)
            for f in range(2):
                dve.wait_ge(s.silu, f + 1)
                nc.vector.tensor_tensor(aT[:, f, :], sg[:, f, :], m.ps[:, 2 * f + 1, :],
                                        ALU.mult).then_inc(s.act_done, 1)
            for j in range(2 * NT):
                t, h = j // 2, j % 2
                cols = slice(h * 512, (h + 1) * 512)
                dve.wait_ge(s.y_ps, j + 1)
                nc.vector.tensor_tensor(y[:, t, cols], m.ps[:, 4 + j % 4, :], y[:, t, cols],
                                        ALU.add).then_inc(s.y_done, 1)
            dve.wait_ge(s.y_done, 1 + 8)
            with dve.Fori(0, pairs) as e:
                nc.vector.tensor_copy(wc[:], wt[:, :, bass.ds(2 * e, 2)]).then_inc(s.col, 1)
                for f in range(4):
                    dve.wait_ge(s.silu, 2 + 4 * e + f + 1)
                    nc.vector.tensor_tensor(aT[:, f, :], sg[:, f % 2, :], m.ps[:, 2 * (f % 2) + 1, :],
                                            ALU.mult).then_inc(s.act_done, 1)
                dve.wait_ge(s.col, e + 1)
                for j in range(4 * NT):
                    x, t, h = j // 8, (j % 8) // 2, j % 2
                    cols = slice(h * 512, (h + 1) * 512)
                    dve.wait_ge(s.y_ps, 8 + 16 * e + j + 1)
                    dve.wait_ge(s.y_done, 1 + 8 + 16 * e + max(j - 7, 0))
                    nc.vector.scalar_tensor_tensor(out=y[:, t, cols], in0=m.ps[:, 4 + j % 4, :],
                                                   scalar=wc[:, t, x:x + 1], in1=y[:, t, cols],
                                                   op0=ALU.mult, op1=ALU.add).then_inc(s.y_done, 1)
                dve.wait_ge(s.y_done, 1 + 24 + 16 * e)
    st.close()


def residual_stage(m, tag, y, gate, after, gain=None, out=None):
    nc = m.nc
    st = Stage(m, f"res{tag}")
    gb = st.sb("gain", [P, D])
    junk = st.sb("junk", [P, D])
    r = st.sb("r", [P, 3, NT])
    s = st.sem("gain_in chain v root done out")
    with st.block() as block:
        @block.sync
        def _(sp):
            if gain is not None:
                sp.dma_start(gb[:], gain.partition_broadcast(P)).then_inc(s.gain_in, 16)
            m.ring.stream(sp, after)
            if out is not None:
                for t in range(NT):
                    sp.wait_ge(s.done, t + 1)
                    sp.dma_start(out[t * P:(t + 1) * P, :], m.x[:, t, :]).then_inc(s.out, 16)
                sp.wait_ge(s.out, 16 * NT)

        @block.scalar
        def _(act):
            if gain is not None:
                act.wait_ge(s.v, 1)
                nc.scalar.activation(r[:, 2, :], r[:, 1, :], ACT.Sqrt).then_inc(s.root, 1)

        @block.vector
        def _(dve):
            link = Linked(dve, s.chain)
            for t in range(NT):
                link(nc.vector.tensor_tensor(y[:, t, :], y[:, t, :], gate, ALU.mult))
                link(nc.vector.tensor_tensor(m.x[:, t, :], m.x[:, t, :], y[:, t, :], ALU.add))
                if gain is not None:
                    link(nc.vector.tensor_tensor_reduce(out=junk[:], in0=m.x[:, t, :], in1=m.x[:, t, :],
                                                        scale=1.0, scalar=0.0, op0=ALU.mult, op1=ALU.add,
                                                        accum_out=r[:, 0, t:t + 1]))
            if gain is not None:
                nc.vector.tensor_scalar(r[:, 1, :], r[:, 0, :], 1.0 / D, EPS, ALU.mult, ALU.add).then_inc(s.v, 1)
                dve.wait_ge(s.v, 1)
                dve.wait_ge(s.root, 1)
                q, v, a = r[:, 2, :], r[:, 1, :], r[:, 0, :]
                link(nc.vector.reciprocal(q, q))
                link(nc.vector.tensor_tensor(a, q, q, ALU.mult))
                link(nc.vector.tensor_tensor(a, a, v, ALU.mult))
                link(nc.vector.tensor_scalar(a, a, -0.5, 1.5, ALU.mult, ALU.add))
                link(nc.vector.tensor_tensor(q, q, a, ALU.mult))
                dve.wait_ge(s.gain_in, 16)
                for t in range(NT):
                    nc.vector.scalar_tensor_tensor(out=m.x[:, t, :], in0=m.x[:, t, :], scalar=q[:, t:t + 1],
                                                   in1=gb[:], op0=ALU.mult, op1=ALU.mult).then_inc(s.done, 1)
    st.close()


def shortconv_stage(m, hT, yT, first, conv, after):
    nc, ring = m.nc, m.ring
    st = Stage(m, "conv")
    W = 64
    cw = st.sb("w", [P, 3, KD])
    u_ = st.sb("u", [P, 2, T + 2 * W])
    cg = st.sb("cg", [P, 2, T])
    acc = st.sb("acc", [P, 2, T])
    s = st.sem("w_in zeroed product c_there u_there chain acc done")
    with st.block() as block:
        @block.sync
        def _(sp):
            for j in range(3):
                sp.dma_start(cw[:, j, :], conv[j, :].rearrange("(k p) -> p k", p=P),
                             allow_slow_non_contiguous=True).then_inc(s.w_in, 16)
            ring.stream(sp, after)

        @block.gpsimd
        def _(pool):
            nc.gpsimd.memset(u_[:], 0.0).then_inc(s.zeroed, 1)

        @block.tensor
        def _(pe):
            for c in range(KD):
                half, q = c // 4, c % 4
                if c >= 2:
                    pe.wait_ge(s.done, c - 1)
                for j in range(3):
                    n = first + 3 * half + j
                    if q == 0:
                        ring.wait(pe, n)
                    w = whole(KD, 512)(ring.slot(n))
                    for k in range(KD):
                        last = nc.tensor.matmul(m.ps[:, 4 * (c % 2) + j, :], w[:, k, q * P:(q + 1) * P],
                                                hT[:, k, :], start=(k == 0), stop=(k == KD - 1))
                last.then_inc(s.product, 1)
                if q == 3:
                    pe.wait_ge(s.product, c + 1)
                    for j in range(3):
                        pe.sem_inc(ring.freed[(first + 3 * half + j) % SLOTS], 1)

        @block.scalar
        def _(act):
            for c in range(KD):
                act.wait_ge(s.product, c + 1)
                if c >= 2:
                    act.wait_ge(s.u_there, c - 1)
                nc.scalar.activation(cg[:, c % 2, :], m.ps[:, 4 * (c % 2) + 1, :], ACT.Copy).then_inc(s.c_there, 1)

        @block.vector
        def _(dve):
            link = Linked(dve, s.chain)
            dve.wait_ge(s.w_in, 48)
            dve.wait_ge(s.zeroed, 1)
            for c in range(KD):
                b = c % 2
                mid = u_[:, b, W:W + T]
                dve.wait_ge(s.c_there, c + 1)
                nc.vector.tensor_tensor(mid, cg[:, b, :], m.ps[:, 4 * b + 2, :], ALU.mult).then_inc(s.u_there, 1)
                dve.wait_ge(s.u_there, c + 1)
                taps = [cw[:, j, c:c + 1] for j in range(3)]
                a = acc[:, b, :]
                link(nc.vector.tensor_scalar(a, mid, taps[1], None, ALU.mult))
                if c < KD // 2:
                    g = mid.rearrange("p (r w) -> p r w", w=W)
                    ag = a.rearrange("p (r w) -> p r w", w=W)
                    link(nc.vector.scalar_tensor_tensor(out=ag[:, :, 1:W], in0=g[:, :, 0:W - 1], scalar=taps[0],
                                                        in1=ag[:, :, 1:W], op0=ALU.mult, op1=ALU.add))
                    link(nc.vector.scalar_tensor_tensor(out=ag[:, :, 0:W - 1], in0=g[:, :, 1:W], scalar=taps[2],
                                                        in1=ag[:, :, 0:W - 1], op0=ALU.mult, op1=ALU.add))
                else:
                    link(nc.vector.scalar_tensor_tensor(out=a, in0=u_[:, b, 0:T], scalar=taps[0],
                                                        in1=a, op0=ALU.mult, op1=ALU.add))
                    link(nc.vector.scalar_tensor_tensor(out=a, in0=u_[:, b, 2 * W:2 * W + T], scalar=taps[2],
                                                        in1=a, op0=ALU.mult, op1=ALU.add))
                nc.vector.tensor_tensor(yT[:, c, :], a, m.ps[:, 4 * b, :], ALU.mult).then_inc(s.done, 1)
    st.close()


HW = 4 * P
SUB = 16
NS = P // SUB


def mix_columns(m, p, hT, first, kv, after):
    nc, ring = m.nc, m.ring
    st = Stage(m, "mixin")
    s = st.sem("product moved chain lb_in lb_max lb_exp lb")
    lg = st.sb("lb", [P, 6, 4])
    U = []
    for h in range(4):
        U.append((first, h * P, P, True, p.q[:, h, :], ACT.Copy))
    for h in range(4):
        U.append((first + 1, h * P, P, True, p.f[:, h, :], ACT.Sigmoid))
    for t in range(NT):
        U.append((first + 2, 0, 512, t, p.v[:, t, :], ACT.Copy))
    for h in range(4):
        U.append((first + 3, h * P, P, True, p.gate[:, h, :], ACT.Silu))
    for h in range(4):
        U.append((first + 4, h * P, P, True, p.nq[:, h, :], ACT.Copy))
    for c, dst in ((0, p.kc), (P, p.vc), (2 * P, p.ks)):
        U.append((kv, c, P, True, dst[:], ACT.Copy))
    for t in range(NT):
        U.append((kv, 3 * P, P, t, p.vs[:, t, :], ACT.Copy))
    U.append((kv + 1, 0, P, True, p.kw[:], ACT.Copy))
    for t in range(NT):
        U.append((kv + 1, P, P, t, p.vw[:, t, :], ACT.Copy))
    for t in range(NT):
        U.append((kv + 1, 2 * P, 24, t, p.ng[:, t, :], ACT.Sigmoid))
    with st.block() as block:
        @block.sync
        def _(sp):
            for i in range(2):
                sp.dma_start(lg[:, i, :], p.lb_logits[i, :].rearrange("(k p) -> p k", p=P),
                             allow_slow_non_contiguous=True).then_inc(s.lb_in, 16)
            ring.stream(sp, after)

        @block.tensor
        def _(pe):
            for u, (n, c0, width, tile, dst, _) in enumerate(U):
                if u == 0 or U[u - 1][0] != n:
                    ring.wait(pe, n)
                wn = 512 if n < kv + 1 else W_IN2 - 3072
                w = whole(KD, wn)(ring.slot(n))
                if u >= 4:
                    pe.wait_ge(s.moved, u - 3)
                for k in range(KD):
                    if tile is True:
                        last = nc.tensor.matmul(m.ps[:, u % 4, :], w[:, k, c0:c0 + P], hT[:, k, :],
                                                start=(k == 0), stop=(k == KD - 1))
                    else:
                        last = nc.tensor.matmul(m.ps[:, u % 4, 0:width], hT[:, k, tile * P:(tile + 1) * P],
                                                w[:, k, c0:c0 + width], start=(k == 0), stop=(k == KD - 1))
                last.then_inc(s.product, 1)
                if u + 1 == len(U) or U[u + 1][0] != n:
                    pe.wait_ge(s.product, u + 1)
                    pe.sem_inc(ring.freed[n % SLOTS], 1)

        @block.scalar
        def _(act):
            for u, (_, _, width, tile, dst, fn) in enumerate(U):
                act.wait_ge(s.product, u + 1)
                w = T if tile is True else width
                nc.scalar.activation(dst, m.ps[:, u % 4, 0:w], fn).then_inc(s.moved, 1)
            act.wait_ge(s.lb_max, 1)
            nc.scalar.activation(lg[:, 3:5, :], lg[:, 3:5, :], ACT.Exp).then_inc(s.lb_exp, 1)

        @block.vector
        def _(dve):
            link = Linked(dve, s.chain)
            dve.wait_ge(s.lb_in, 32)
            link(nc.vector.tensor_tensor(lg[:, 2, :], lg[:, 0, :], lg[:, 1, :], ALU.max))
            link(nc.vector.tensor_tensor(lg[:, 3, :], lg[:, 0, :], lg[:, 2, :], ALU.subtract))
            nc.vector.tensor_tensor(lg[:, 4, :], lg[:, 1, :], lg[:, 2, :], ALU.subtract).then_inc(s.lb_max, 1)
            dve.wait_ge(s.lb_exp, 1)
            link(nc.vector.tensor_tensor(lg[:, 5, :], lg[:, 3, :], lg[:, 4, :], ALU.add))
            link(nc.vector.reciprocal(lg[:, 5, :], lg[:, 5, :]))
            link(nc.vector.tensor_tensor(lg[:, 3, :], lg[:, 3, :], lg[:, 5, :], ALU.mult))
            link(nc.vector.tensor_scalar(lg[:, 4, :], lg[:, 3, :], -1.0, 1.0, ALU.mult, ALU.add))
            for h in range(4):
                link(nc.vector.tensor_scalar(p.f[:, h, :], p.f[:, h, :], lg[:, 4, h:h + 1], lg[:, 3, h:h + 1],
                                             ALU.mult, ALU.add))
                link(nc.vector.tensor_scalar(p.k[:, h, :], p.f[:, h, :], -1.0, 1.0, ALU.mult, ALU.add))
                link(nc.vector.tensor_scalar(p.q[:, h, :], p.q[:, h, :], P ** -0.5, None, ALU.mult))
    st.close()


def mask(p, name):
    at, n = p.where[name]
    return p.masks[:, at:at + n]


def hgrn_prepare(m, p):
    nc = m.nc
    st = Stage(m, "hgprep")
    wq = st.sb("wq", [P, 4, T])
    dd = st.sb("pair", [P, 2, 4, T])
    rr = st.sb("suffix", [P, 4, T])
    s = st.sem("zeroed chain updated paired banded moved pool_chain")
    sub = lambda ap: ap.rearrange("p h (c s) -> p (h c) s", s=SUB)
    with st.block() as block:
        @block.gpsimd
        def _(pool):
            nc.gpsimd.memset(dd[:], 0.0).then_inc(s.zeroed, 1)
            link = Linked(pool, s.pool_chain)
            f, pr, kd = sub(p.f[:]), sub(p.qd[:]), sub(p.kd[:])
            link(nc.gpsimd.tensor_copy(p.qd[:], p.f[:]))
            link(nc.gpsimd.memset(p.kd[:], 1.0))
            link(nc.gpsimd.tensor_copy(kd[:, :, 0:SUB - 1], f[:, :, 1:SUB]))
            for n in (1, 2, 4, 8):
                r = sub(rr[:])
                link(nc.gpsimd.tensor_tensor(r[:, :, n:SUB], pr[:, :, n:SUB], pr[:, :, 0:SUB - n], ALU.mult))
                link(nc.gpsimd.tensor_copy(pr[:, :, n:SUB], r[:, :, n:SUB]))
                link(nc.gpsimd.tensor_tensor(r[:, :, 0:SUB - n], kd[:, :, 0:SUB - n], kd[:, :, n:SUB], ALU.mult))
                link(nc.gpsimd.tensor_copy(kd[:, :, 0:SUB - n], r[:, :, 0:SUB - n]))
            link(nc.gpsimd.tensor_copy(p.last[:].unsqueeze(2), pr[:, :, SUB - 1:SUB]))
            link(nc.gpsimd.tensor_tensor(p.qd[:], p.qd[:], p.q[:], ALU.mult))
            link(nc.gpsimd.tensor_tensor(p.kd[:], p.kd[:], p.k[:], ALU.mult))

        @block.vector
        def _(dve):
            link = Linked(dve, s.chain)
            link(nc.vector.tensor_copy(wq[:], p.q[:]))
            dve.wait_ge(s.zeroed, 1)
            w, f, k = sub(wq[:]), sub(p.f[:]), sub(p.k[:])
            for d in range(SUB):
                if d:
                    dve.wait_ge(s.paired, d)
                    link(nc.vector.tensor_tensor(w[:, :, d:SUB], w[:, :, d:SUB], f[:, :, 1:SUB - d + 1], ALU.mult))
                if d >= 2:
                    dve.wait_ge(s.banded, d - 1)
                pair = sub(dd[:, d % 2, :, :])
                nc.vector.tensor_tensor(pair[:, :, d:SUB], w[:, :, d:SUB], k[:, :, 0:SUB - d],
                                        ALU.mult).then_inc(s.paired, 1)
            dve.wait_ge(s.banded, SUB)
            nc.vector.tensor_copy(p.band[:], m.ps[:, 0, 0:16 * SUB].rearrange("p (u d) -> p u d", d=SUB)
                                  ).then_inc(s.moved, 1)

        @block.tensor
        def _(pe):
            for d in range(SUB):
                pe.wait_ge(s.paired, d + 1)
                for u in range(16):
                    h, t = u // 4, u % 4
                    last = nc.tensor.matmul(m.ps[:, 0, u * SUB + d:u * SUB + d + 1],
                                            dd[:, d % 2, h, t * P:(t + 1) * P], m.ones[:, 0:1],
                                            start=True, stop=True)
                last.then_inc(s.banded, 1)
    st.close()


def hgrn_scan(m, p, mT):
    nc = m.nc
    st = Stage(m, "hgscan")
    loc = st.sb("local", [P, 16, SUB])
    prod = st.sb("prod", [P, 16, SUB])
    dense = st.sb("dense", [P, 2, P])
    aT = st.sb("aT", [P, 2, P])
    kt = st.sb("kt", [P, 2, P])
    vm = st.sb("vm", [P, 2, NS, P])
    S = st.sb("S", [P, 4, NS + 1, P])
    o = p.q
    g = st.sb("norm", [P, 4])
    s = st.sem("g_in zeroed chain local dense a_turned a_moved k_turned k_moved v_masked kv state o_ps o_moved "
               "square summed root done carried")
    units = [(t, h) for t in range(NT) for h in range(4)]
    with st.block() as block:
        @block.sync
        def _(sp):
            sp.dma_start(g[:], p.hg_norm.rearrange("(k p) -> p k", p=P),
                         allow_slow_non_contiguous=True).then_inc(s.g_in, 16)

        @block.gpsimd
        def _(pool):
            nc.gpsimd.memset(S[:, :, 0, :], 0.0).then_inc(s.zeroed, 1)
            for u, (t, h) in enumerate(units):
                if u >= 2:
                    pool.wait_ge(s.kv, u - 1)
                v = p.v[:, t, h * P:(h + 1) * P]
                nc.gpsimd.tensor_tensor(vm[:, u % 2, :, :], across(v, NS), column(mask(p, "chunk"), NS, P),
                                        ALU.mult).then_inc(s.v_masked, 1)

        @block.vector
        def _(dve):
            link = Linked(dve, s.chain)
            sh = mask(p, "shift").rearrange("p (d s) -> p d s", s=SUB)
            for d in range(SUB):
                dst = loc if d == 0 else prod
                link(nc.vector.tensor_tensor(dst[:], across(sh[:, d, :], 16),
                                             p.band[:, :, d:d + 1].to_broadcast([P, 16, SUB]), ALU.mult))
                if d:
                    link(nc.vector.tensor_tensor(loc[:], loc[:], prod[:], ALU.add))
            dve.wait_ge(s.zeroed, 1)
            sp_ = mask(p, "spread").rearrange("p (c s) -> p c s", s=SUB)
            for u, (t, h) in enumerate(units):
                if u >= 2:
                    dve.wait_ge(s.a_turned, u - 1)
                nc.vector.tensor_tensor(dense[:, u % 2, :].rearrange("p (c s) -> p c s", s=SUB),
                                        across(loc[:, h * 4 + t, :], NS), sp_, ALU.mult).then_inc(s.dense, 1)
                dve.wait_ge(s.kv, u + 1)
                if t:
                    dve.wait_ge(s.o_ps, u - 3)
                    link(nc.vector.tensor_copy(S[:, h, 0, :], S[:, h, NS, :]))
                for c in range(NS):
                    last = nc.vector.scalar_tensor_tensor(
                        out=S[:, h, c + 1, :], in0=S[:, h, c, :], scalar=p.last[:, h * 32 + t * NS + c:h * 32 + t * NS + c + 1],
                        in1=m.ps[:, (u % 2) * 2 + c // 4, (c % 4) * P:(c % 4 + 1) * P], op0=ALU.mult, op1=ALU.add)
                    if c < NS - 1:
                        link(last)
                last.then_inc(s.state, 1)
                dve.wait_ge(s.state, u + 1)
            for h in range(4):
                dve.wait_ge(s.o_moved, 13 + h)
                nc.vector.tensor_tensor(p.qd[:, h, :], o[:, h, :], o[:, h, :], ALU.mult).then_inc(s.square, 1)
            dve.wait_ge(s.g_in, 16)
            for h in range(4):
                r = p.kd[:, h, :]
                dve.wait_ge(s.root, h + 1)
                link(nc.vector.reciprocal(r, r))
                link(nc.vector.tensor_tensor(r, r, o[:, h, :], ALU.mult))
                nc.vector.scalar_tensor_tensor(out=mT[:, h, :], in0=r, scalar=g[:, h:h + 1], in1=p.gate[:, h, :],
                                               op0=ALU.mult, op1=ALU.mult).then_inc(s.done, 1)

        @block.scalar
        def _(act):
            def move_out(u):
                t, h = units[u]
                act.wait_ge(s.o_ps, u + 1)
                nc.scalar.activation(o[:, h, t * P:(t + 1) * P], m.ps[:, 6 + u % 2, 0:P], ACT.Copy).then_inc(s.o_moved, 1)

            for u, (t, h) in enumerate(units):
                act.wait_ge(s.k_turned, u + 1)
                if u >= 2:
                    act.wait_ge(s.kv, u - 1)
                nc.scalar.activation(kt[:, u % 2, :], m.ps[:, 4, 0:P], ACT.Copy).then_inc(s.k_moved, 1)
                act.wait_ge(s.a_turned, u + 1)
                if u >= 2:
                    act.wait_ge(s.o_ps, u - 1)
                nc.scalar.activation(aT[:, u % 2, :], m.ps[:, 5, 0:P], ACT.Copy).then_inc(s.a_moved, 1)
                if u:
                    move_out(u - 1)
            move_out(len(units) - 1)
            for h in range(4):
                act.wait_ge(s.summed, h + 1)
                nc.scalar.activation(p.kd[:, h, :], m.ps[:, h, :], ACT.Sqrt, bias=m.eps[:],
                                     scale=1.0 / P).then_inc(s.root, 1)

        @block.tensor
        def _(pe):
            def turn(u):
                t, h = units[u]
                if u:
                    pe.wait_ge(s.k_moved, u)
                nc.tensor.transpose(m.ps[:, 4, 0:P], p.kd[:, h, t * P:(t + 1) * P], m.ident).then_inc(s.k_turned, 1)
                pe.wait_ge(s.dense, u + 1)
                if u:
                    pe.wait_ge(s.a_moved, u)
                nc.tensor.transpose(m.ps[:, 5, 0:P], dense[:, u % 2, :], m.ident).then_inc(s.a_turned, 1)

            def outer(u):
                pe.wait_ge(s.k_moved, u + 1)
                pe.wait_ge(s.v_masked, u + 1)
                if u >= 2:
                    pe.wait_ge(s.state, u - 1)
                for q in range(2):
                    last = nc.tensor.matmul(m.ps[:, (u % 2) * 2 + q, :], kt[:, u % 2, :],
                                            flat(vm[:, u % 2, 4 * q:4 * q + 4, :]), start=True, stop=True)
                last.then_inc(s.kv, 1)

            def output(u):
                t, h = units[u]
                pe.wait_ge(s.a_moved, u + 1)
                pe.wait_ge(s.state, u + 1)
                if u >= 2:
                    pe.wait_ge(s.o_moved, u - 1)
                out = m.ps[:, 6 + u % 2, 0:P]
                nc.tensor.matmul(out, p.v[:, t, h * P:(h + 1) * P], aT[:, u % 2, :], start=True, stop=False)
                for c in range(NS):
                    last = nc.tensor.matmul(out[:, c * SUB:(c + 1) * SUB], S[:, h, c, :],
                                            p.qd[:, h, t * P + c * SUB:t * P + (c + 1) * SUB],
                                            start=False, stop=(c == NS - 1))
                last.then_inc(s.o_ps, 1)

            for u in range(len(units)):
                turn(u)
                outer(u)
                if u:
                    output(u - 1)
            output(len(units) - 1)
            for h in range(4):
                pe.wait_ge(s.square, h + 1)
                nc.tensor.matmul(m.ps[:, h, :], m.ones, p.qd[:, h, :], start=True, stop=True).then_inc(s.summed, 1)
    st.close()


NC = 31


def compress_stage(m, p, first, after):
    nc, ring = m.nc, m.ring
    st = Stage(m, "cmp")
    pos = st.sb("pos", [P, 2, 32])
    xin = st.sb("xin", [P, 2, 32, NC])
    b1 = st.sb("b1", [1, 2, 256])
    w2 = st.sb("w2", [P, 2, 2, 2, 64])
    g = st.sb("g", [NC, 4, 2, 256])
    gT = st.sb("gT", [P, 4, 2, NC])
    s = st.sem("in_ chain xin product moved tanh gelu turned t_moved final f_moved")
    units = [(x, gr) for x in range(2) for gr in range(2)]
    with st.block() as block:
        @block.sync
        def _(sp):
            for x in range(2):
                for half in range(2):
                    sp.dma_start(pos[64 * half:64 * half + 64, x, :], p.pos[x].rearrange("l d -> d l"),
                                 allow_slow_non_contiguous=True).then_inc(s.in_, 16)
                    sp.dma_start(w2[:, x, :, half, :], p.w2[x].rearrange("(k p) d -> p k d", p=P)).then_inc(s.in_, 16)
                sp.dma_start(b1[:, x, :], p.b1[x].unsqueeze(0)).then_inc(s.in_, 16)
            ring.stream(sp, after)

        @block.vector
        def _(dve):
            link = Linked(dve, s.chain)
            dve.wait_ge(s.in_, 160)
            for x, src in enumerate((p.kc, p.vc)):
                for l in range(32):
                    tok = src[:, l:l + 16 * (NC - 1) + 1:16]
                    last = nc.vector.tensor_scalar(xin[:, x, l, :], tok, pos[:, x, l:l + 1], None, ALU.add)
                last.then_inc(s.xin, 1)
            for u in range(4):
                a, b = g[:, u, 0, :], g[:, u, 1, :]
                dve.wait_ge(s.product, u + 1)
                link(nc.vector.tensor_copy(a, m.ps[0:NC, u, 0:256]))
                link(nc.vector.tensor_tensor(b, a, a, ALU.mult))
                link(nc.vector.tensor_scalar(b, b, 0.044715, 1.0, ALU.mult, ALU.add))
                nc.vector.tensor_tensor(b, b, a, ALU.mult).then_inc(s.moved, 1)
                dve.wait_ge(s.tanh, u + 1)
                nc.vector.tensor_tensor(a, a, b, ALU.mult).then_inc(s.gelu, 1)

        @block.scalar
        def _(act):
            for u in range(4):
                act.wait_ge(s.moved, u + 1)
                nc.scalar.activation(g[:, u, 1, :], g[:, u, 1, :], ACT.Sigmoid,
                                     scale=2.0 * (2.0 / np.pi) ** 0.5).then_inc(s.tanh, 1)
            for u in range(4):
                act.wait_ge(s.turned, u + 1)
                nc.scalar.activation(gT[:, u, :, :],
                                     m.ps[:, 4 + u, 0:2 * NC].rearrange("p (k c) -> p k c", k=2),
                                     ACT.Copy).then_inc(s.t_moved, 1)
            for u, (x, gr) in enumerate(units):
                act.wait_ge(s.final, u + 1)
                if x == 0:
                    nc.scalar.activation(p.kcmp[:, gr, :], m.ps[:, u, 0:NC], ACT.Copy).then_inc(s.f_moved, 1)
                else:
                    nc.scalar.activation(p.vpad_c[:, gr, 64:128], m.ps[0:NC, u, 0:64], ACT.Copy).then_inc(s.f_moved, 1)

        @block.tensor
        def _(pe):
            pe.wait_ge(s.in_, 160)
            for x in range(2):
                pe.wait_ge(s.xin, x + 1)
                for gr in range(2):
                    u, rows = 2 * x + gr, slice(64 * gr, 64 * gr + 64)
                    for half in range(2):
                        n = first + 2 * x + half
                        if gr == 0:
                            ring.wait(pe, n)
                        w = ring.slot(n)[rows, :].rearrange("p (l n) -> p l n", l=16)
                        for l in range(16):
                            nc.tensor.matmul(m.ps[0:NC, u, 0:256], xin[rows, x, 16 * half + l, :], w[:, l, :],
                                             start=(half == 0 and l == 0), stop=False)
                    last = nc.tensor.matmul(m.ps[0:NC, u, 0:256], m.ones[0:1, 0:NC], b1[0:1, x, :],
                                            start=False, stop=True)
                    last.then_inc(s.product, 1)
                pe.wait_ge(s.product, 2 * x + 2)
                for half in range(2):
                    pe.sem_inc(ring.freed[(first + 2 * x + half) % SLOTS], 1)
            for u in range(4):
                pe.wait_ge(s.gelu, u + 1)
                for k in range(2):
                    last = nc.tensor.transpose(m.ps[:, 4 + u, k * NC:(k + 1) * NC], g[:, u, 0, k * P:(k + 1) * P],
                                               m.ident[0:NC, 0:NC])
                last.then_inc(s.turned, 1)
            for u, (x, gr) in enumerate(units):
                pe.wait_ge(s.t_moved, u + 1)
                for k in range(2):
                    if x == 0:
                        last = nc.tensor.matmul(m.ps[:, u, 0:NC], flat(w2[:, 0, k, :, :]), gT[:, u, k, :],
                                                start=(k == 0), stop=(k == 1))
                    else:
                        last = nc.tensor.matmul(m.ps[0:NC, u, 0:64], gT[:, u, k, :], w2[:, 1, k, 0, :],
                                                start=(k == 0), stop=(k == 1))
                last.then_inc(s.final, 1)
    st.close()


def rope_stage(m, p):
    nc = m.nc
    st = Stage(m, "rope")
    tmp = st.sb("tmp", [P, 2, T])
    s = st.sem("zeroed vals rotated mixed added krot dup moved")
    src = [p.nq[:, c, :] for c in range(4)] + [p.ks[:], p.kw[:]]
    dst = [p.qr[:, c, :] for c in range(4)] + [p.kc[:], p.vc[:]]
    with st.block() as block:
        @block.gpsimd
        def _(pool):
            nc.gpsimd.memset(p.vpad[:], 0.0).then_inc(s.zeroed, 1)
            pool.wait_ge(s.zeroed, 1)
            for i, v in enumerate((p.vs, p.vw)):
                for t in range(NT):
                    nc.gpsimd.tensor_copy(p.vpad[:, i, t, :, 64:128],
                                          v[:, t, :].rearrange("p (g d) -> p g d", g=2)).then_inc(s.vals, 1)
            pool.wait_ge(s.vals, 2 * NT)

        @block.tensor
        def _(pe):
            for u in range(6):
                if u >= 2:
                    pe.wait_ge(s.mixed, u - 1)
                nc.tensor.matmul(m.ps[:, u % 2, :], mask(p, "rot"), src[u], start=True, stop=True).then_inc(s.rotated, 1)
            for i in range(2):
                pe.wait_ge(s.added, 5 + i)
                for g in range(2):
                    nc.tensor.matmul(m.ps[:, 2 + 2 * i + g, :], mask(p, f"dup{g}"), dst[4 + i],
                                     start=True, stop=True).then_inc(s.dup, 1)

        @block.scalar
        def _(act):
            for i in range(2):
                for g in range(2):
                    act.wait_ge(s.dup, 2 * i + g + 1)
                    nc.scalar.activation(p.kr[:, i, g, :], m.ps[:, 2 + 2 * i + g, :], ACT.Copy).then_inc(s.moved, 1)

        @block.vector
        def _(dve):
            for u in range(6):
                dve.wait_ge(s.rotated, u + 1)
                nc.vector.tensor_tensor(tmp[:, u % 2, :], m.ps[:, u % 2, :], mask(p, "sin"), ALU.mult).then_inc(s.mixed, 1)
                nc.vector.tensor_tensor(dst[u], src[u], mask(p, "cos"), ALU.mult).then_inc(s.krot, 1)
                dve.wait_ge(s.mixed, u + 1)
                dve.wait_ge(s.krot, u + 1)
                nc.vector.tensor_tensor(dst[u], dst[u], tmp[:, u % 2, :], ALU.add).then_inc(s.added, 1)
                dve.wait_ge(s.added, u + 1)
    st.close()


def attention_stage(m, p, mT):
    nc = m.nc
    st = Stage(m, "attn")
    NB = 3
    pr = st.sb("probs", [P, NB, T])
    pT = st.sb("probsT", [P, 2, NT, P])
    c = st.sb("cols", [P, NB, 4])
    s = st.sem("score top ntop exp total scaled turned t_moved out o_moved masked")
    units = [(c2, t, h, b) for c2 in range(4) for t in range(NT) for h in range(2) for b in range(3)]

    def width(u):
        return NC if units[u][3] == 2 else (units[u][1] + 1) * P

    with st.block() as block:
        @block.tensor
        def _(pe):
            def scores(u):
                c2, t, h, b = units[u]
                g, rows, w = c2 // 2, slice(64 * h, 64 * h + 64), width(u)
                if u >= 3:
                    pe.wait_ge(s.exp, u - 2)
                ps = m.ps[:, u % 3, :]
                if b == 2:
                    nc.tensor.matmul(ps[:, 0:NC], p.nq[rows, c2, t * P:(t + 1) * P], p.kcmp[rows, g, :],
                                     start=True, stop=False)
                    last = nc.tensor.matmul(ps[:, 0:NC], m.ident, mask(p, "cneg")[:, t * NC:(t + 1) * NC],
                                            start=False, stop=True)
                else:
                    nc.tensor.matmul(ps[:, 0:w], p.qr[rows, c2, t * P:(t + 1) * P], p.kr[rows, b, g, 0:w],
                                     start=True, stop=False)
                    last = nc.tensor.matmul(ps[:, w - P:w], m.ident, mask(p, "causal"), start=False, stop=True)
                last.then_inc(s.score, 1)

            def turn(u):
                w = width(u)
                pe.wait_ge(s.scaled, u + 1)
                if u >= 2:
                    pe.wait_ge(s.t_moved, u - 1)
                for j in range(0, w, P):
                    n = min(P, w - j)
                    last = nc.tensor.transpose(m.ps[0:n, 3 + u % 2, j:j + P], pr[:, u % NB, j:j + n], m.ident)
                last.then_inc(s.turned, 1)

            def values(u):
                c2, t, h, b = units[u]
                g, o = c2 // 2, u // 6
                pe.wait_ge(s.t_moved, u + 1)
                first, final = u % 6 == 0, u % 6 == 5
                if first and o >= 2:
                    pe.wait_ge(s.o_moved, o - 1)
                ps = m.ps[:, 6 + o % 2, 0:P]
                lo = 64 if h == 0 else 0
                if b == 2:
                    last = nc.tensor.matmul(ps, p.vpad_c[:, g, lo:lo + P], pT[0:NC, u % 2, 0, :],
                                            start=first, stop=final)
                else:
                    for j in range(t + 1):
                        last = nc.tensor.matmul(ps, p.vpad[:, b, j, g, lo:lo + P], pT[:, u % 2, j, :],
                                                start=(first and j == 0), stop=final)
                last.then_inc(s.out, 1)

            n = len(units)
            for u in range(n + 2):
                if u < n:
                    scores(u)
                if 1 <= u <= n:
                    turn(u - 1)
                if u >= 2:
                    values(u - 2)

        @block.vector
        def _(dve):
            for u, (c2, t, h, b) in enumerate(units):
                w = width(u)
                k = c[:, u % NB, :]
                dve.wait_ge(s.score, u + 1)
                nc.vector.tensor_reduce(k[:, 0:1], m.ps[:, u % 3, 0:w], AX_X, ALU.max).then_inc(s.top, 1)
                dve.wait_ge(s.top, u + 1)
                if u >= NB:
                    dve.wait_ge(s.exp, u - NB + 1)
                nc.vector.tensor_scalar(k[:, 1:2], k[:, 0:1], -0.125, None, ALU.mult).then_inc(s.ntop, 1)
                dve.wait_ge(s.exp, u + 1)
                nc.vector.reciprocal(k[:, 3:4], k[:, 2:3]).then_inc(s.total, 1)
                gate = p.ng[:, t, 3 * (2 * c2 + h) + (1, 2, 0)[b]:3 * (2 * c2 + h) + (1, 2, 0)[b] + 1]
                dve.wait_ge(s.total, u + 1)
                if b == 2:
                    nc.vector.tensor_tensor(pr[:, u % NB, 0:w], pr[:, u % NB, 0:w],
                                            mask(p, "cok")[:, t * NC:(t + 1) * NC], ALU.mult).then_inc(s.masked, 1)
                    dve.wait_ge(s.masked, u // 3 + 1)
                nc.vector.tensor_scalar(pr[:, u % NB, 0:w], pr[:, u % NB, 0:w], k[:, 3:4], gate,
                                        ALU.mult, ALU.mult).then_inc(s.scaled, 1)

        @block.scalar
        def _(act):
            def move(u):
                c2, t, h, b = units[u]
                w = width(u)
                n = min(P, w)
                act.wait_ge(s.turned, u + 1)
                if u >= 2:
                    act.wait_ge(s.out, u - 1)
                src = m.ps[0:n, 3 + u % 2, 0:max(w, P)].rearrange("p (j c) -> p j c", c=P)
                nc.scalar.activation(pT[0:n, u % 2, 0:max(w, P) // P, :], src, ACT.Copy).then_inc(s.t_moved, 1)

            def out(o):
                c2, t = units[6 * o][0:2]
                act.wait_ge(s.out, 6 * o + 6)
                nc.scalar.activation(mT[:, 4 + c2, t * P:(t + 1) * P], m.ps[:, 6 + o % 2, 0:P],
                                     ACT.Copy).then_inc(s.o_moved, 1)

            n = len(units)
            for u in range(n + 2):
                if u < n:
                    w = width(u)
                    act.wait_ge(s.ntop, u + 1)
                    if u >= NB:
                        act.wait_ge(s.turned, u - NB + 1)
                        act.wait_ge(s.total, u - NB + 1)
                    nc.scalar.activation(pr[:, u % NB, 0:w], m.ps[:, u % 3, 0:w], ACT.Exp, bias=c[:, u % NB, 1:2],
                                         scale=0.125, accum_out=c[:, u % NB, 2:3]).then_inc(s.exp, 1)
                if 1 <= u <= n:
                    move(u - 1)
                if u >= 2 and (u - 2) % 6 == 5:
                    out((u - 2) // 6)
    st.close()


def setup_stage(m, a):
    nc = m.nc
    st = Stage(m, "setup")
    s = st.sem("in_ eps")
    with st.block() as block:
        @block.sync
        def _(sp):
            sp.dma_start(m.base[:], a["c_base"]).then_inc(s.in_, 16)
            sp.dma_start(m.before, a["c_before"]).then_inc(s.in_, 16)
            sp.dma_start(m.x[:], a["x"][0].rearrange("(t p) d -> p t d", p=P)).then_inc(s.in_, 16)
            m.ring.stream(sp, SLOTS)
            sp.wait_ge(s.in_, 48)

        @block.gpsimd
        def _(pool):
            nc.gpsimd.memset(m.eps[:], EPS).then_inc(s.eps, 1)
            pool.wait_ge(s.eps, 1)
    st.close()


def simple_load(m, tag, pairs, zero=()):
    nc = m.nc
    st = Stage(m, f"load{tag}")
    s = st.sem("in_ zero")
    with st.block() as block:
        @block.sync
        def _(sp):
            for dst, src in pairs:
                sp.dma_start(dst, src, allow_slow_non_contiguous=True).then_inc(s.in_, 16)
            sp.wait_ge(s.in_, 16 * len(pairs))

        @block.gpsimd
        def _(pool):
            for z in zero:
                nc.gpsimd.memset(z, 0.0).then_inc(s.zero, 1)
            if zero:
                pool.wait_ge(s.zero, len(zero))
    st.close()


def plan_weights(m, a):
    ring, at = m.ring, {}

    def columns(name, w, c0, n=512, k=KD):
        return ring.add([(whole(k, n), rows_of(w, c0, n))])

    def ada(name, w):
        at[name] = [columns(name, w, 512 * i) for i in range(12)][0]

    def experts(name, w1, w3, w2):
        at[name] = len(ring.tiles)
        for e in range(E1):
            columns(name, w1[e], 0)
            columns(name, w3[e], 0)
            columns(name, w2[e], 0, D, 4)

    ada("mod0", a["ada_w"][0])
    w = a["w_in_a"][0]
    for hg in range(2):
        at[f"heads{hg}"] = len(ring.tiles)
        for kind in range(3):
            columns("", w, kind * D + hg * 512)
    at["z"] = len(ring.tiles)
    for h in range(2):
        columns("", w, 3 * D + h * 512)
    at["out0"] = len(ring.tiles)
    for h in range(2):
        columns("", a["w_out_a"][0], h * 512)
    experts("moe0", a["w1"][0], a["w3"][0], a["w2"][0])
    ada("mod1", a["ada_w"][1])
    at["conv"] = len(ring.tiles)
    for half in range(2):
        for j in range(3):
            columns("", a["w_in_b"][0], j * D + half * 512)
    at["out1"] = len(ring.tiles)
    for h in range(2):
        columns("", a["w_out_b"][0], h * 512)
    experts("moe1", a["w1"][1], a["w3"][1], a["w2"][1])
    ada("mod2", a["w_ada_2"][0])
    w = a["w_in_2"][0]
    at["mix"] = len(ring.tiles)
    for c in range(5):
        columns("", w, 512 * c)
    at["kv"] = len(ring.tiles)
    columns("", w, 2560)
    columns("", w, 3072, W_IN2 - 3072)
    at["cmp"] = len(ring.tiles)
    for x in "kv":
        w1 = a[f"cmp_w1_{x}_2"][0].rearrange("(l d) n -> d l n", d=64)
        for half in range(2):
            src = w1[:, 16 * half:16 * half + 16, :]
            ring.add([(lambda s, g=g: s[64 * g:64 * g + 64, :].rearrange("p (l n) -> p l n", l=16), src)
                      for g in range(2)])
    at["out2"] = len(ring.tiles)
    for h in range(2):
        columns("", a["w_out_2"][0], h * 512)
    at["moe2"] = len(ring.tiles)
    columns("", a["w_sh_gu_2"][0], 0)
    columns("", a["w_sh_dn_2"][0], 0, D, 2)
    for e in range(E2 // 2):
        columns("", a["w_exp_gu_2"][0, 2 * e], 0)
        columns("", a["w_exp_gu_2"][0, 2 * e + 1], 0)
        ring.add([(whole(4, D), a["w_exp_dn_2"][0, 2 * e:2 * e + 2].rearrange("o (k p) n -> p (o k) n", p=P))])
    return at


def build(nc, a, out):
    ctx = ExitStack()
    m = Bag()
    m.nc = nc
    with ctx:
        m.ring = WeightRing(nc, ctx)
        m.x = ctx.enter_context(nc.sbuf_tensor("x_resident", [P, NT, D], F32))
        m.mod = ctx.enter_context(nc.sbuf_tensor("modulation", [P, 6 * D], F32))
        m.base = ctx.enter_context(nc.sbuf_tensor("base", [P, 2, P], F32))
        m.beforeb = ctx.enter_context(nc.sbuf_tensor("before", [P, 64], F32))
        m.eps = ctx.enter_context(nc.sbuf_tensor("eps", [P, 1], F32))
        m.ps = ctx.enter_context(nc.psum_tensor("ps", [P, 8, 512], F32))
        m.ident, m.ones, m.before = m.base[:, 0, :], m.base[:, 1, :], m.beforeb[:, :]
        at = plan_weights(m, a)
        m.where = mix_masks()[1]
        xt = [m.x[:, t, :] for t in range(NT)]
        mod = [m.mod[:, i * D:(i + 1) * D] for i in range(6)]
        hid = nc.dram_tensor("hidden", [T, D], F32).ap()
        setup_stage(m, a)
        dctx = ExitStack()
        def dsb(name, shape):
            return dctx.enter_context(nc.sbuf_tensor(f"delta_{name}", shape, F32))
        hx = dsb("hx", [P, KD, CT + T])
        p = Bag()
        p.masks, p.conv, p.o = dsb("masks", [P, 20, P]), dsb("conv", [P, 3, 24]), dsb("o", [P, NT, D])
        nt = NCT + NT
        p.cum, p.ncum, p.g, p.egc, p.ekd, p.egl, p.beta, p.bege = [
            dsb(g, [P, nt, 16]) for g in ("cum", "ncum", "g", "egc", "ekd", "egl", "beta", "bege")]
        p.onorm = a["onorm_a"][0]
        with nc.sbuf_tensor("ctx_tiles", [P, NCT, D], F32) as xc, nc.sbuf_tensor("ctx_mod", [P, 2 * D], F32) as mc:
            modulation_stage(m, 0, [(a["c"][0], m.mod, 12), (a["c_ctx"], mc, 4)], at["mod0"],
                             a["ada_b"][0], at["mod0"] + 12 + SLOTS)
            simple_load(m, "ctx", [(xc[:], a["ctx"][0].rearrange("(t p) d -> p t d", p=P)),
                                   (p.masks[:], a["c_delta"])] +
                        [(p.conv[:, j, :], a["conv_a"][0, j, :].rearrange("(k p) -> p k", p=P)) for j in range(3)],
                        [p.o[:]])
            prepare_stage(m, 0, [(xt, mod[0], mod[1], hx, CT, None),
                                 ([xc[:, t, :] for t in range(NCT)], mc[:, 0:D], mc[:, D:2 * D], hx, 0, None)],
                          a["norm_mix"][0], 0)
        delta_gates(m, hx, p, a["w_in_a"][0][:, 4 * D:4 * D + 32],
                    a["a_log_a"][0].rearrange("a b -> (a b)"), a["dt_bias_a"][0].rearrange("a b -> (a b)"))
        for hg in range(2):
            with nc.sbuf_tensor(f"qT{hg}", [P, 4, T], F32) as p.qT, nc.sbuf_tensor(f"kT{hg}", [P, 4, SPAN], F32) as p.kT,                     nc.sbuf_tensor(f"k{hg}", [P, nt, 512], F32) as p.k, nc.sbuf_tensor(f"v{hg}", [P, nt, 512], F32) as p.v:
                delta_heads(m, hg, hx, p, at[f"heads{hg}"], at[f"heads{hg}"] + 6)
                delta_scan(m, hg, p)
        with nc.sbuf_tensor("oT0", [P, KD, T], F32) as oT:
            p.oT = oT
            delta_finish(m, hx, p, at["z"], at["z"] + 5)
            simple_load(m, "x", [(m.x[:], a["x"][0].rearrange("(t p) d -> p t d", p=P))])
            project_stage(m, 0, oT, at["out0"], mod[2], at["out0"] + 5)
        dctx.close()

        def moe(layer, first):
            with nc.sbuf_tensor(f"moe_hT{layer}", [P, KD, T], F32) as hT,                     nc.sbuf_tensor(f"moe_y{layer}", [P, NT, D], F32) as y,                     nc.sbuf_tensor(f"moe_w{layer}", [P, NT, E2], F32) as wt:
                gain = a["norm_ffn"][layer] if layer < 2 else a["norm2_g_2"][0]
                prepare_stage(m, f"f{layer}", [(xt, mod[3], mod[4], hT, 0, None)], gain, 0)
                simple_load(m, f"y{layer}", [], [y[:]])
                if layer < 2:
                    w = wt[:, :, 0:E1]
                    route_groups_stage(m, layer, hT, a["router_g"][layer], a["router_e"][layer], w, 0)
                    experts_stage(m, layer, hT, w, y, first, (a["w1"][layer], a["w3"][layer], a["w2"][layer]),
                                  E1, first + 3 * E1 + SLOTS)
                    residual_stage(m, layer, y, mod[5], 0, *([a["final_norm"]] if layer == 1 else []))
                else:
                    w = wt[:, :, :]
                    route_sigmoid_stage(m, layer, hT, a["router_w_2"][0], a["router_bias_2"][0], w, 0)
                    pair_experts_stage(m, layer, hT, w, y, first, None, a["w_exp_gu_2"][0], a["w_exp_dn_2"][0],
                                       E2, 10 ** 6)
                    residual_stage(m, layer, y, mod[5], 0, a["final_g_2"], out[0])

        moe(0, at["moe0"])
        modulation_stage(m, 1, [(a["c"][0], m.mod, 12)], at["mod1"], a["ada_b"][1], at["mod1"] + 12 + SLOTS)
        with nc.sbuf_tensor("hT1", [P, KD, T], F32) as hT, nc.sbuf_tensor("yT1", [P, KD, T], F32) as yT:
            prepare_stage(m, 1, [(xt, mod[0], mod[1], hT, 0, None)], a["norm_mix"][1], 0)
            shortconv_stage(m, hT, yT, at["conv"], a["conv_b"][0], at["conv"] + 9)
            project_stage(m, 1, yT, at["out1"], mod[2], at["out1"] + 5)
        moe(1, at["moe1"])
        modulation_stage(m, 2, [(a["c_2"][0], m.mod, 12)], at["mod2"], a["b_ada_2"][0], at["mod2"] + 12 + SLOTS)
        xctx = ExitStack()
        mT = xctx.enter_context(nc.sbuf_tensor("mT", [P, KD, T], F32))
        q = Bag()
        q.where, q.lb_logits, q.hg_norm = m.where, a["hg_lb_logits_2"], a["hg_norm_g_2"][0]
        q.pos, q.b1, q.w2 = [[a[f"cmp_{w}_{x}_2"][0] for x in "kv"] for w in ("pos", "b1", "w2")]

        def xsb(c, name, shape):
            return c.enter_context(nc.sbuf_tensor(f"mix_{name}", shape, F32))
        q.masks = xsb(xctx, "masks", [P, a["c_mix"].shape[1]])
        q.nq = xsb(xctx, "nq", [P, 4, T])
        q.kc, q.vc, q.ks, q.kw = [xsb(xctx, n, [P, T]) for n in ("kc", "vc", "ks", "kw")]
        q.vs, q.vw, q.ng = xsb(xctx, "vs", [P, NT, P]), xsb(xctx, "vw", [P, NT, P]), xsb(xctx, "ng", [P, NT, 24])
        hctx = ExitStack()
        q.q, q.f, q.k, q.gate = [xsb(hctx, n, [P, 4, T]) for n in ("hq", "hf", "hk", "hgate")]
        q.v = xsb(hctx, "v", [P, NT, HW])
        with nc.sbuf_tensor("hT2", [P, KD, T], F32) as hT:
            prepare_stage(m, 2, [(xt, mod[0], mod[1], hT, 0, None)], a["norm1_g_2"][0], 0)
            spill = nc.dram_tensor("x_spill", [P, NT, D], F32).ap()
            simple_load(m, "mix", [(q.masks[:], a["c_mix"]), (spill, m.x[:])])
            mix_columns(m, q, hT, at["mix"], at["kv"], at["kv"] + 2 + SLOTS)
        q.band, q.last = xsb(hctx, "band", [P, 16, SUB]), xsb(hctx, "last", [P, 128])
        q.qd = m.x[:, 0:2, :].rearrange("p a b -> p (a b)").rearrange("p (h t) -> p h t", h=4)
        q.kd = m.x[:, 2:4, :].rearrange("p a b -> p (a b)").rearrange("p (h t) -> p h t", h=4)
        hgrn_prepare(m, q)
        hgrn_scan(m, q, mT)
        hctx.close()
        simple_load(m, "x2", [(m.x[:], spill)])
        q.kcmp, q.vpad_c = xsb(xctx, "kcmp", [P, 2, NC]), xsb(xctx, "vpadc", [NC, 2, 192])
        simple_load(m, "vpadc", [], [q.vpad_c[:]])
        compress_stage(m, q, at["cmp"], at["cmp"] + 7)
        q.qr, q.kr = xsb(xctx, "qr", [P, 4, T]), xsb(xctx, "kr", [P, 2, 2, T])
        q.vpad = xsb(xctx, "vpad", [P, 2, NT, 2, 192])
        rope_stage(m, q)
        attention_stage(m, q, mT)
        project_stage(m, 2, mT, at["out2"], mod[2], at["out2"] + 5)
        xctx.close()
        moe(2, at["moe2"])


INPUTS = ["x", "c", "ctx", "c_ctx", "ada_w", "ada_b", "norm_mix", "norm_ffn", "w_in_a", "conv_a", "a_log_a",
          "dt_bias_a", "onorm_a", "w_out_a", "w_in_b", "conv_b", "w_out_b", "router_g", "router_e", "w1", "w3", "w2",
          "final_norm", "c_2", "w_ada_2", "b_ada_2", "norm1_g_2", "w_in_2", "hg_lb_logits_2", "hg_norm_g_2",
          "cmp_pos_k_2", "cmp_w1_k_2", "cmp_b1_k_2", "cmp_w2_k_2", "cmp_pos_v_2", "cmp_w1_v_2", "cmp_b1_v_2",
          "cmp_w2_v_2", "w_out_2", "norm2_g_2", "router_w_2", "router_bias_2", "w_exp_gu_2", "w_exp_dn_2",
          "w_sh_gu_2", "w_sh_dn_2", "final_g_2"]


def host_constants():
    before = (np.arange(8)[None, :] < np.arange(8)[:, None]).astype(np.float32).reshape(1, 64)
    return {"c_base": base_masks(), "c_before": np.tile(before, (P, 1)), "c_delta": delta_masks(),
            "c_mix": mix_masks()[0]}


def kernel(**inputs):
    import concourse.bacc as bacc
    from concourse.bass_utils import run_bass_kernel_spmd as run

    nc = bacc.Bacc("TRN2", target_bir_lowering=False, num_devices=1)
    arrays, args = {}, {}
    for name, v in [(n, inputs[n]) for n in INPUTS] + list(host_constants().items()):
        v = np.ascontiguousarray(v)
        arrays[f"in_{name}_dram"] = v
        args[name] = nc.dram_tensor(f"in_{name}_dram", v.shape, mybir.dt.from_np(v.dtype), kind="ExternalInput").ap()
    out = nc.dram_tensor("out_0_dram", (1, T, D), F32, kind="ExternalOutput").ap()
    build(nc, args, out)
    r = run(nc, [arrays], core_ids=[0])
    return r.results[0]["out_0_dram"]
```

```python
from contextlib import ExitStack
from collections import namedtuple

import numpy as np
import concourse.bass as bass
from concourse import mybir

ALU = mybir.AluOpType
ACT = mybir.ActivationFunctionType
F32 = mybir.dt.float32
U32 = mybir.dt.uint32
AX_X = mybir.AxisListType.X

P = 128
D = 1024
KD = D // P
T = 512
NT = T // P
CT = 256
NCT = CT // P
EPS = 1e-6
EMPTY = 4096
TOP1, TOP2 = 2, 8
UNITS1 = 32 + 1024 // P - 1
UNITS2 = 64 + 4096 // P - 1
NEG = -1e30
SLOTS = 3
SLOT = KD * 512
HEADS = 8
E1, F1 = 32, 512
E2, F2 = 64, 256
W_IN2 = 3352


def base_masks():
    i = np.arange(P)
    return np.stack([np.eye(P), np.ones((P, P)), i[:, None] < i[None, :]], 1).astype(np.float32)


def delta_masks():
    r, c = np.arange(P)[:, None], np.arange(P)[None, :]
    out = [r <= c, r >= c]
    neg = [np.where(ok, 0.0, NEG) for ok in (c < r, c > r, c >= r, c <= r)]
    levels = []
    for n in (1, 2, 4, 8, 16, 32, 64):
        levels.append((r // (2 * n) == c // (2 * n)) & (r % (2 * n) >= n) & (c % (2 * n) < n))
    levels += [m.T for m in levels]
    return np.stack([np.asarray(m, np.float32) for m in out + neg + levels], 1)


def mix_masks():
    p = np.arange(P)
    r, c = p[:, None], p[None, :]
    half = 32
    inv = 10000.0 ** (-np.arange(half, dtype=np.float32) / half)
    ang = np.arange(T, dtype=np.float32)[None, :] * inv.astype(np.float32)[p % half][:, None]
    cos, sin = np.cos(ang), np.sin(ang)
    rot = np.where(c % 64 < half, -(r == c + half).astype(np.float32), (r == c - half).astype(np.float32))
    dup = [(r == g * 64 + c % 64) for g in range(2)]
    block = np.arange(31)
    pos = np.arange(T).reshape(NT, P).T
    ok = (block[None, None, :] * 16 + 31) <= pos[:, :, None]
    local = np.arange(16)
    shift = (p[:, None, None] % 16 - local[None, None, :]) == local[None, :, None]
    chunk = (p[:, None] // 16) == np.arange(8)[None, :]
    spread = np.repeat(chunk, 16, axis=1)
    notstart = np.tile(np.arange(16) != 0, (P, 1))
    start = np.tile(np.arange(16) == 0, (P, 1))
    notend = np.tile(np.arange(16) != 15, (P, 1))
    parts = [("cos", cos), ("sin", sin), ("rot", rot), ("dup0", dup[0]), ("dup1", dup[1]),
             ("causal", np.where(c <= r, 0.0, NEG)),
             ("cneg", np.where(ok, 0.0, NEG).reshape(P, -1)), ("cok", ok.reshape(P, -1)),
             ("shift", shift.reshape(P, -1)), ("chunk", chunk), ("spread", spread),
             ("notstart", notstart), ("start", start), ("notend", notend)]
    where, at = {}, 0
    for name, a in parts:
        where[name] = (at, a.shape[1])
        at += a.shape[1]
    return np.concatenate([np.asarray(a, np.float32) for _, a in parts], 1), where


def column(ap, n, width):
    return ap.unsqueeze(2).to_broadcast([ap.shape[0], n, width])


def across(ap, n):
    return ap.unsqueeze(1).to_broadcast([ap.shape[0], n, ap.shape[1]])


def flat(ap):
    return ap.rearrange("p a b -> p (a b)")


class Bag:
    pass


class Linked:

    def __init__(self, eng, sem):
        self.eng, self.sem, self.n = eng, sem, 0

    def __call__(self, ins):
        ins.then_inc(self.sem, 1)
        self.n += 1
        self.eng.wait_ge(self.sem, self.n)


class WeightRing:

    def __init__(self, nc, ctx):
        self.buf = ctx.enter_context(nc.sbuf_tensor("weight_ring", [P, SLOTS, SLOT], F32))
        self.loaded = [ctx.enter_context(nc.semaphore(f"weights_loaded{i}")) for i in range(SLOTS)]
        self.freed = [ctx.enter_context(nc.semaphore(f"weights_used{i}")) for i in range(SLOTS)]
        self.tiles = []
        self.sent = 0

    def add(self, dmas):
        self.tiles.append(dmas)
        return len(self.tiles) - 1

    def slot(self, n):
        return self.buf[:, n % SLOTS, :]

    def loads(self, n):
        return 16 * sum(len(self.tiles[i]) for i in range(n % SLOTS, n + 1, SLOTS))

    def uses(self, n):
        return n // SLOTS

    def stream(self, sp, upto):
        while self.sent < min(upto, len(self.tiles)):
            n = self.sent
            if n >= SLOTS:
                sp.wait_ge(self.freed[n % SLOTS], self.uses(n))
            for dst, src in self.tiles[n]:
                sp.dma_start(dst(self.slot(n)), src).then_inc(self.loaded[n % SLOTS], 16)
            self.sent += 1

    def wait(self, pe, n):
        pe.wait_ge(self.loaded[n % SLOTS], self.loads(n))


class Stage:

    def __init__(self, m, name):
        self.m, self.nc, self.name = m, m.nc, name
        self.ctx = ExitStack()
        self.sems = []

    def sb(self, name, shape, dt=F32):
        return self.ctx.enter_context(self.nc.sbuf_tensor(f"{self.name}_{name}", shape, dt))

    def sem(self, names, mark=""):
        new = [self.nc.alloc_semaphore(f"{self.name}{mark}_{n}") for n in names.split()]
        self.sems += new
        return namedtuple("Semaphores", names)(*new)

    def block(self):
        return self.nc.Block()

    def clear(self):
        self.nc.clear_and_free_semaphores(self.sems)
        self.nc.all_engine_barrier()
        self.sems = []

    def close(self):
        self.clear()
        self.ctx.close()


def whole(k, n):
    return lambda s: s[:, 0:k * n].rearrange("p (k n) -> p k n", k=k)


def rows_of(w, c0, n):
    return w[:, c0:c0 + n].rearrange("(k p) n -> p k n", p=P)


def blank_rows(m, sp, zeros):
    rows = m.expert_rows[E1 * P:UNITS2 * P, :].rearrange("(u p) d -> p u d", p=P)
    sp.dma_start(rows, across(zeros, UNITS2 - E1)).then_inc(m.rows_blank, 16)


def modulation_stage(m, tag, conds, first, bias, after):
    nc, ring = m.nc, m.ring
    st = Stage(m, f"mod{tag}")
    nv = len(conds)
    craw = st.sb("craw", [P, nv, KD])
    csil = st.sb("csil", [P, nv, KD])
    wide = st.sb("wide", [P, nv, KD, P])
    s = st.sem("vector_in bias_in silu wide product added")
    units = [(n, v) for n in range(6 * D // 512) for v in range(nv) if n < conds[v][2]]
    with st.block() as block:
        @block.sync
        def _(sp):
            for v, (c, _, _) in enumerate(conds):
                sp.dma_start(craw[:, v, :], c.rearrange("(k p) -> p k", p=P),
                             allow_slow_non_contiguous=True).then_inc(s.vector_in, 16)
            ring.stream(sp, first + 1)
            for v, (_, dst, blocks) in enumerate(conds):
                sp.dma_start(dst[:, 0:blocks * 512],
                             bias[0:blocks * 512].partition_broadcast(P)).then_inc(s.bias_in, 16)
            ring.stream(sp, after)

        @block.scalar
        def _(act):
            act.wait_ge(s.vector_in, 16 * nv)
            nc.scalar.activation(csil[:], craw[:], ACT.Silu).then_inc(s.silu, 1)

        @block.vector
        def _(dve):
            dve.wait_ge(s.silu, 1)
            nc.vector.tensor_copy(wide[:].rearrange("p v k c -> p (v k) c"),
                                  column(flat(csil[:]), nv * KD, P)).then_inc(s.wide, 1)
            dve.wait_ge(s.bias_in, 16 * nv)
            for u, (n, v) in enumerate(units):
                dst = conds[v][1][:, n * 512:(n + 1) * 512]
                dve.wait_ge(s.product, u + 1)
                nc.vector.tensor_tensor(dst, m.ps[:, u % 4, :], dst, ALU.add).then_inc(s.added, 1)

        @block.tensor
        def _(pe):
            pe.wait_ge(s.wide, 1)
            for u, (n, v) in enumerate(units):
                ring.wait(pe, first + n)
                w = whole(KD, 512)(ring.slot(first + n))
                if u >= 4:
                    pe.wait_ge(s.added, u - 3)
                for k in range(KD):
                    last = nc.tensor.matmul(m.ps[:, u % 4, :], wide[:, v, k, :], w[:, k, :],
                                            start=(k == 0), stop=(k == KD - 1))
                last.then_inc(s.product, 1)
                if u + 1 == len(units) or units[u + 1][0] != n:
                    pe.wait_ge(s.product, u + 1)
                    pe.sem_inc(ring.freed[(first + n) % SLOTS], 1)
    st.close()


def prepare_stage(m, tag, groups, gain, after):
    nc = m.nc
    st = Stage(m, f"prep{tag}")
    tiles = [(x, g, i) for g, grp in enumerate(groups) for i, x in enumerate(grp[0])]
    n = len(tiles)
    gbc = st.sb("gain", [P, D])
    xn = st.sb("xn", [P, 2, D])
    junk = st.sb("junk", [P, D])
    ss = st.sb("ss", [P, 3, n])
    s = st.sem("gain_in v root chain ready turned evac kept0 kept1")
    kept = [s.kept0, s.kept1]
    with st.block() as block:
        @block.sync
        def _(sp):
            sp.dma_start(gbc[:], gain.partition_broadcast(P)).then_inc(s.gain_in, 16)
            for u, (_, g, i) in enumerate(tiles):
                keep = groups[g][5]
                if keep is not None:
                    sp.wait_ge(s.ready, u + 1)
                    sp.dma_start(keep[i * P:(i + 1) * P, :], xn[:, u % 2, :]).then_inc(kept[u % 2], 16)
            m.ring.stream(sp, after)
            if any(grp[5] is not None for grp in groups):
                for b in range(2):
                    sp.wait_ge(kept[b], 16 * (n // 2))

        @block.vector
        def _(dve):
            link = Linked(dve, s.chain)
            for u, (x, _, _) in enumerate(tiles):
                link(nc.vector.tensor_tensor_reduce(out=junk[:], in0=x, in1=x, scale=1.0, scalar=0.0,
                                                    op0=ALU.mult, op1=ALU.add, accum_out=ss[:, 0, u:u + 1]))
            link(nc.vector.tensor_scalar(ss[:, 1, :], ss[:, 0, :], 1.0 / D, EPS, ALU.mult, ALU.add))
            nc.vector.tensor_copy(ss[:, 1, :], ss[:, 1, :]).then_inc(s.v, 1)
            dve.wait_ge(s.gain_in, 16)
            for g, (_, _, scale, _, _, _) in enumerate(groups):
                link(nc.vector.scalar_tensor_tensor(out=scale, in0=scale, scalar=1.0, in1=gbc[:],
                                                    op0=ALU.add, op1=ALU.mult))
            dve.wait_ge(s.root, 1)
            r, v, a = ss[:, 2, :], ss[:, 1, :], ss[:, 0, :]
            link(nc.vector.reciprocal(r, r))
            link(nc.vector.tensor_tensor(a, r, r, ALU.mult))
            link(nc.vector.tensor_tensor(a, a, v, ALU.mult))
            link(nc.vector.tensor_scalar(a, a, -0.5, 1.5, ALU.mult, ALU.add))
            link(nc.vector.tensor_tensor(r, r, a, ALU.mult))
            for u, (x, g, i) in enumerate(tiles):
                _, shift, scale, _, _, keep = groups[g]
                if u >= 2:
                    dve.wait_ge(s.turned, u - 1)
                    if keep is not None:
                        dve.wait_ge(kept[u % 2], 16 * (u // 2))
                link(nc.vector.scalar_tensor_tensor(out=xn[:, u % 2, :], in0=x, scalar=r[:, u:u + 1],
                                                    in1=scale, op0=ALU.mult, op1=ALU.mult))
                nc.vector.tensor_tensor(xn[:, u % 2, :], xn[:, u % 2, :], shift, ALU.add).then_inc(s.ready, 1)

        @block.scalar
        def _(act):
            act.wait_ge(s.v, 1)
            nc.scalar.activation(ss[:, 2, :], ss[:, 1, :], ACT.Sqrt).then_inc(s.root, 1)
            for u, (_, g, i) in enumerate(tiles):
                _, _, _, dst, c0, _ = groups[g]
                act.wait_ge(s.turned, u + 1)
                for h in range(2):
                    last = nc.scalar.activation(
                        dst[:, 4 * h:4 * h + 4, c0 + i * P:c0 + (i + 1) * P],
                        m.ps[:, (u % 2) * 2 + h, :].rearrange("p (k t) -> p k t", k=4), ACT.Copy)
                last.then_inc(s.evac, 1)

        @block.tensor
        def _(pe):
            for u in range(n):
                pe.wait_ge(s.ready, u + 1)
                if u >= 2:
                    pe.wait_ge(s.evac, u - 1)
                for k in range(KD):
                    last = nc.tensor.transpose(m.ps[:, (u % 2) * 2 + k // 4, (k % 4) * P:(k % 4 + 1) * P],
                                               xn[:, u % 2, k * P:(k + 1) * P], m.ident)
                last.then_inc(s.turned, 1)
    st.close()


def project_stage(m, tag, aT, first, gate, after):
    nc, ring = m.nc, m.ring
    st = Stage(m, f"out{tag}")
    tmp = st.sb("tmp", [P, 2, 512])
    s = st.sem("product gated added")
    units = [(h, t) for h in range(2) for t in range(NT)]
    with st.block() as block:
        @block.sync
        def _(sp):
            ring.stream(sp, after)

        @block.tensor
        def _(pe):
            for u, (h, t) in enumerate(units):
                ring.wait(pe, first + h)
                w = whole(KD, 512)(ring.slot(first + h))
                if u >= 4:
                    pe.wait_ge(s.gated, u - 3)
                for k in range(KD):
                    last = nc.tensor.matmul(m.ps[:, u % 4, :], aT[:, k, t * P:(t + 1) * P], w[:, k, :],
                                            start=(k == 0), stop=(k == KD - 1))
                last.then_inc(s.product, 1)
                if t == NT - 1:
                    pe.wait_ge(s.product, u + 1)
                    pe.sem_inc(ring.freed[(first + h) % SLOTS], 1)

        @block.vector
        def _(dve):
            for u, (h, t) in enumerate(units):
                cols = slice(h * 512, (h + 1) * 512)
                dve.wait_ge(s.product, u + 1)
                nc.vector.tensor_tensor(tmp[:, u % 2, :], m.ps[:, u % 4, :], gate[:, cols],
                                        ALU.mult).then_inc(s.gated, 1)
                dve.wait_ge(s.gated, u + 1)
                nc.vector.tensor_tensor(m.x[:, t, cols], m.x[:, t, cols], tmp[:, u % 2, :],
                                        ALU.add).then_inc(s.added, 1)
                dve.wait_ge(s.added, u + 1)
    st.close()


LAT = CT + 2
SPAN = LAT + T
DK = 128


def delta_gates(m, hx, p, w_small, a_log, dt_bias):
    nc = m.nc
    st = Stage(m, "gates")
    n = NCT + NT
    ws = st.sb("w", [P, KD, 32])
    al = st.sb("alog", [P, 16])
    dt = st.sb("dt", [P, 16])
    raw = st.sb("raw", [P, n, 32])
    b = st.sb("b", [P, 6, n, 16])
    s = st.sem("small_in sum_in logits raw_there beta expA expB decay chain sums exps")
    with st.block() as block:
        @block.sync
        def _(sp):
            sp.dma_start(ws[:], w_small.rearrange("(k p) n -> p k n", p=P)).then_inc(s.small_in, 16)
            sp.dma_start(al[:], a_log.partition_broadcast(P)).then_inc(s.sum_in, 16)
            sp.dma_start(dt[:], dt_bias.partition_broadcast(P)).then_inc(s.sum_in, 16)

        @block.tensor
        def _(pe):
            pe.wait_ge(s.small_in, 16)
            for t in range(n):
                for k in range(KD):
                    last = nc.tensor.matmul(m.ps[:, 0, t * 32:(t + 1) * 32], hx[:, k, t * P:(t + 1) * P],
                                            ws[:, k, :], start=(k == 0), stop=(k == KD - 1))
            last.then_inc(s.logits, 1)
            pe.wait_ge(s.decay, 1)
            for d in range(2):
                g = b[:, 5, :, 8 * d:8 * d + 8]
                nc.tensor.matmul(m.ps[:, 1 + d, 0:8 * n].rearrange("p (t h) -> p t h", h=8),
                                 p.masks[:, d, :], g, start=True, stop=True)
                last = nc.tensor.matmul(m.ps[:, 3 + d, 0:8 * n].rearrange("p (t h) -> p t h", h=8),
                                        m.ones, g, start=True, stop=True)
            last.then_inc(s.sums, 1)

        @block.scalar
        def _(act):
            act.wait_ge(s.raw_there, 1)
            nc.scalar.activation(p.beta[:], raw[:, :, 0:16], ACT.Sigmoid).then_inc(s.beta, 1)
            act.wait_ge(s.sum_in, 32)
            nc.scalar.activation(al[:], al[:], ACT.Exp).then_inc(s.expA, 1)
            act.wait_ge(s.chain, 3)
            nc.scalar.activation(b[:, 2, :, :], b[:, 1, :, :], ACT.Exp).then_inc(s.expB, 1)
            act.wait_ge(s.chain, 4)
            nc.scalar.activation(b[:, 3, :, :], b[:, 2, :, :], ACT.Ln).then_inc(s.expB, 1)
            act.wait_ge(s.chain, 8)
            nc.scalar.activation(p.egc[:], p.cum[:], ACT.Exp).then_inc(s.exps, 1)
            nc.scalar.activation(p.ekd[:], b[:, 0, :, :], ACT.Exp).then_inc(s.exps, 1)
            nc.scalar.activation(p.egl[:], p.egl[:], ACT.Exp).then_inc(s.exps, 1)

        @block.vector
        def _(dve):
            link = Linked(dve, s.chain)
            dve.wait_ge(s.logits, 1)
            nc.vector.tensor_copy(raw[:], m.ps[:, 0, 0:n * 32].rearrange("p (t c) -> p t c", c=32)
                                  ).then_inc(s.raw_there, 1)
            dve.wait_ge(s.raw_there, 1)
            dve.wait_ge(s.sum_in, 32)
            link(nc.vector.tensor_tensor(b[:, 0, :, :], raw[:, :, 16:32], across(dt[:], n), ALU.add))
            link(nc.vector.tensor_scalar(b[:, 4, :, :], b[:, 0, :, :], -1.0, None, ALU.mult))
            link(nc.vector.tensor_tensor(b[:, 1, :, :], b[:, 0, :, :], b[:, 4, :, :], ALU.min))
            dve.wait_ge(s.expB, 1)
            link(nc.vector.tensor_scalar(b[:, 2, :, :], b[:, 2, :, :], 1.0, None, ALU.add))
            dve.wait_ge(s.expB, 2)
            link(nc.vector.scalar_tensor_tensor(out=b[:, 4, :, :], in0=b[:, 0, :, :], scalar=0.0,
                                                in1=b[:, 3, :, :], op0=ALU.max, op1=ALU.add))
            dve.wait_ge(s.expA, 1)
            nc.vector.scalar_tensor_tensor(out=b[:, 5, :, :], in0=b[:, 4, :, :], scalar=-1.0,
                                           in1=across(al[:], n), op0=ALU.mult, op1=ALU.mult
                                           ).then_inc(s.decay, 1)
            dve.wait_ge(s.sums, 1)
            for d in range(2):
                hs = slice(8 * d, 8 * d + 8)
                nc.vector.tensor_copy(p.cum[:, :, hs],
                                      m.ps[:, 1 + d, 0:8 * n].rearrange("p (t h) -> p t h", h=8))
                nc.vector.tensor_copy(p.egl[:, :, hs],
                                      m.ps[:, 3 + d, 0:8 * n].rearrange("p (t h) -> p t h", h=8))
            nc.vector.tensor_copy(p.g[:], b[:, 5, :, :])
            link(nc.vector.tensor_copy(b[:, 4, :, 0:1], b[:, 4, :, 0:1]))
            link(nc.vector.tensor_scalar(p.ncum[:], p.cum[:], -1.0, None, ALU.mult))
            link(nc.vector.tensor_tensor(b[:, 0, :, :], p.egl[:], p.cum[:], ALU.subtract))
            dve.wait_ge(s.exps, 3)
            dve.wait_ge(s.beta, 1)
            link(nc.vector.tensor_tensor(p.bege[:], p.beta[:], p.egc[:], ALU.mult))
    st.close()


def delta_heads(m, hg, hx, p, first, after):
    nc, ring = m.nc, m.ring
    st = Stage(m, f"heads{hg}")
    raw = st.sb("raw", [P, 2, SPAN + 2])
    acc = st.sb("acc", [P, 2, SPAN])
    xw = m.x[:].rearrange("p t d -> p (t d)")
    y = xw[:, 0:2 * SPAN].rearrange("p (b c) -> p b c", b=2)
    sq = xw[:, 2 * SPAN:4 * SPAN].rearrange("p (b c) -> p b c", b=2)
    s = st.sem("product copied zeroed chain tapped silu squared summed root turned moved done")
    kinds = [(0, h) for h in range(4)] + [(1, h) for h in range(4)] + [(2, h) for h in range(4)]
    with st.block() as block:
        @block.sync
        def _(sp):
            if hg == 0:
                blank_rows(m, sp, p.o[:, 0, :])
            ring.stream(sp, after)
            sp.wait_ge(m.rows_blank, 16)

        @block.gpsimd
        def _(pool):
            nc.gpsimd.memset(raw[:], 0.0).then_inc(s.zeroed, 1)

        @block.tensor
        def _(pe):
            def project(u):
                kind, h = kinds[u]
                n = first + kind
                if h == 0:
                    ring.wait(pe, n)
                w = whole(KD, 512)(ring.slot(n))
                if u >= 2:
                    pe.wait_ge(s.copied, u - 1)
                b = (u % 2) * 2
                for k in range(KD):
                    last = nc.tensor.matmul(m.ps[:, b, :], w[:, k, h * P:(h + 1) * P], hx[:, k, CT:CT + T],
                                            start=(k == 0), stop=(k == KD - 1))
                if kind > 0:
                    for k in range(KD):
                        last = nc.tensor.matmul(m.ps[:, b + 1, 0:CT], w[:, k, h * P:(h + 1) * P],
                                                hx[:, k, 0:CT], start=(k == 0), stop=(k == KD - 1))
                last.then_inc(s.product, 1)
                if h == 3:
                    pe.wait_ge(s.product, u + 1)
                    pe.sem_inc(ring.freed[n % SLOTS], 1)

            def norm_sum(u):
                kind, h = kinds[u]
                if kind < 2:
                    pe.wait_ge(s.squared, u + 1)
                    if u >= 1:
                        pe.wait_ge(s.root, u)
                    last = nc.tensor.matmul(m.ps[:, 4, :], m.ones, sq[:, u % 2, LAT:SPAN], start=True, stop=True)
                    if kind == 1:
                        last = nc.tensor.matmul(m.ps[:, 5, 0:CT], m.ones, sq[:, u % 2, 0:CT],
                                                start=True, stop=True)
                    last.then_inc(s.summed, 1)

            def turn(u):
                kind, h = kinds[u]
                i = u - 4
                pe.wait_ge(s.silu, u + 1)
                if kind == 1:
                    pe.wait_ge(s.done, u + 1)
                if i >= 1:
                    pe.wait_ge(s.moved, 2 * i)
                src = p.kT[:, h, :] if kind == 1 else y[:, u % 2, :]
                for t in range(NCT + NT):
                    c = t * P if t < NCT else LAT + (t - NCT) * P
                    last = nc.tensor.transpose(m.ps[:, 6 + t // 4, (t % 4) * P:(t % 4 + 1) * P],
                                               src[:, c:c + P], m.ident)
                last.then_inc(s.turned, 1)

            for u in range(len(kinds) + 1):
                if u < len(kinds):
                    project(u)
                if u >= 1:
                    norm_sum(u - 1)
                if 6 <= u <= 9:
                    turn(u - 2)
                if u >= 9:
                    turn(u - 1)

        @block.scalar
        def _(act):
            act.wait_ge(s.zeroed, 1)
            for u, (kind, h) in enumerate(kinds):
                b = (u % 2) * 2
                act.wait_ge(s.product, u + 1)
                if u >= 2:
                    act.wait_ge(s.tapped, u - 1)
                last = nc.scalar.activation(raw[:, u % 2, 1 + LAT:1 + SPAN], m.ps[:, b, :], ACT.Copy)
                if kind > 0:
                    last = nc.scalar.activation(raw[:, u % 2, 1:1 + CT], m.ps[:, b + 1, 0:CT], ACT.Copy)
                last.then_inc(s.copied, 1)
                act.wait_ge(s.tapped, u + 1)
                if u >= 2:
                    act.wait_ge(s.done, min(u - 1, 8))
                    if u - 2 >= 8:
                        act.wait_ge(s.turned, u - 2 - 4 + 1)
                nc.scalar.activation(y[:, u % 2, :], acc[:, u % 2, :], ACT.Silu).then_inc(s.silu, 1)
                if kind < 2:
                    act.wait_ge(s.silu, u + 1)
                    nc.scalar.activation(sq[:, u % 2, :], y[:, u % 2, :], ACT.Square).then_inc(s.squared, 1)
                    act.wait_ge(s.summed, u + 1)
                    if kind == 0:
                        nc.scalar.activation(sq[:, u % 2, LAT:SPAN], m.ps[:, 4, :], ACT.Sqrt,
                                             bias=m.eps[:]).then_inc(s.root, 1)
                    else:
                        nc.scalar.activation(sq[:, u % 2, LAT:SPAN], m.ps[:, 4, :], ACT.Sqrt, bias=m.eps[:])
                        nc.scalar.activation(sq[:, u % 2, 0:CT], m.ps[:, 5, 0:CT], ACT.Sqrt,
                                             bias=m.eps[:]).then_inc(s.root, 1)
                for j in {1: [u - 1] if h else [], 2: [u] if h else [u - 1, u]}.get(kind, []):
                    i, (kj, h) = j - 4, kinds[j]
                    dst = p.k if kj == 1 else p.v
                    act.wait_ge(s.turned, i + 1)
                    nc.scalar.activation(dst[:, 0:4, h * P:(h + 1) * P],
                                         m.ps[:, 6, :].rearrange("p (t c) -> p t c", c=P),
                                         ACT.Copy).then_inc(s.moved, 1)
                    nc.scalar.activation(dst[:, 4:6, h * P:(h + 1) * P],
                                         m.ps[:, 7, 0:2 * P].rearrange("p (t c) -> p t c", c=P),
                                         ACT.Copy).then_inc(s.moved, 1)

        @block.vector
        def _(dve):
            link = Linked(dve, s.chain)
            def norm(u):
                kind, h = kinds[u]
                dve.wait_ge(s.root, u + 1)
                lo = LAT if kind == 0 else 0
                link(nc.vector.reciprocal(sq[:, u % 2, lo:SPAN], sq[:, u % 2, lo:SPAN]))
                if kind == 0:
                    nc.vector.scalar_tensor_tensor(out=p.qT[:, h, :], in0=y[:, u % 2, LAT:SPAN],
                                               scalar=DK ** -0.5, in1=sq[:, u % 2, LAT:SPAN],
                                               op0=ALU.mult, op1=ALU.mult).then_inc(s.done, 1)
                else:
                    nc.vector.tensor_tensor(p.kT[:, h, :], y[:, u % 2, :], sq[:, u % 2, :],
                                        ALU.mult).then_inc(s.done, 1)

            for u, (kind, h) in enumerate(kinds):
                taps = [p.conv[:, j, kind * 8 + hg * 4 + h:kind * 8 + hg * 4 + h + 1] for j in range(3)]
                dve.wait_ge(s.copied, u + 1)
                if u >= 2:
                    dve.wait_ge(s.silu, u - 1)
                link(nc.vector.tensor_scalar(acc[:, u % 2, :], raw[:, u % 2, 0:SPAN], taps[0], None, ALU.mult))
                link(nc.vector.scalar_tensor_tensor(out=acc[:, u % 2, :], in0=raw[:, u % 2, 1:1 + SPAN],
                                                    scalar=taps[1], in1=acc[:, u % 2, :],
                                                    op0=ALU.mult, op1=ALU.add))
                nc.vector.scalar_tensor_tensor(out=acc[:, u % 2, :], in0=raw[:, u % 2, 2:2 + SPAN],
                                               scalar=taps[2], in1=acc[:, u % 2, :],
                                               op0=ALU.mult, op1=ALU.add).then_inc(s.tapped, 1)
                if 1 <= u <= 8:
                    norm(u - 1)
    st.close()


def delta_scan(m, hg, p):
    nc = m.nc
    st = Stage(m, f"scan{hg}")
    W4 = 4 * P
    names = ["L", "Tm", "A", "X", "XT", "Z", "bV", "bK", "kd", "S"]
    spare = [m.x[:, i // 2, (i % 2) * 512:(i % 2) * 512 + 512] for i in range(8)] + \
            [m.mod[:, i * 512:(i + 1) * 512] for i in range(4)]
    extra = st.sb("extra", [P, 8, 512])
    spare += [extra[:, i, :] for i in range(8)]
    B = [{nm: spare[d * 10 + i] for i, nm in enumerate(names)} for d in range(2)]
    ev = ("gcb kk qk argA argB expA expB lower attn bv bk kdec lm inv0 turned0 xt0 z zcopied pq xt xx "
          "w wcopied vps vnew q_s o_s o_add a_v o_done s_ps s_scaled state zero")
    S2 = [st.sem(ev, "f"), st.sem(ev, "b")]
    order = [[0, 1, 2, 3, 4, 5], [1, 0, 5, 4, 3, 2]]
    steps = 6
    LV = 6
    XL = LV - 1

    def blocks(ap, l, odd):
        return ap.rearrange("p (n two s) -> p n two s", two=2, s=2 ** (l + 1))[:, :, int(odd), :]

    def cols(t):
        return t * P if t < NCT else LAT + (t - NCT) * P

    def lat_count(i):
        return max(0, i - NCT)

    def bank(d, b):
        return m.ps[:, 4 * d + b, :]

    def h3(ap):
        return ap.rearrange("p (h c) -> p h c", h=4)

    def hd(ap, h):
        return ap[:, h * P:(h + 1) * P]

    def gate(buf, t, d):
        return buf[:, t, 8 * d + 4 * hg:8 * d + 4 * hg + 4]

    with st.block() as block:
        @block.tensor
        def _(pe):
            def scores(i, d):
                e, b, t = S2[d], B[d], order[d][i]
                c = cols(t)
                if i >= 1:
                    pe.wait_ge(e.xx, XL * i)
                for h in range(4):
                    g = p.g[:, t, 8 * d + 4 * hg + h:8 * d + 4 * hg + h + 1]
                    if i >= NCT + 1 and h == 0:
                        pe.wait_ge(e.o_done, lat_count(i))
                    last = nc.tensor.matmul(hd(bank(d, 2), h), g.to_broadcast([P, P]), p.masks[:, d, :],
                                            start=True, stop=True)
                last.then_inc(e.gcb, 1)
                if i >= 1:
                    pe.wait_ge(e.vnew, i)
                for h in range(4):
                    kt = p.kT[:, h, c:c + P]
                    last = nc.tensor.matmul(hd(bank(d, 0), h), kt, kt, start=True, stop=True)
                last.then_inc(e.kk, 1)
                if t >= NCT:
                    if i >= NCT + 1:
                        pe.wait_ge(e.o_s, lat_count(i))
                    for h in range(4):
                        last = nc.tensor.matmul(hd(bank(d, 1), h), p.kT[:, h, c:c + P],
                                                p.qT[:, h, (t - NCT) * P:(t - NCT + 1) * P],
                                                start=True, stop=True)
                    last.then_inc(e.qk, 1)

            def first_level(i, d):
                e, b = S2[d], B[d]
                pe.wait_ge(e.lm, (LV + 1) * i + 1)
                pe.wait_ge(e.lower, i + 1)
                for h in range(4):
                    last = nc.tensor.transpose(hd(bank(d, 0), h), hd(b["Tm"], h), m.ident)
                last.then_inc(e.turned0, 1)

            def level_z(i, l, d):
                e, b = S2[d], B[d]
                pe.wait_ge(e.lm, (LV + 1) * i + l + 2)
                pe.wait_ge(e.xt0, i + 1)
                pe.wait_ge(e.xt, LV * i + l)
                for h in range(4):
                    out, rhs = hd(bank(d, 0), h), hd(b["XT"], h)
                    if l == LV - 1:
                        out, rhs = blocks(out, l, d == 0), blocks(rhs, l, d == 0)
                    last = nc.tensor.matmul(out, hd(b["Tm"], h), rhs, start=True, stop=True)
                last.then_inc(e.z, 1)

            def level_pq(i, l, d):
                e, b = S2[d], B[d]
                pe.wait_ge(e.zcopied, LV * i + l + 1)
                pe.wait_ge(e.inv0, i + 1)
                pe.wait_ge(e.xx, XL * i + l)
                if order[d][i] >= NCT:
                    pe.wait_ge(e.attn, lat_count(i) + 1)
                for h in range(4):
                    last = nc.tensor.matmul(blocks(hd(bank(d, 1), h), l, d == 0), hd(b["X"], h),
                                            blocks(hd(b["Z"], h), l, d == 0), start=True, stop=True)
                if l < XL:
                    for h in range(4):
                        last = nc.tensor.matmul(blocks(hd(bank(d, 2), h), l, d == 1), hd(b["Z"], h),
                                                blocks(hd(b["X"], h), l, d == 1), start=True, stop=True)
                last.then_inc(e.pq, 1)

            def make_w(i, d):
                e, b = S2[d], B[d]
                pe.wait_ge(e.xt, LV * (i + 1))
                pe.wait_ge(e.bk, i + 1)
                pe.wait_ge(e.state, i)
                for h in range(4):
                    last = nc.tensor.matmul(hd(bank(d, 3), h), hd(b["bK"], h), hd(b["XT"], h),
                                            start=True, stop=True)
                last.then_inc(e.w, 1)

            def chain(i, d):
                e, b, t = S2[d], B[d], order[d][i]
                pe.wait_ge(e.wcopied, i + 1)
                pe.wait_ge(e.bv, i + 1)
                pe.wait_ge(e.zero, 1)
                for h in range(4):
                    nc.tensor.matmul(hd(bank(d, 0), h), hd(b["XT"], h), hd(b["bV"], h), start=True, stop=False)
                    last = nc.tensor.matmul(hd(bank(d, 0), h), hd(b["Z"], h), hd(b["S"], h),
                                            start=False, stop=True)
                last.then_inc(e.vps, 1)
                if t >= NCT:
                    q0 = (t - NCT) * P
                    for h in range(4):
                        last = nc.tensor.matmul(hd(bank(d, 1), h), p.qT[:, h, q0:q0 + P], hd(b["S"], h),
                                                start=True, stop=True)
                    last.then_inc(e.q_s, 1)
                pe.wait_ge(e.vnew, i + 1)
                pe.wait_ge(e.kdec, i + 1)
                if i < steps - 1:
                    for h in range(4):
                        last = nc.tensor.matmul(hd(bank(d, 3), h), hd(b["kd"], h), hd(b["bK"], h),
                                                start=True, stop=True)
                    last.then_inc(e.s_ps, 1)
                if t >= NCT:
                    pe.wait_ge(e.xx, XL * (i + 1))
                    for h in range(4):
                        last = nc.tensor.matmul(hd(bank(d, 2), h), hd(b["A"], h), hd(b["bK"], h),
                                                start=True, stop=True)
                    last.then_inc(e.a_v, 1)

            for i in range(steps):
                for d in range(2):
                    scores(i, d)
                for d in range(2):
                    first_level(i, d)
                for l in range(LV):
                    for d in range(2):
                        level_z(i, l, d)
                    for d in range(2):
                        level_pq(i, l, d)
                for d in range(2):
                    make_w(i, d)
                for d in range(2):
                    chain(i, d)

        @block.scalar
        def _(act):
            for i in range(steps):
                for d in range(2):
                    e, b, t = S2[d], B[d], order[d][i]
                    act.wait_ge(e.argA, i + 1)
                    for h in range(4):
                        j = 8 * d + 4 * hg + h
                        last = nc.scalar.activation(hd(b["L"], h), hd(b["L"], h), ACT.Exp,
                                                    bias=p.cum[:, t, j:j + 1])
                    last.then_inc(e.expA, 1)
                    if t >= NCT:
                        act.wait_ge(e.argB, lat_count(i) + 1)
                        for h in range(4):
                            j = 8 * d + 4 * hg + h
                            last = nc.scalar.activation(hd(b["A"], h), hd(b["A"], h), ACT.Exp,
                                                        bias=p.ncum[:, t, j:j + 1])
                        last.then_inc(e.expB, 1)
                for l in range(LV):
                    for d in range(2):
                        e, b = S2[d], B[d]
                        act.wait_ge(e.z, LV * i + l + 1)
                        if l >= 1:
                            act.wait_ge(e.pq, LV * i + l)
                        elif i >= 1:
                            act.wait_ge(e.vps, i)
                        src, dst = bank(d, 0), b["Z"]
                        if l == LV - 1:
                            src, dst = blocks(src, l, d == 0), blocks(dst, l, d == 0)
                        nc.scalar.activation(dst, src, ACT.Copy).then_inc(e.zcopied, 1)
                for d in range(2):
                    e, b = S2[d], B[d]
                    act.wait_ge(e.w, i + 1)
                    act.wait_ge(e.pq, LV * (i + 1))
                    nc.scalar.mul(b["Z"], bank(d, 3), -1.0).then_inc(e.wcopied, 1)

        @block.gpsimd
        def _(pool):
            for d in range(2):
                nc.gpsimd.memset(B[d]["S"], 0.0).then_inc(S2[d].zero, 1)
            for i in range(steps):
                for d in range(2):
                    e, b, t = S2[d], B[d], order[d][i]
                    if i >= 1:
                        pool.wait_ge(e.vps, i)
                        if i < steps:
                            pool.wait_ge(e.s_ps, i)
                        if lat_count(i):
                            pool.wait_ge(e.a_v, lat_count(i))
                    nc.gpsimd.tensor_tensor(h3(b["bV"]), h3(p.v[:, t, :]), column(gate(p.beta, t, d), 4, P),
                                            ALU.mult).then_inc(e.bv, 1)
                    nc.gpsimd.tensor_tensor(h3(b["bK"]), h3(p.k[:, t, :]), column(gate(p.bege, t, d), 4, P),
                                            ALU.mult).then_inc(e.bk, 1)
                    nc.gpsimd.tensor_tensor(h3(b["kd"]), h3(p.k[:, t, :]), column(gate(p.ekd, t, d), 4, P),
                                            ALU.mult).then_inc(e.kdec, 1)
                for l in range(LV + 1):
                    for d in range(2):
                        e, b = S2[d], B[d]
                        pool.wait_ge(e.lower, i + 1)
                        if l == 1:
                            pool.wait_ge(e.inv0, i + 1)
                            pool.wait_ge(e.turned0, i + 1)
                        if l >= 2:
                            pool.wait_ge(e.z, LV * i + l - 1)
                        if l == 0 and i >= 1:
                            pool.wait_ge(e.z, LV * i)
                        nc.gpsimd.tensor_tensor(h3(b["Tm"]), h3(b["L"]), across(p.masks[:, 6 + 7 * d + l, :], 4),
                                                ALU.mult).then_inc(e.lm, 1)
                if i < steps - 1:
                    for d in range(2):
                        e, b, t = S2[d], B[d], order[d][i]
                        pool.wait_ge(e.vps, i + 1)
                        if t >= NCT:
                            pool.wait_ge(e.q_s, lat_count(i) + 1)
                        if i >= 1:
                            pool.wait_ge(e.state, i)
                        nc.gpsimd.tensor_tensor(h3(b["S"]), h3(b["S"]), column(gate(p.egl, t, d), 4, P),
                                                ALU.mult).then_inc(e.s_scaled, 1)

        @block.vector
        def _(dve):
            for i in range(steps):
                for d in range(2):
                    e, b, t = S2[d], B[d], order[d][i]
                    dve.wait_ge(e.gcb, i + 1)
                    if i >= 1:
                        dve.wait_ge(e.lm, (LV + 1) * i)
                    nc.vector.scalar_tensor_tensor(out=h3(b["L"]), in0=h3(bank(d, 2)), scalar=-1.0,
                                                   in1=across(p.masks[:, 2 + d, :], 4),
                                                   op0=ALU.mult, op1=ALU.add).then_inc(e.argA, 1)
                    if t >= NCT:
                        if i > NCT:
                            dve.wait_ge(e.a_v, lat_count(i))
                        nc.vector.tensor_tensor(h3(b["A"]), h3(bank(d, 2)), across(p.masks[:, 4 + d, :], 4),
                                                ALU.add).then_inc(e.argB, 1)
                for d in range(2):
                    e, b, t = S2[d], B[d], order[d][i]
                    dve.wait_ge(e.expA, i + 1)
                    dve.wait_ge(e.kk, i + 1)
                    for h in range(4):
                        j = 8 * d + 4 * hg + h
                        last = nc.vector.scalar_tensor_tensor(out=hd(b["L"], h), in0=hd(b["L"], h),
                                                              scalar=p.beta[:, t, j:j + 1],
                                                              in1=hd(bank(d, 0), h),
                                                              op0=ALU.mult, op1=ALU.mult)
                    last.then_inc(e.lower, 1)
                    if t >= NCT:
                        dve.wait_ge(e.expB, lat_count(i) + 1)
                        dve.wait_ge(e.qk, lat_count(i) + 1)
                        nc.vector.tensor_tensor(b["A"], b["A"], bank(d, 1), ALU.mult).then_inc(e.attn, 1)
                for d in range(2):
                    e, b = S2[d], B[d]
                    dve.wait_ge(e.lm, (LV + 1) * i + 1)
                    nc.vector.scalar_tensor_tensor(out=h3(b["X"]), in0=h3(b["Tm"]), scalar=-1.0,
                                                   in1=across(m.ident, 4), op0=ALU.mult,
                                                   op1=ALU.add).then_inc(e.inv0, 1)
                    dve.wait_ge(e.turned0, i + 1)
                    nc.vector.scalar_tensor_tensor(out=h3(b["XT"]), in0=h3(bank(d, 0)), scalar=-1.0,
                                                   in1=across(m.ident, 4), op0=ALU.mult,
                                                   op1=ALU.add).then_inc(e.xt0, 1)
                for l in range(LV):
                    for d in range(2):
                        e, b = S2[d], B[d]
                        dve.wait_ge(e.pq, LV * i + l + 1)
                        dve.wait_ge(e.xt0, i + 1)
                        if l:
                            dve.wait_ge(e.xt, LV * i + l)
                            dve.wait_ge(e.xx, XL * i + l)
                        xt, x = blocks(b["XT"], l, d == 0), blocks(b["X"], l, d == 1)
                        nc.vector.tensor_tensor(xt, xt, blocks(bank(d, 1), l, d == 0), ALU.subtract
                                                ).then_inc(e.xt, 1)
                        if l < XL:
                            nc.vector.tensor_tensor(x, x, blocks(bank(d, 2), l, d == 1), ALU.subtract
                                                    ).then_inc(e.xx, 1)
                for d in range(2):
                    e, b, t = S2[d], B[d], order[d][i]
                    dve.wait_ge(e.vps, i + 1)
                    nc.vector.tensor_copy(b["bK"], bank(d, 0)).then_inc(e.vnew, 1)
                    if i < steps - 1:
                        dve.wait_ge(e.s_ps, i + 1)
                        dve.wait_ge(e.s_scaled, i + 1)
                        nc.vector.tensor_tensor(b["S"], b["S"], bank(d, 3), ALU.add).then_inc(e.state, 1)
                    if t >= NCT:
                        n = lat_count(i) + 1
                        dve.wait_ge(e.q_s, n)
                        dve.wait_ge(e.xx, XL * (i + 1))
                        nc.vector.tensor_tensor(h3(b["X"]), h3(bank(d, 1)), column(gate(p.egc, t, d), 4, P),
                                                ALU.mult).then_inc(e.o_s, 1)
                        o = p.o[:, t - NCT, hg * 512:(hg + 1) * 512]
                        dve.wait_ge(e.o_s, n)
                        if i > NCT:
                            dve.wait_ge(S2[1 - d].o_done, lat_count(i) if d == 0 else n)
                            dve.wait_ge(e.o_done, n - 1)
                        elif d == 1:
                            dve.wait_ge(S2[0].o_done, 1)
                        nc.vector.tensor_tensor(o, o, b["X"], ALU.add).then_inc(e.o_add, 1)
                        dve.wait_ge(e.o_add, n)
                        dve.wait_ge(e.a_v, n)
                        nc.vector.tensor_tensor(o, o, bank(d, 2), ALU.add).then_inc(e.o_done, 1)
    st.close()


def delta_finish(m, hx, p, first, after):
    nc, ring = m.nc, m.ring
    st = Stage(m, "ofin")
    zs = st.sb("z", [P, 2, NT, 512])
    sq = st.sb("sq", [P, 512])
    on = st.sb("onorm", [P, DK])
    r = st.sb("r", [P, 3, NT * HEADS])
    s = st.sem("norm_in product silu chain root ready turned evac v")
    units = [(h, t) for h in range(2) for t in range(NT)]
    with st.block() as block:
        @block.sync
        def _(sp):
            sp.dma_start(on[:], p.onorm.partition_broadcast(P)).then_inc(s.norm_in, 16)
            ring.stream(sp, after)

        @block.tensor
        def _(pe):
            for u, (h, t) in enumerate(units):
                ring.wait(pe, first + h)
                w = whole(KD, 512)(ring.slot(first + h))
                if u >= 2:
                    pe.wait_ge(s.silu, u - 1)
                for k in range(KD):
                    last = nc.tensor.matmul(m.ps[:, u % 2, :], hx[:, k, CT + t * P:CT + (t + 1) * P], w[:, k, :],
                                            start=(k == 0), stop=(k == KD - 1))
                last.then_inc(s.product, 1)
                if t == NT - 1:
                    pe.wait_ge(s.product, u + 1)
                    pe.sem_inc(ring.freed[(first + h) % SLOTS], 1)
            for t in range(NT):
                pe.wait_ge(s.ready, t + 1)
                if t >= 1:
                    pe.wait_ge(s.evac, t)
                for k in range(KD):
                    last = nc.tensor.transpose(m.ps[:, 4 + k // 4, (k % 4) * P:(k % 4 + 1) * P],
                                               p.o[:, t, k * P:(k + 1) * P], m.ident)
                last.then_inc(s.turned, 1)

        @block.scalar
        def _(act):
            for u, (h, t) in enumerate(units):
                act.wait_ge(s.product, u + 1)
                nc.scalar.activation(zs[:, h, t, :], m.ps[:, u % 2, :], ACT.Silu).then_inc(s.silu, 1)
            act.wait_ge(s.v, 1)
            nc.scalar.activation(r[:, 2, :], r[:, 1, :], ACT.Sqrt).then_inc(s.root, 1)
            for t in range(NT):
                act.wait_ge(s.turned, t + 1)
                for h in range(2):
                    last = nc.scalar.activation(p.oT[:, 4 * h:4 * h + 4, t * P:(t + 1) * P],
                                                m.ps[:, 4 + h, :].rearrange("p (k t) -> p k t", k=4), ACT.Copy)
                last.then_inc(s.evac, 1)

        @block.vector
        def _(dve):
            link = Linked(dve, s.chain)
            for t in range(NT):
                for h in range(HEADS):
                    link(nc.vector.tensor_tensor_reduce(
                        out=sq[:, 0:P], in0=p.o[:, t, h * P:(h + 1) * P], in1=p.o[:, t, h * P:(h + 1) * P],
                        scale=1.0, scalar=0.0, op0=ALU.mult, op1=ALU.add,
                        accum_out=r[:, 0, t * HEADS + h:t * HEADS + h + 1]))
            nc.vector.tensor_scalar(r[:, 1, :], r[:, 0, :], 1.0 / DK, EPS, ALU.mult, ALU.add).then_inc(s.v, 1)
            dve.wait_ge(s.root, 1)
            link(nc.vector.reciprocal(r[:, 2, :], r[:, 2, :]))
            dve.wait_ge(s.norm_in, 16)
            for t in range(NT):
                o = p.o[:, t, :].rearrange("p (h c) -> p h c", h=HEADS)
                link(nc.vector.tensor_tensor(o, o, column(r[:, 2, t * HEADS:(t + 1) * HEADS], HEADS, P), ALU.mult))
                link(nc.vector.tensor_tensor(o, o, across(on[:], HEADS), ALU.mult))
                dve.wait_ge(s.silu, NT + t + 1)
                o2 = p.o[:, t, :].rearrange("p (h c) -> p h c", h=2)
                nc.vector.tensor_tensor(o2, o2, zs[:, :, t, :], ALU.mult).then_inc(s.ready, 1)
    st.close()


def rank_in_eights(nc, link, src, gt, eq, before, rank):
    n = src.shape[1]
    other, own = src.unsqueeze(2).to_broadcast([P, n, 8, 8]), src.unsqueeze(3).to_broadcast([P, n, 8, 8])
    earlier = before.rearrange("p (i j) -> p i j", i=8).unsqueeze(1).to_broadcast([P, n, 8, 8])
    link(nc.vector.tensor_tensor(gt, other, own, ALU.is_gt))
    link(nc.vector.tensor_tensor(eq, other, own, ALU.is_equal))
    link(nc.vector.tensor_tensor(eq, eq, earlier, ALU.mult))
    link(nc.vector.tensor_tensor(gt, gt, eq, ALU.add))
    link(nc.vector.tensor_reduce(rank, gt, AX_X, ALU.add))


def route_groups_stage(m, tag, hT, router_g, router_e, wt, sel, after):
    nc = m.nc
    st = Stage(m, f"route{tag}")
    rw = st.sb("w", [P, KD, 36])
    lg = st.sb("group_logits", [P, NT, 8])
    le = st.sb("expert_logits", [P, NT, 32])
    gt = st.sb("gt", [P, NT * 4, 8, 8])
    eq = st.sb("eq", [P, NT * 4, 8, 8])
    rk = st.sb("rank", [P, NT * 4, 8])
    ge = st.sb("group_rank", [P, NT, 8])
    c = st.sb("cols", [P, 6, NT])
    s = st.sem("in_ logits chain groups_shifted groups_exp shifted exp")
    with st.block() as block:
        @block.sync
        def _(sp):
            sp.dma_start(rw[:, :, 0:4], router_g.rearrange("(k p) n -> p k n", p=P)).then_inc(s.in_, 16)
            sp.dma_start(rw[:, :, 4:36], router_e.rearrange("(k p) n -> p k n", p=P)).then_inc(s.in_, 16)
            m.ring.stream(sp, after)

        @block.tensor
        def _(pe):
            pe.wait_ge(s.in_, 32)
            for t in range(NT):
                for k in range(KD):
                    last = nc.tensor.matmul(m.ps[:, 0, t * 36:(t + 1) * 36], hT[:, k, t * P:(t + 1) * P],
                                            rw[:, k, :], start=(k == 0), stop=(k == KD - 1))
            last.then_inc(s.logits, 1)

        @block.scalar
        def _(act):
            act.wait_ge(s.groups_shifted, 1)
            nc.scalar.activation(ge[:, :, 0:4], ge[:, :, 0:4], ACT.Exp).then_inc(s.groups_exp, 1)
            act.wait_ge(s.shifted, 1)
            nc.scalar.activation(wt, wt, ACT.Exp).then_inc(s.exp, 1)

        @block.vector
        def _(dve):
            link = Linked(dve, s.chain)
            link(nc.vector.memset(lg[:, :, 4:8], NEG))
            dve.wait_ge(s.logits, 1)
            src = m.ps[:, 0, 0:NT * 36].rearrange("p (t c) -> p t c", c=36)
            link(nc.vector.tensor_copy(lg[:, :, 0:4], src[:, :, 0:4]))
            link(nc.vector.tensor_copy(le[:], src[:, :, 4:36]))
            link(nc.vector.tensor_reduce(c[:, 0, :], lg[:], AX_X, ALU.max))
            nc.vector.tensor_tensor(ge[:, :, 0:4], lg[:, :, 0:4], column(c[:, 0, :], NT, 4),
                                    ALU.subtract).then_inc(s.groups_shifted, 1)
            dve.wait_ge(s.groups_exp, 1)
            link(nc.vector.tensor_reduce(c[:, 1, :], ge[:, :, 0:4], AX_X, ALU.add))
            link(nc.vector.reciprocal(c[:, 1, :], c[:, 1, :]))
            rank_in_eights(nc, link, lg[:], gt[:, 0:NT], eq[:, 0:NT], m.before, ge[:])
            link(nc.vector.tensor_scalar(ge[:], ge[:], 0.5, NEG, ALU.is_gt, ALU.mult))
            le8 = le[:].rearrange("p t (g e) -> p t g e", g=4)
            wt8 = wt.rearrange("p t (g e) -> p t g e", g=4)
            link(nc.vector.tensor_tensor(wt8, le8, ge[:, :, 0:4].unsqueeze(3).to_broadcast([P, NT, 4, 8]), ALU.add))
            link(nc.vector.tensor_reduce(c[:, 2, :], wt, AX_X, ALU.max))
            nc.vector.tensor_tensor(wt, wt, column(c[:, 2, :], NT, 32), ALU.subtract).then_inc(s.shifted, 1)
            rank_in_eights(nc, link, le[:].rearrange("p t (g e) -> p (t g) e", e=8), gt[:], eq[:], m.before, rk[:])
            link(nc.vector.tensor_scalar(rk[:], rk[:], 1.5, None, ALU.is_lt))
            link(nc.vector.tensor_scalar(ge[:], ge[:], -0.5, None, ALU.is_gt))
            link(nc.vector.tensor_tensor(sel.rearrange("p t (g e) -> p t g e", g=4),
                                         rk[:].rearrange("p (t g) e -> p t g e", t=NT),
                                         ge[:, :, 0:4].unsqueeze(3).to_broadcast([P, NT, 4, 8]), ALU.mult))
            dve.wait_ge(s.exp, 1)
            link(nc.vector.tensor_tensor(wt, wt, sel, ALU.mult))
            link(nc.vector.tensor_reduce(c[:, 3, :], wt, AX_X, ALU.add))
            link(nc.vector.reciprocal(c[:, 3, :], c[:, 3, :]))
            link(nc.vector.tensor_tensor(c[:, 4, :], c[:, 3, :], c[:, 1, :], ALU.mult))
            link(nc.vector.tensor_tensor(wt, wt, column(c[:, 4, :], NT, 32), ALU.mult))
    st.close()


def route_sigmoid_stage(m, tag, hT, router, bias, wt, sel, after):
    nc = m.nc
    st = Stage(m, f"route{tag}")
    rw = st.sb("w", [P, KD, E2])
    bb = st.sb("bias", [P, E2])
    sc = st.sb("scores", [P, NT, E2])
    ch = st.sb("choice", [P, NT, E2])
    gt = st.sb("gt", [P, NT * 8, 8, 8])
    eq = st.sb("eq", [P, NT * 8, 8, 8])
    rk = st.sb("rank", [P, NT * 8, 8])
    gs = st.sb("group", [P, NT, 8])
    gr = st.sb("group_rank", [P, NT, 8])
    top = st.sb("top", [P, NT, 8])
    c = st.sb("cols", [P, NT])
    s = st.sem("in_ logits chain scores")
    with st.block() as block:
        @block.sync
        def _(sp):
            sp.dma_start(rw[:], router.rearrange("(k p) n -> p k n", p=P)).then_inc(s.in_, 16)
            sp.dma_start(bb[:], bias.partition_broadcast(P)).then_inc(s.in_, 16)
            m.ring.stream(sp, after)

        @block.tensor
        def _(pe):
            pe.wait_ge(s.in_, 32)
            for t in range(NT):
                for k in range(KD):
                    last = nc.tensor.matmul(m.ps[:, 0, t * E2:(t + 1) * E2], hT[:, k, t * P:(t + 1) * P],
                                            rw[:, k, :], start=(k == 0), stop=(k == KD - 1))
            last.then_inc(s.logits, 1)

        @block.scalar
        def _(act):
            act.wait_ge(s.logits, 1)
            nc.scalar.activation(sc[:], m.ps[:, 0, 0:NT * E2].rearrange("p (t e) -> p t e", t=NT),
                                 ACT.Sigmoid).then_inc(s.scores, 1)

        @block.vector
        def _(dve):
            link = Linked(dve, s.chain)
            dve.wait_ge(s.in_, 32)
            dve.wait_ge(s.scores, 1)
            link(nc.vector.tensor_tensor(ch[:], sc[:], across(bb[:], NT), ALU.add))
            ch8 = ch[:].rearrange("p t (g e) -> p (t g) e", e=8)
            rank_in_eights(nc, link, ch8, gt[:], eq[:], m.before, rk[:])
            link(nc.vector.scalar_tensor_tensor(out=rk[:], in0=rk[:], scalar=1.5, in1=ch8,
                                                op0=ALU.is_lt, op1=ALU.mult))
            link(nc.vector.tensor_reduce(gs[:].rearrange("p t g -> p (t g)"), rk[:], AX_X, ALU.add))
            rank_in_eights(nc, link, gs[:], gt[:, 0:NT], eq[:, 0:NT], m.before, gr[:])
            link(nc.vector.tensor_scalar(gr[:], gr[:], 3.5, NEG, ALU.is_gt, ALU.mult))
            c8 = ch[:].rearrange("p t (g e) -> p t g e", e=8)
            link(nc.vector.tensor_tensor(c8, c8, gr[:].unsqueeze(3).to_broadcast([P, NT, 8, 8]), ALU.add))
            for t in range(NT):
                link(nc.vector.max(top[:, t, :], ch[:, t, :]))
                link(nc.vector.match_replace(wt[:, t, :], top[:, t, :], ch[:, t, :], -3e38))
            link(nc.vector.tensor_tensor(sel, wt, ch[:], ALU.not_equal))
            link(nc.vector.tensor_tensor(wt, sel, sc[:], ALU.mult))
            link(nc.vector.tensor_reduce(c[:], wt, AX_X, ALU.add))
            link(nc.vector.reciprocal(c[:], c[:]))
            link(nc.vector.tensor_scalar(c[:], c[:], 2.5, None, ALU.mult))
            link(nc.vector.tensor_tensor(wt, wt, column(c[:], NT, E2), ALU.mult))
    st.close()


def dispatch_stage(m, tag, hT, sel, wt, n_exp, top, units, r, after):
    nc = m.nc
    st = Stage(m, f"disp{tag}")
    E = n_exp
    rank = st.sb("rank", [P, NT, E])
    cnt = st.sb("count", [P, 3, E + 1])
    nth = st.sb("nth", [P, 2, NT, E])
    pick = st.sb("pick", [P, NT, E])
    pick2 = st.sb("pick2", [P, NT, E])
    destf = st.sb("destf", [P, NT, top])
    tab = st.sb("table", [P, 2, P])
    ids = st.sb("ids", [P, NT])
    earlier = st.sb("earlier", [P, P])
    table = nc.dram_tensor(f"slot_table{tag}", [(units + 1) * P, 1], F32).ap()
    s = st.sem("ids_in earlier_in empty filled ranks chain dest scattered read_back turned done")
    with st.block() as block:
        @block.sync
        def _(sp):
            sp.dma_start(ids[:], m.ids).then_inc(s.ids_in, 16)
            sp.dma_start(earlier[:], m.earlier).then_inc(s.earlier_in, 16)
            sp.wait_ge(s.empty, 1)
            rows = table.rearrange("(u s) o -> u (s o)", s=P)
            sp.dma_start(rows, tab[0:units + 1, 0, :]).then_inc(s.filled, 16)
            m.ring.stream(sp, after)
            sp.wait_ge(s.scattered, 16 * NT * top)
            sp.dma_start(tab[0:units + 1, 1, :], rows).then_inc(s.read_back, 16)
            sp.wait_ge(s.read_back, 16)

        @block.tensor
        def _(pe):
            pe.wait_ge(s.earlier_in, 16)
            for t in range(NT):
                out = m.ps[:, 0, t * E:(t + 1) * E]
                for b in range(t):
                    nc.tensor.matmul(out, m.ones, sel[:, b, :], start=(b == 0), stop=False)
                nc.tensor.matmul(out, earlier[:], sel[:, t, :], start=(t == 0), stop=True)
            for t in range(NT):
                last = nc.tensor.matmul(m.ps[:, 1, 0:E], m.ones, sel[:, t, :], start=(t == 0), stop=(t == NT - 1))
            last.then_inc(s.ranks, 1)
            pe.wait_ge(s.read_back, 16)
            nc.tensor.transpose(m.ps[:, 2, 0:units + 1], tab[0:units + 1, 1, :],
                                m.ident[0:units + 1, 0:units + 1]).then_inc(s.turned, 1)

        @block.vector
        def _(dve):
            link = Linked(dve, s.chain)
            nc.vector.memset(tab[:, 0, :], float(EMPTY)).then_inc(s.empty, 1)
            dve.wait_ge(s.ranks, 1)
            a, b, c = cnt[:, 0, :], cnt[:, 1, :], cnt[:, 2, :]
            link(nc.vector.memset(cnt[:], 0.0))
            n, o = m.ps[:, 1, 0:E], b[:, 1:E + 1]
            link(nc.vector.tensor_scalar(o, n, 128.5, 1.0, ALU.is_gt, ALU.add))
            for more in (256.5, 384.5):
                link(nc.vector.tensor_scalar(a[:, 0:E], n, more, None, ALU.is_gt))
                link(nc.vector.tensor_tensor(o, o, a[:, 0:E], ALU.add))
            cur, new, d = b, c, 1
            while d <= E:
                link(nc.vector.tensor_copy(new[:, 0:d], cur[:, 0:d]))
                link(nc.vector.tensor_tensor(new[:, d:E + 1], cur[:, d:E + 1], cur[:, 0:E + 1 - d], ALU.add))
                cur, new, d = new, cur, 2 * d
            link(nc.vector.tensor_copy(r.start[:], cur[0:1, :]))
            link(nc.vector.tensor_scalar(new, cur, float(P), None, ALU.mult))
            link(nc.vector.tensor_tensor(rank[:], m.ps[:, 0, 0:NT * E].rearrange("p (t e) -> p t e", t=NT),
                                         across(new[:, 0:E], NT), ALU.add))
            x, y, d = nth[:, 0], nth[:, 1], 1
            link(nc.vector.tensor_copy(x, sel))
            while d < E:
                link(nc.vector.tensor_copy(y[:, :, 0:d], x[:, :, 0:d]))
                link(nc.vector.tensor_tensor(y[:, :, d:E], x[:, :, d:E], x[:, :, 0:E - d], ALU.add))
                x, y, d = y, x, 2 * d
            link(nc.vector.tensor_tensor(x, x, sel, ALU.mult))
            for k in range(top):
                link(nc.vector.tensor_scalar(pick[:], x, float(k + 1), None, ALU.is_equal))
                link(nc.vector.tensor_tensor(pick2[:], pick[:], rank[:], ALU.mult))
                link(nc.vector.tensor_reduce(destf[:, :, k], pick2[:], AX_X, ALU.add))
                nc.vector.tensor_copy(r.dest[:, :, k], destf[:, :, k]).then_inc(s.dest, 1)
                link(nc.vector.tensor_tensor(pick[:], pick[:], wt, ALU.mult))
                link(nc.vector.tensor_reduce(r.share[:, :, k], pick[:], AX_X, ALU.add))
            dve.wait_ge(s.turned, 1)
            link(nc.vector.tensor_copy(r.slot_token[:, units + 1:units + 2], tab[:, 0, 0:1]))
            nc.vector.tensor_copy(r.slot_token[:, 0:units + 1], m.ps[:, 2, 0:units + 1]).then_inc(s.done, 1)
            dve.wait_ge(s.done, 1)

        @block.gpsimd
        def _(pool):
            pool.wait_ge(s.ids_in, 16)
            pool.wait_ge(s.filled, 16)
            for k in range(top):
                pool.wait_ge(s.dest, k + 1)
                for t in range(NT):
                    nc.gpsimd.indirect_dma_start(
                        out=table, out_offset=bass.IndirectOffsetOnAxis(ap=r.dest[:, t, k:k + 1], axis=0),
                        in_=ids[:, t:t + 1], in_offset=None).then_inc(s.scattered, 16)
            pool.wait_ge(s.scattered, 16 * NT * top)
    st.close()


def sparse_experts_stage(m, tag, first, groups, G, F, hidden, rows, r, source, after):
    nc, ring = m.nc, m.ring
    st = Stage(m, f"moe{tag}")
    FC = F // P
    spare = st.sb("spare", [P, 3, SLOT])
    xin = st.sb("xin", [P, D])
    xg = st.sb("xg", [P, D])
    xT = st.sb("xT", [P, KD, P])
    sg = st.sb("sg", [P, F])
    act_ = st.sb("act", [P, F])
    aT = st.sb("aT", [P, FC, P])
    yo = st.sb("y", [P, D])
    icol = st.sb("icol", [P, 1], U32)
    s = st.sem("spare_in0 spare_in1 spare_in2 zeroed icol x_in x_moved x_turned x_ready up silu act h_turned a_ready y_ps y_copied "
               "y_out all_out gathers paced")
    spare_in = [s.spare_in0, s.spare_in1, s.spare_in2]
    slot = [(first + j) % SLOTS for j in range(3)]
    bufs = [[ring.slot(first + j) for j in range(3)], [spare[:, j, :] for j in range(3)]]
    halves = groups // 2

    def shape(j):
        return whole(4, D) if j == 2 else whole(KD, 512)

    with st.block() as block:
        @block.sync
        def _(sp):
            ring.stream(sp, first + 3)
            for j in range(3):
                sp.dma_start(shape(j)(bufs[1][j]), source(1, j)).then_inc(spare_in[j], 16)
            with sp.Fori(1, halves) as i:
                for half in range(2):
                    done = sp.value_load(r.start[0:1, bass.ds((2 * i + half - 1) * G, 1)],
                                         min_val=1, max_val=r.units)
                    for j in range(3):
                        sp.wait_ge(s.y_ps, 2 * done)
                        sp.sem_inc(s.paced, 1)
                        before = (j + 1) % 3
                        if (half == 0) == (j == 2):
                            sp.wait_ge(ring.loaded[slot[before]], ring.loads(first + before) + 16 * i)
                        else:
                            sp.wait_ge(spare_in[before], 16 * i + 16 * int(j == 2))
                        sp.sem_inc(s.paced, 1)
                        sp.dma_start(shape(j)(bufs[half][j]), source(2 * i + half, j)
                                     ).then_inc(ring.loaded[slot[j]] if half == 0 else spare_in[j], 16)
            ring.sent = first + 3 * halves
            ring.stream(sp, after)

        @block.gpsimd
        def _(pool):
            nc.gpsimd.memset(xin[:], 0.0).then_inc(s.zeroed, 1)
            pool.wait_ge(s.zeroed, 1)
            token_limit = pool.to_reg(T - 1)

            def gather(u):
                nc.gpsimd.tensor_copy(icol[:], r.slot_token[:, bass.ds(u, 1)]).then_inc(s.icol, 1)
                pool.wait_ge(s.icol, u + 1)
                pool.sem_inc(s.gathers, 1)
                nc.gpsimd.indirect_dma_start(
                    out=xin[:], out_offset=None, in_=hidden,
                    in_offset=bass.IndirectOffsetOnAxis(ap=icol[:, 0:1], axis=0),
                    bounds_check=token_limit, oob_is_err=False).then_inc(s.x_in, 16)

            n = pool.value_load(r.start[0:1, groups * G:groups * G + 1], min_val=groups * G, max_val=r.units)
            gather(0)
            pool.wait_ge(s.x_in, 16)
            nc.gpsimd.tensor_copy(xg[:], xin[:]).then_inc(s.x_moved, 1)
            pool.wait_ge(s.x_moved, 1)
            gather(1)
            with pool.Fori(1, n + 1) as u:
                pool.wait_ge(s.x_in, 16 * u + 16)
                pool.wait_ge(s.x_turned, u)
                pool.sem_inc(s.gathers, 1)
                nc.gpsimd.tensor_copy(xg[:], xin[:]).then_inc(s.x_moved, 1)
                pool.wait_ge(s.x_moved, u + 1)
                gather(u + 1)
            pool.wait_ge(s.x_in, 16 * n + 32)
            pool.sem_inc(s.gathers, 1)

        @block.tensor
        def _(pe):
            def turn_x(u, half):
                if half == 0:
                    pe.wait_ge(s.x_moved, u + 1)
                for k in range(4 * half, 4 * half + 4):
                    last = nc.tensor.transpose(m.ps[:, 2 + k // 4, (k % 4) * P:(k % 4 + 1) * P],
                                               xg[:, k * P:(k + 1) * P], m.ident)
                if half == 1:
                    last.then_inc(s.x_turned, 1)

            def unit(u, gate, up, down, x, weights_there):
                pe.wait_ge(s.x_ready, u + 1)
                weights_there(x)
                if G == 1:
                    pe.wait_ge(s.silu, u + 1)
                    for k in range(KD):
                        last = nc.tensor.matmul(m.ps[:, 0, :], xT[:, k, :], gate[:, k, :],
                                                start=(k == 0), stop=(k == KD - 1))
                    last.then_inc(s.up, 1)
                    weights_there(1)
                    pe.wait_ge(s.act, FC * u + 1)
                    for k in range(KD):
                        last = nc.tensor.matmul(m.ps[:, 1, :], xT[:, k, :], up[:, k, :],
                                                start=(k == 0), stop=(k == KD - 1))
                    last.then_inc(s.up, 1)
                else:
                    pe.wait_ge(s.act, FC * u + 1)
                    for k in range(KD):
                        last = nc.tensor.matmul(m.ps[:, 0, :], xT[:, k, :], gate[:, k, :],
                                                start=(k == 0), stop=(k == KD - 1))
                    last.then_inc(s.up, 1)
                turn_x(u + 1, 0)
                pe.wait_ge(s.a_ready, u + 1)
                for j in range(FC):
                    pe.wait_ge(s.act, FC * u + j + 2)
                    last = nc.tensor.transpose(m.ps[:, 4, j * P:(j + 1) * P], act_[:, j * P:(j + 1) * P], m.ident)
                last.then_inc(s.h_turned, 1)
                turn_x(u + 1, 1)
                weights_there(2)
                pe.wait_ge(s.a_ready, u + 2)
                pe.wait_ge(s.y_copied, 2 * u + 1)
                for h in range(2):
                    for j in range(FC):
                        last = nc.tensor.matmul(m.ps[:, 5 + h, :], aT[:, j, :], down[:, j, h * 512:(h + 1) * 512],
                                                start=(j == 0), stop=(j == FC - 1))
                    last.then_inc(s.y_ps, 1)

            turn_x(0, 0)
            turn_x(0, 1)
            with pe.Fori(0, halves) as i:
                for half in range(2):
                    v = [shape(j)(bufs[half][j]) for j in range(3)]
                    e = (2 * i + half) * G
                    bounds = [pe.value_load(r.start[0:1, bass.ds(e + x, 1)], min_val=0, max_val=r.units)
                              for x in range(G + 1)]

                    def weights_there(j):
                        if half == 0:
                            pe.wait_ge(ring.loaded[slot[j]], ring.loads(first + j) + 16 * i)
                        else:
                            pe.wait_ge(spare_in[j], 16 * i + 16)

                    for x in range(G):
                        with pe.Fori(bounds[x], bounds[x + 1]) as u:
                            if G == 1:
                                unit(u, v[0], v[1], v[2], 0, weights_there)
                            else:
                                unit(u, v[x], None, v[2][:, x * FC:(x + 1) * FC, :], x, weights_there)
            pe.wait_ge(s.y_ps, 2 * bounds[G])
            for j in range(3):
                pe.sem_inc(ring.freed[slot[j]], halves)

        @block.scalar
        def _(act):
            act.sem_inc(s.silu, 1)
            act.sem_inc(s.a_ready, 1)
            n = act.value_load(r.start[0:1, groups * G:groups * G + 1], min_val=groups * G, max_val=r.units)

            def move_x(u):
                act.wait_ge(s.x_turned, u + 1)
                for h in range(2):
                    last = nc.scalar.activation(xT[:, 4 * h:4 * h + 4, :],
                                                m.ps[:, 2 + h, :].rearrange("p (k c) -> p k c", k=4), ACT.Copy)
                last.then_inc(s.x_ready, 1)

            move_x(0)
            with act.Fori(0, n) as u:
                act.wait_ge(s.up, (2 if G == 1 else 1) * u + 1)
                act.wait_ge(s.act, FC * u + 1)
                nc.scalar.activation(sg[:], m.ps[:, 0, 0:F], ACT.Silu).then_inc(s.silu, 1)
                act.wait_ge(s.h_turned, u + 1)
                nc.scalar.activation(aT[:], m.ps[:, 4, 0:F].rearrange("p (k c) -> p k c", k=FC),
                                     ACT.Copy).then_inc(s.a_ready, 1)
                move_x(u + 1)
                for h in range(2):
                    act.wait_ge(s.y_copied, 2 * u + 2 + h)
                act.dma_start(rows[bass.ds(u * P, P), :], yo[:]).then_inc(s.y_out, 16)
            act.wait_ge(s.y_out, 16 * n + 16)
            act.sem_inc(s.all_out, 1)

        @block.vector
        def _(dve):
            dve.sem_inc(s.act, 1)
            dve.sem_inc(s.y_copied, 1)
            dve.sem_inc(s.y_out, 16)
            n = dve.value_load(r.start[0:1, groups * G:groups * G + 1], min_val=groups * G, max_val=r.units)
            with dve.Fori(0, n) as u:
                dve.wait_ge(s.silu, u + 2)
                dve.wait_ge(s.up, (2 if G == 1 else 1) * (u + 1))
                for j in range(FC):
                    up = m.ps[:, 1, j * P:(j + 1) * P] if G == 1 else m.ps[:, 0, F + j * P:F + (j + 1) * P]
                    nc.vector.tensor_tensor(act_[:, j * P:(j + 1) * P], sg[:, j * P:(j + 1) * P], up,
                                            ALU.mult).then_inc(s.act, 1)
                dve.wait_ge(s.y_out, 16 * u + 16)
                for h in range(2):
                    dve.wait_ge(s.y_ps, 2 * u + h + 1)
                    nc.vector.tensor_copy(yo[:, h * 512:(h + 1) * 512], m.ps[:, 5 + h, :]).then_inc(s.y_copied, 1)
    st.close()


def shared_expert_stage(m, hT, y, first, after):
    nc, ring = m.nc, m.ring
    st = Stage(m, "shared")
    F = F2
    sg = st.sb("sg", [P, 2, F])
    a = st.sb("act", [P, 2, F])
    aT = st.sb("aT", [P, 2, 2, P])
    s = st.sem("gu silu act turned a_ready y_ps y_copied")
    with st.block() as block:
        @block.sync
        def _(sp):
            ring.stream(sp, after)

        @block.tensor
        def _(pe):
            gu, dn = whole(KD, 512)(ring.slot(first)), whole(2, D)(ring.slot(first + 1))
            ring.wait(pe, first)
            ring.wait(pe, first + 1)
            for t in range(NT + 1):
                if t < NT:
                    if t >= 2:
                        pe.wait_ge(s.act, t - 1)
                    for k in range(KD):
                        last = nc.tensor.matmul(m.ps[:, t % 2, :], hT[:, k, t * P:(t + 1) * P], gu[:, k, :],
                                                start=(k == 0), stop=(k == KD - 1))
                    last.then_inc(s.gu, 1)
                if t:
                    v = t - 1
                    pe.wait_ge(s.act, v + 1)
                    if v:
                        pe.wait_ge(s.a_ready, v)
                    for j in range(2):
                        last = nc.tensor.transpose(m.ps[:, 2, j * P:(j + 1) * P], a[:, v % 2, j * P:(j + 1) * P],
                                                   m.ident)
                    last.then_inc(s.turned, 1)
                    pe.wait_ge(s.a_ready, v + 1)
                    if v:
                        pe.wait_ge(s.y_copied, 2 * v)
                    for h in range(2):
                        for j in range(2):
                            last = nc.tensor.matmul(m.ps[:, 4 + h, :], aT[:, v % 2, j, :],
                                                    dn[:, j, h * 512:(h + 1) * 512], start=(j == 0), stop=(j == 1))
                        last.then_inc(s.y_ps, 1)
            pe.wait_ge(s.y_ps, 2 * NT)
            for n in (first, first + 1):
                pe.sem_inc(ring.freed[n % SLOTS], 1)

        @block.scalar
        def _(act):
            for t in range(NT):
                act.wait_ge(s.gu, t + 1)
                if t >= 2:
                    act.wait_ge(s.act, t - 1)
                nc.scalar.activation(sg[:, t % 2, :], m.ps[:, t % 2, 0:F], ACT.Silu).then_inc(s.silu, 1)
                act.wait_ge(s.turned, t + 1)
                if t >= 2:
                    act.wait_ge(s.y_ps, 2 * t - 2)
                nc.scalar.activation(aT[:, t % 2, :, :], m.ps[:, 2, 0:F].rearrange("p (k c) -> p k c", k=2),
                                     ACT.Copy).then_inc(s.a_ready, 1)

        @block.vector
        def _(dve):
            for t in range(NT):
                dve.wait_ge(s.silu, t + 1)
                if t >= 2:
                    dve.wait_ge(s.turned, t - 1)
                nc.vector.tensor_tensor(a[:, t % 2, :], sg[:, t % 2, :], m.ps[:, t % 2, F:2 * F],
                                        ALU.mult).then_inc(s.act, 1)
                for h in range(2):
                    dve.wait_ge(s.y_ps, 2 * t + h + 1)
                    nc.vector.tensor_copy(y[:, t, h * 512:(h + 1) * 512], m.ps[:, 4 + h, :]).then_inc(s.y_copied, 1)
    st.close()


def combine_stage(m, tag, top, rows, r, y, fresh, after):
    nc = m.nc
    st = Stage(m, f"comb{tag}")
    NG = 4
    g = st.sb("rows", [P, NG, D])
    s = st.sem("in0 in1 in2 in3 added")
    arrived = [s.in0, s.in1, s.in2, s.in3]
    pairs = [(k, t) for k in range(top) for t in range(NT)]
    with st.block() as block:
        @block.sync
        def _(sp):
            m.ring.stream(sp, after)

        @block.gpsimd
        def _(pool):
            for i, (k, t) in enumerate(pairs):
                if i >= NG:
                    pool.wait_ge(s.added, i - NG + 1)
                nc.gpsimd.indirect_dma_start(
                    out=g[:, i % NG, :], out_offset=None, in_=rows,
                    in_offset=bass.IndirectOffsetOnAxis(ap=r.dest[:, t, k:k + 1], axis=0)
                ).then_inc(arrived[i % NG], 16)

        @block.vector
        def _(dve):
            for i, (k, t) in enumerate(pairs):
                dve.wait_ge(arrived[i % NG], 16 * (i // NG + 1))
                if i >= NT:
                    dve.wait_ge(s.added, i - NT + 1)
                if fresh and k == 0:
                    nc.vector.tensor_scalar(y[:, t, :], g[:, i % NG, :], r.share[:, t, k:k + 1], None,
                                            ALU.mult).then_inc(s.added, 1)
                else:
                    nc.vector.scalar_tensor_tensor(out=y[:, t, :], in0=g[:, i % NG, :], scalar=r.share[:, t, k:k + 1],
                                                   in1=y[:, t, :], op0=ALU.mult, op1=ALU.add).then_inc(s.added, 1)
    st.close()


def residual_stage(m, tag, y, gate, after, gain=None, out=None):
    nc = m.nc
    st = Stage(m, f"res{tag}")
    gb = st.sb("gain", [P, D])
    junk = st.sb("junk", [P, D])
    r = st.sb("r", [P, 3, NT])
    s = st.sem("gain_in chain v root done out")
    with st.block() as block:
        @block.sync
        def _(sp):
            if gain is not None:
                sp.dma_start(gb[:], gain.partition_broadcast(P)).then_inc(s.gain_in, 16)
            m.ring.stream(sp, after)
            if out is not None:
                for t in range(NT):
                    sp.wait_ge(s.done, t + 1)
                    sp.dma_start(out[t * P:(t + 1) * P, :], m.x[:, t, :]).then_inc(s.out, 16)
                sp.wait_ge(s.out, 16 * NT)

        @block.scalar
        def _(act):
            if gain is not None:
                act.wait_ge(s.v, 1)
                nc.scalar.activation(r[:, 2, :], r[:, 1, :], ACT.Sqrt).then_inc(s.root, 1)

        @block.vector
        def _(dve):
            link = Linked(dve, s.chain)
            for t in range(NT):
                link(nc.vector.tensor_tensor(y[:, t, :], y[:, t, :], gate, ALU.mult))
                link(nc.vector.tensor_tensor(m.x[:, t, :], m.x[:, t, :], y[:, t, :], ALU.add))
                if gain is not None:
                    link(nc.vector.tensor_tensor_reduce(out=junk[:], in0=m.x[:, t, :], in1=m.x[:, t, :],
                                                        scale=1.0, scalar=0.0, op0=ALU.mult, op1=ALU.add,
                                                        accum_out=r[:, 0, t:t + 1]))
            if gain is not None:
                nc.vector.tensor_scalar(r[:, 1, :], r[:, 0, :], 1.0 / D, EPS, ALU.mult, ALU.add).then_inc(s.v, 1)
                dve.wait_ge(s.v, 1)
                dve.wait_ge(s.root, 1)
                q, v, a = r[:, 2, :], r[:, 1, :], r[:, 0, :]
                link(nc.vector.reciprocal(q, q))
                link(nc.vector.tensor_tensor(a, q, q, ALU.mult))
                link(nc.vector.tensor_tensor(a, a, v, ALU.mult))
                link(nc.vector.tensor_scalar(a, a, -0.5, 1.5, ALU.mult, ALU.add))
                link(nc.vector.tensor_tensor(q, q, a, ALU.mult))
                dve.wait_ge(s.gain_in, 16)
                for t in range(NT):
                    nc.vector.scalar_tensor_tensor(out=m.x[:, t, :], in0=m.x[:, t, :], scalar=q[:, t:t + 1],
                                                   in1=gb[:], op0=ALU.mult, op1=ALU.mult).then_inc(s.done, 1)
    st.close()


def shortconv_stage(m, hT, yT, first, conv, after):
    nc, ring = m.nc, m.ring
    st = Stage(m, "conv")
    W = 64
    cw = st.sb("w", [P, 3, KD])
    u_ = st.sb("u", [P, 2, T + 2 * W])
    cg = st.sb("cg", [P, 2, T])
    acc = st.sb("acc", [P, 2, T])
    s = st.sem("w_in zeroed product c_there u_there chain acc done")
    with st.block() as block:
        @block.sync
        def _(sp):
            for j in range(3):
                sp.dma_start(cw[:, j, :], conv[j, :].rearrange("(k p) -> p k", p=P),
                             allow_slow_non_contiguous=True).then_inc(s.w_in, 16)
            ring.stream(sp, after)

        @block.gpsimd
        def _(pool):
            nc.gpsimd.memset(u_[:], 0.0).then_inc(s.zeroed, 1)

        @block.tensor
        def _(pe):
            for c in range(KD):
                half, q = c // 4, c % 4
                if c >= 2:
                    pe.wait_ge(s.done, c - 1)
                for j in range(3):
                    n = first + 3 * half + j
                    if q == 0:
                        ring.wait(pe, n)
                    w = whole(KD, 512)(ring.slot(n))
                    for k in range(KD):
                        last = nc.tensor.matmul(m.ps[:, 4 * (c % 2) + j, :], w[:, k, q * P:(q + 1) * P],
                                                hT[:, k, :], start=(k == 0), stop=(k == KD - 1))
                last.then_inc(s.product, 1)
                if q == 3:
                    pe.wait_ge(s.product, c + 1)
                    for j in range(3):
                        pe.sem_inc(ring.freed[(first + 3 * half + j) % SLOTS], 1)

        @block.scalar
        def _(act):
            for c in range(KD):
                act.wait_ge(s.product, c + 1)
                if c >= 2:
                    act.wait_ge(s.u_there, c - 1)
                nc.scalar.activation(cg[:, c % 2, :], m.ps[:, 4 * (c % 2) + 1, :], ACT.Copy).then_inc(s.c_there, 1)

        @block.vector
        def _(dve):
            link = Linked(dve, s.chain)
            dve.wait_ge(s.w_in, 48)
            dve.wait_ge(s.zeroed, 1)
            for c in range(KD):
                b = c % 2
                mid = u_[:, b, W:W + T]
                dve.wait_ge(s.c_there, c + 1)
                nc.vector.tensor_tensor(mid, cg[:, b, :], m.ps[:, 4 * b + 2, :], ALU.mult).then_inc(s.u_there, 1)
                dve.wait_ge(s.u_there, c + 1)
                taps = [cw[:, j, c:c + 1] for j in range(3)]
                a = acc[:, b, :]
                link(nc.vector.tensor_scalar(a, mid, taps[1], None, ALU.mult))
                if c < KD // 2:
                    g = mid.rearrange("p (r w) -> p r w", w=W)
                    ag = a.rearrange("p (r w) -> p r w", w=W)
                    link(nc.vector.scalar_tensor_tensor(out=ag[:, :, 1:W], in0=g[:, :, 0:W - 1], scalar=taps[0],
                                                        in1=ag[:, :, 1:W], op0=ALU.mult, op1=ALU.add))
                    link(nc.vector.scalar_tensor_tensor(out=ag[:, :, 0:W - 1], in0=g[:, :, 1:W], scalar=taps[2],
                                                        in1=ag[:, :, 0:W - 1], op0=ALU.mult, op1=ALU.add))
                else:
                    link(nc.vector.scalar_tensor_tensor(out=a, in0=u_[:, b, 0:T], scalar=taps[0],
                                                        in1=a, op0=ALU.mult, op1=ALU.add))
                    link(nc.vector.scalar_tensor_tensor(out=a, in0=u_[:, b, 2 * W:2 * W + T], scalar=taps[2],
                                                        in1=a, op0=ALU.mult, op1=ALU.add))
                nc.vector.tensor_tensor(yT[:, c, :], a, m.ps[:, 4 * b, :], ALU.mult).then_inc(s.done, 1)
    st.close()


HW = 4 * P
SUB = 16
NS = P // SUB


def mix_columns(m, p, hT, first, kv, after):
    nc, ring = m.nc, m.ring
    st = Stage(m, "mixin")
    s = st.sem("product moved chain lb_in lb_max lb_exp lb")
    lg = st.sb("lb", [P, 6, 4])
    U = []
    for h in range(4):
        U.append((first, h * P, P, True, p.q[:, h, :], ACT.Copy))
    for h in range(4):
        U.append((first + 1, h * P, P, True, p.f[:, h, :], ACT.Sigmoid))
    for t in range(NT):
        U.append((first + 2, 0, 512, t, p.v[:, t, :], ACT.Copy))
    for h in range(4):
        U.append((first + 3, h * P, P, True, p.gate[:, h, :], ACT.Silu))
    for h in range(4):
        U.append((first + 4, h * P, P, True, p.nq[:, h, :], ACT.Copy))
    for c, dst in ((0, p.kc), (P, p.vc), (2 * P, p.ks)):
        U.append((kv, c, P, True, dst[:], ACT.Copy))
    for t in range(NT):
        U.append((kv, 3 * P, P, t, p.vs[:, t, :], ACT.Copy))
    U.append((kv + 1, 0, P, True, p.kw[:], ACT.Copy))
    for t in range(NT):
        U.append((kv + 1, P, P, t, p.vw[:, t, :], ACT.Copy))
    for t in range(NT):
        U.append((kv + 1, 2 * P, 24, t, p.ng[:, t, :], ACT.Sigmoid))
    with st.block() as block:
        @block.sync
        def _(sp):
            for i in range(2):
                sp.dma_start(lg[:, i, :], p.lb_logits[i, :].rearrange("(k p) -> p k", p=P),
                             allow_slow_non_contiguous=True).then_inc(s.lb_in, 16)
            ring.stream(sp, after)

        @block.tensor
        def _(pe):
            for u, (n, c0, width, tile, dst, _) in enumerate(U):
                if u == 0 or U[u - 1][0] != n:
                    ring.wait(pe, n)
                wn = 512 if n < kv + 1 else W_IN2 - 3072
                w = whole(KD, wn)(ring.slot(n))
                if u >= 4:
                    pe.wait_ge(s.moved, u - 3)
                for k in range(KD):
                    if tile is True:
                        last = nc.tensor.matmul(m.ps[:, u % 4, :], w[:, k, c0:c0 + P], hT[:, k, :],
                                                start=(k == 0), stop=(k == KD - 1))
                    else:
                        last = nc.tensor.matmul(m.ps[:, u % 4, 0:width], hT[:, k, tile * P:(tile + 1) * P],
                                                w[:, k, c0:c0 + width], start=(k == 0), stop=(k == KD - 1))
                last.then_inc(s.product, 1)
                if u + 1 == len(U) or U[u + 1][0] != n:
                    pe.wait_ge(s.product, u + 1)
                    pe.sem_inc(ring.freed[n % SLOTS], 1)

        @block.scalar
        def _(act):
            for u, (_, _, width, tile, dst, fn) in enumerate(U):
                act.wait_ge(s.product, u + 1)
                w = T if tile is True else width
                nc.scalar.activation(dst, m.ps[:, u % 4, 0:w], fn).then_inc(s.moved, 1)
            act.wait_ge(s.lb_max, 1)
            nc.scalar.activation(lg[:, 3:5, :], lg[:, 3:5, :], ACT.Exp).then_inc(s.lb_exp, 1)

        @block.vector
        def _(dve):
            link = Linked(dve, s.chain)
            dve.wait_ge(s.lb_in, 32)
            link(nc.vector.tensor_tensor(lg[:, 2, :], lg[:, 0, :], lg[:, 1, :], ALU.max))
            link(nc.vector.tensor_tensor(lg[:, 3, :], lg[:, 0, :], lg[:, 2, :], ALU.subtract))
            nc.vector.tensor_tensor(lg[:, 4, :], lg[:, 1, :], lg[:, 2, :], ALU.subtract).then_inc(s.lb_max, 1)
            dve.wait_ge(s.lb_exp, 1)
            link(nc.vector.tensor_tensor(lg[:, 5, :], lg[:, 3, :], lg[:, 4, :], ALU.add))
            link(nc.vector.reciprocal(lg[:, 5, :], lg[:, 5, :]))
            link(nc.vector.tensor_tensor(lg[:, 3, :], lg[:, 3, :], lg[:, 5, :], ALU.mult))
            link(nc.vector.tensor_scalar(lg[:, 4, :], lg[:, 3, :], -1.0, 1.0, ALU.mult, ALU.add))
            for h in range(4):
                link(nc.vector.tensor_scalar(p.f[:, h, :], p.f[:, h, :], lg[:, 4, h:h + 1], lg[:, 3, h:h + 1],
                                             ALU.mult, ALU.add))
                link(nc.vector.tensor_scalar(p.k[:, h, :], p.f[:, h, :], -1.0, 1.0, ALU.mult, ALU.add))
                link(nc.vector.tensor_scalar(p.q[:, h, :], p.q[:, h, :], P ** -0.5, None, ALU.mult))
    st.close()


def mask(p, name):
    at, n = p.where[name]
    return p.masks[:, at:at + n]


def hgrn_prepare(m, p, mT):
    nc = m.nc
    st = Stage(m, "hgprep")
    wq = st.sb("wq", [P, 4, T])
    dd = st.sb("pair", [P, 2, 4, T])
    rr = st.sb("suffix", [P, 4, T])
    pick = mT[:, 0, 0:2 * SUB - 1]
    s = st.sem("zeroed picks chain paired banded lifted turned moved pool_chain begun stepped carried")
    sub = lambda ap: ap.rearrange("p h (c s) -> p (h c) s", s=SUB)
    doublings = []
    for ap, suffix in ((p.qd[:], False), (p.kd[:], True)):
        new, old = sub(rr[:]), sub(ap)
        for n in (1, 2, 4, 8):
            doublings.append((new, old, n, slice(SUB - n, SUB) if suffix else slice(0, n)))
            new, old = old, new
    with st.block() as block:
        @block.gpsimd
        def _(pool):
            nc.gpsimd.memset(pick, 0.0).then_inc(s.picks, 1)
            pool.wait_ge(s.picks, 1)
            nc.gpsimd.memset(pick[:, SUB - 1:SUB], 1.0).then_inc(s.picks, 1)
            nc.gpsimd.memset(dd[:], 0.0).then_inc(s.zeroed, 1)
            link = Linked(pool, s.pool_chain)
            link(nc.gpsimd.memset(p.kd[:], 1.0))
            link(nc.gpsimd.tensor_copy(sub(p.kd[:])[:, :, 0:SUB - 1], sub(p.f[:])[:, :, 1:SUB]))
            nc.gpsimd.tensor_copy(p.qd[:], p.f[:]).then_inc(s.begun, 1)
            pool.wait_ge(s.begun, 1)
            for i, (new, old, n, rest) in enumerate(doublings):
                if i:
                    pool.wait_ge(s.stepped, i)
                    pool.wait_ge(s.carried, i)
                if i < 4:
                    ins = nc.gpsimd.tensor_tensor(new[:, :, n:SUB], old[:, :, n:SUB], old[:, :, 0:SUB - n], ALU.mult)
                else:
                    ins = nc.gpsimd.tensor_tensor(new[:, :, 0:SUB - n], old[:, :, 0:SUB - n], old[:, :, n:SUB],
                                                  ALU.mult)
                ins.then_inc(s.stepped, 1)
            pool.wait_ge(s.stepped, 8)
            pool.wait_ge(s.carried, 8)
            link(nc.gpsimd.tensor_copy(p.last[:].unsqueeze(2), sub(p.qd[:])[:, :, SUB - 1:SUB]))
            link(nc.gpsimd.tensor_tensor(p.qd[:], p.qd[:], p.q[:], ALU.mult))
            link(nc.gpsimd.tensor_tensor(p.kd[:], p.kd[:], p.k[:], ALU.mult))

        @block.scalar
        def _(act):
            act.wait_ge(s.begun, 1)
            for i, (new, old, n, rest) in enumerate(doublings):
                if i:
                    act.wait_ge(s.stepped, i)
                    act.wait_ge(s.carried, i)
                nc.scalar.activation(new[:, :, rest], old[:, :, rest], ACT.Copy).then_inc(s.carried, 1)

        @block.vector
        def _(dve):
            link = Linked(dve, s.chain)
            link(nc.vector.tensor_copy(wq[:], p.q[:]))
            dve.wait_ge(s.zeroed, 1)
            w, f, k = sub(wq[:]), sub(p.f[:]), sub(p.k[:])
            for d in range(SUB):
                if d:
                    dve.wait_ge(s.paired, d)
                    link(nc.vector.tensor_tensor(w[:, :, d:SUB], w[:, :, d:SUB], f[:, :, 1:SUB - d + 1], ALU.mult))
                if d >= 2:
                    dve.wait_ge(s.banded, d - 1)
                pair = sub(dd[:, d % 2, :, :])
                nc.vector.tensor_tensor(pair[:, :, d:SUB], w[:, :, d:SUB], k[:, :, 0:SUB - d],
                                        ALU.mult).then_inc(s.paired, 1)
            dve.wait_ge(s.banded, SUB)
            nc.vector.tensor_copy(wq[0:SUB, :, :], m.ps[0:SUB, 0:4, :]).then_inc(s.lifted, 1)
            dve.wait_ge(s.turned, 1)
            nc.vector.tensor_copy(p.band[:], m.ps[:, 4, 0:16 * SUB].rearrange("p (u d) -> p u d", d=SUB)
                                  ).then_inc(s.moved, 1)

        @block.tensor
        def _(pe):
            pe.wait_ge(s.picks, 2)
            for d in range(SUB):
                pe.wait_ge(s.paired, d + 1)
                for h in range(4):
                    last = nc.tensor.matmul(m.ps[0:SUB, h, :], pick[:, SUB - 1 - d:2 * SUB - 1 - d],
                                            dd[:, d % 2, h, :], start=(d == 0), stop=(d == SUB - 1))
                last.then_inc(s.banded, 1)
            pe.wait_ge(s.lifted, 1)
            for u in range(16):
                h, t = u // 4, u % 4
                last = nc.tensor.transpose(m.ps[:, 4, u * SUB:(u + 1) * SUB], wq[0:SUB, h, t * P:(t + 1) * P],
                                           m.ident[0:SUB, 0:SUB])
            last.then_inc(s.turned, 1)
    st.close()


def hgrn_scan(m, p, mT):
    nc = m.nc
    st = Stage(m, "hgscan")
    loc = st.sb("local", [P, 16, SUB])
    prod = st.sb("prod", [P, 16, SUB])
    dense = st.sb("dense", [P, 2, P])
    aT = st.sb("aT", [P, 2, P])
    kt = st.sb("kt", [P, 2, P])
    vm = st.sb("vm", [P, 2, NS, P])
    S = st.sb("S", [P, 4, NS + 1, P])
    o = p.q
    g = st.sb("norm", [P, 4])
    s = st.sem("g_in zeroed chain local dense a_turned a_moved k_turned k_moved v_masked kv state o_ps o_moved "
               "square summed root done carried")
    units = [(t, h) for t in range(NT) for h in range(4)]
    with st.block() as block:
        @block.sync
        def _(sp):
            sp.dma_start(g[:], p.hg_norm.rearrange("(k p) -> p k", p=P),
                         allow_slow_non_contiguous=True).then_inc(s.g_in, 16)

        @block.gpsimd
        def _(pool):
            nc.gpsimd.memset(S[:, :, 0, :], 0.0).then_inc(s.zeroed, 1)
            for u, (t, h) in enumerate(units):
                if u >= 2:
                    pool.wait_ge(s.kv, u - 1)
                v = p.v[:, t, h * P:(h + 1) * P]
                nc.gpsimd.tensor_tensor(vm[:, u % 2, :, :], across(v, NS), column(mask(p, "chunk"), NS, P),
                                        ALU.mult).then_inc(s.v_masked, 1)

        @block.vector
        def _(dve):
            link = Linked(dve, s.chain)
            sh = mask(p, "shift").rearrange("p (d s) -> p d s", s=SUB)
            for d in range(SUB):
                dst = loc if d == 0 else prod
                link(nc.vector.tensor_tensor(dst[:], across(sh[:, d, :], 16),
                                             p.band[:, :, d:d + 1].to_broadcast([P, 16, SUB]), ALU.mult))
                if d:
                    link(nc.vector.tensor_tensor(loc[:], loc[:], prod[:], ALU.add))
            dve.wait_ge(s.zeroed, 1)
            sp_ = mask(p, "spread").rearrange("p (c s) -> p c s", s=SUB)
            for u, (t, h) in enumerate(units):
                if u >= 2:
                    dve.wait_ge(s.a_turned, u - 1)
                nc.vector.tensor_tensor(dense[:, u % 2, :].rearrange("p (c s) -> p c s", s=SUB),
                                        across(loc[:, h * 4 + t, :], NS), sp_, ALU.mult).then_inc(s.dense, 1)
                dve.wait_ge(s.kv, u + 1)
                if t:
                    dve.wait_ge(s.o_ps, u - 3)
                    link(nc.vector.tensor_copy(S[:, h, 0, :], S[:, h, NS, :]))
                for c in range(NS):
                    last = nc.vector.scalar_tensor_tensor(
                        out=S[:, h, c + 1, :], in0=S[:, h, c, :], scalar=p.last[:, h * 32 + t * NS + c:h * 32 + t * NS + c + 1],
                        in1=m.ps[:, (u % 2) * 2 + c // 4, (c % 4) * P:(c % 4 + 1) * P], op0=ALU.mult, op1=ALU.add)
                    if c < NS - 1:
                        link(last)
                last.then_inc(s.state, 1)
                dve.wait_ge(s.state, u + 1)
            for h in range(4):
                dve.wait_ge(s.o_moved, 13 + h)
                nc.vector.tensor_tensor(p.qd[:, h, :], o[:, h, :], o[:, h, :], ALU.mult).then_inc(s.square, 1)
            dve.wait_ge(s.g_in, 16)
            for h in range(4):
                r = p.kd[:, h, :]
                dve.wait_ge(s.root, h + 1)
                link(nc.vector.reciprocal(r, r))
                link(nc.vector.tensor_tensor(r, r, o[:, h, :], ALU.mult))
                nc.vector.scalar_tensor_tensor(out=mT[:, h, :], in0=r, scalar=g[:, h:h + 1], in1=p.gate[:, h, :],
                                               op0=ALU.mult, op1=ALU.mult).then_inc(s.done, 1)

        @block.scalar
        def _(act):
            def move_out(u):
                t, h = units[u]
                act.wait_ge(s.o_ps, u + 1)
                nc.scalar.activation(o[:, h, t * P:(t + 1) * P], m.ps[:, 6 + u % 2, 0:P], ACT.Copy).then_inc(s.o_moved, 1)

            for u, (t, h) in enumerate(units):
                act.wait_ge(s.k_turned, u + 1)
                if u >= 2:
                    act.wait_ge(s.kv, u - 1)
                nc.scalar.activation(kt[:, u % 2, :], m.ps[:, 4, 0:P], ACT.Copy).then_inc(s.k_moved, 1)
                act.wait_ge(s.a_turned, u + 1)
                if u >= 2:
                    act.wait_ge(s.o_ps, u - 1)
                nc.scalar.activation(aT[:, u % 2, :], m.ps[:, 5, 0:P], ACT.Copy).then_inc(s.a_moved, 1)
                if u:
                    move_out(u - 1)
            move_out(len(units) - 1)
            for h in range(4):
                act.wait_ge(s.summed, h + 1)
                nc.scalar.activation(p.kd[:, h, :], m.ps[:, h, :], ACT.Sqrt, bias=m.eps[:],
                                     scale=1.0 / P).then_inc(s.root, 1)

        @block.tensor
        def _(pe):
            def turn(u):
                t, h = units[u]
                if u:
                    pe.wait_ge(s.k_moved, u)
                nc.tensor.transpose(m.ps[:, 4, 0:P], p.kd[:, h, t * P:(t + 1) * P], m.ident).then_inc(s.k_turned, 1)
                pe.wait_ge(s.dense, u + 1)
                if u:
                    pe.wait_ge(s.a_moved, u)
                nc.tensor.transpose(m.ps[:, 5, 0:P], dense[:, u % 2, :], m.ident).then_inc(s.a_turned, 1)

            def outer(u):
                pe.wait_ge(s.k_moved, u + 1)
                pe.wait_ge(s.v_masked, u + 1)
                if u >= 2:
                    pe.wait_ge(s.state, u - 1)
                for q in range(2):
                    last = nc.tensor.matmul(m.ps[:, (u % 2) * 2 + q, :], kt[:, u % 2, :],
                                            flat(vm[:, u % 2, 4 * q:4 * q + 4, :]), start=True, stop=True)
                last.then_inc(s.kv, 1)

            def output(u):
                t, h = units[u]
                pe.wait_ge(s.a_moved, u + 1)
                pe.wait_ge(s.state, u + 1)
                if u >= 2:
                    pe.wait_ge(s.o_moved, u - 1)
                out = m.ps[:, 6 + u % 2, 0:P]
                nc.tensor.matmul(out, p.v[:, t, h * P:(h + 1) * P], aT[:, u % 2, :], start=True, stop=False)
                for c in range(NS):
                    last = nc.tensor.matmul(out[:, c * SUB:(c + 1) * SUB], S[:, h, c, :],
                                            p.qd[:, h, t * P + c * SUB:t * P + (c + 1) * SUB],
                                            start=False, stop=(c == NS - 1))
                last.then_inc(s.o_ps, 1)

            for u in range(len(units)):
                turn(u)
                outer(u)
                if u:
                    output(u - 1)
            output(len(units) - 1)
            for h in range(4):
                pe.wait_ge(s.square, h + 1)
                nc.tensor.matmul(m.ps[:, h, :], m.ones, p.qd[:, h, :], start=True, stop=True).then_inc(s.summed, 1)
    st.close()


NC = 31


def compress_stage(m, p, first, after):
    nc, ring = m.nc, m.ring
    st = Stage(m, "cmp")
    pos = st.sb("pos", [P, 2, 32])
    xin = st.sb("xin", [P, 2, 32, NC])
    b1 = st.sb("b1", [1, 2, 256])
    w2 = st.sb("w2", [P, 2, 2, 2, 64])
    g = st.sb("g", [NC, 4, 2, 256])
    gT = st.sb("gT", [P, 4, 2, NC])
    s = st.sem("in_ chain xin product moved tanh gelu turned t_moved final f_moved")
    units = [(x, gr) for x in range(2) for gr in range(2)]
    with st.block() as block:
        @block.sync
        def _(sp):
            for x in range(2):
                for half in range(2):
                    sp.dma_start(pos[64 * half:64 * half + 64, x, :], p.pos[x].rearrange("l d -> d l"),
                                 allow_slow_non_contiguous=True).then_inc(s.in_, 16)
                    sp.dma_start(w2[:, x, :, half, :], p.w2[x].rearrange("(k p) d -> p k d", p=P)).then_inc(s.in_, 16)
                sp.dma_start(b1[:, x, :], p.b1[x].unsqueeze(0)).then_inc(s.in_, 16)
            ring.stream(sp, after)

        @block.vector
        def _(dve):
            link = Linked(dve, s.chain)
            dve.wait_ge(s.in_, 160)
            for x, src in enumerate((p.kc, p.vc)):
                for l in range(32):
                    tok = src[:, l:l + 16 * (NC - 1) + 1:16]
                    last = nc.vector.tensor_scalar(xin[:, x, l, :], tok, pos[:, x, l:l + 1], None, ALU.add)
                last.then_inc(s.xin, 1)
            for u in range(4):
                a, b = g[:, u, 0, :], g[:, u, 1, :]
                dve.wait_ge(s.product, u + 1)
                link(nc.vector.tensor_copy(a, m.ps[0:NC, u, 0:256]))
                link(nc.vector.tensor_tensor(b, a, a, ALU.mult))
                link(nc.vector.tensor_scalar(b, b, 0.044715, 1.0, ALU.mult, ALU.add))
                nc.vector.tensor_tensor(b, b, a, ALU.mult).then_inc(s.moved, 1)
                dve.wait_ge(s.tanh, u + 1)
                nc.vector.tensor_tensor(a, a, b, ALU.mult).then_inc(s.gelu, 1)

        @block.scalar
        def _(act):
            for u in range(4):
                act.wait_ge(s.moved, u + 1)
                nc.scalar.activation(g[:, u, 1, :], g[:, u, 1, :], ACT.Sigmoid,
                                     scale=2.0 * (2.0 / np.pi) ** 0.5).then_inc(s.tanh, 1)
            for u in range(4):
                act.wait_ge(s.turned, u + 1)
                nc.scalar.activation(gT[:, u, :, :],
                                     m.ps[:, 4 + u, 0:2 * NC].rearrange("p (k c) -> p k c", k=2),
                                     ACT.Copy).then_inc(s.t_moved, 1)
            for u, (x, gr) in enumerate(units):
                act.wait_ge(s.final, u + 1)
                if x == 0:
                    nc.scalar.activation(p.kcmp[:, gr, :], m.ps[:, u, 0:NC], ACT.Copy).then_inc(s.f_moved, 1)
                else:
                    nc.scalar.activation(p.vpad_c[:, gr, 64:128], m.ps[0:NC, u, 0:64], ACT.Copy).then_inc(s.f_moved, 1)

        @block.tensor
        def _(pe):
            pe.wait_ge(s.in_, 160)
            for x in range(2):
                pe.wait_ge(s.xin, x + 1)
                for gr in range(2):
                    u, rows = 2 * x + gr, slice(64 * gr, 64 * gr + 64)
                    for half in range(2):
                        n = first + 2 * x + half
                        if gr == 0:
                            ring.wait(pe, n)
                        w = ring.slot(n)[rows, :].rearrange("p (l n) -> p l n", l=16)
                        for l in range(16):
                            nc.tensor.matmul(m.ps[0:NC, u, 0:256], xin[rows, x, 16 * half + l, :], w[:, l, :],
                                             start=(half == 0 and l == 0), stop=False)
                    last = nc.tensor.matmul(m.ps[0:NC, u, 0:256], m.ones[0:1, 0:NC], b1[0:1, x, :],
                                            start=False, stop=True)
                    last.then_inc(s.product, 1)
                pe.wait_ge(s.product, 2 * x + 2)
                for half in range(2):
                    pe.sem_inc(ring.freed[(first + 2 * x + half) % SLOTS], 1)
            for u in range(4):
                pe.wait_ge(s.gelu, u + 1)
                for k in range(2):
                    last = nc.tensor.transpose(m.ps[:, 4 + u, k * NC:(k + 1) * NC], g[:, u, 0, k * P:(k + 1) * P],
                                               m.ident[0:NC, 0:NC])
                last.then_inc(s.turned, 1)
            for u, (x, gr) in enumerate(units):
                pe.wait_ge(s.t_moved, u + 1)
                for k in range(2):
                    if x == 0:
                        last = nc.tensor.matmul(m.ps[:, u, 0:NC], flat(w2[:, 0, k, :, :]), gT[:, u, k, :],
                                                start=(k == 0), stop=(k == 1))
                    else:
                        last = nc.tensor.matmul(m.ps[0:NC, u, 0:64], gT[:, u, k, :], w2[:, 1, k, 0, :],
                                                start=(k == 0), stop=(k == 1))
                last.then_inc(s.final, 1)
    st.close()


def rope_stage(m, p):
    nc = m.nc
    st = Stage(m, "rope")
    tmp = st.sb("tmp", [P, 2, T])
    s = st.sem("zeroed vals rotated mixed added krot dup moved")
    src = [p.nq[:, c, :] for c in range(4)] + [p.ks[:], p.kw[:]]
    dst = [p.qr[:, c, :] for c in range(4)] + [p.kc[:], p.vc[:]]
    with st.block() as block:
        @block.gpsimd
        def _(pool):
            nc.gpsimd.memset(p.vpad[:], 0.0).then_inc(s.zeroed, 1)
            pool.wait_ge(s.zeroed, 1)
            for i, v in enumerate((p.vs, p.vw)):
                for t in range(NT):
                    nc.gpsimd.tensor_copy(p.vpad[:, i, t, :, 64:128],
                                          v[:, t, :].rearrange("p (g d) -> p g d", g=2)).then_inc(s.vals, 1)
            pool.wait_ge(s.vals, 2 * NT)

        @block.tensor
        def _(pe):
            for u in range(6):
                if u >= 2:
                    pe.wait_ge(s.mixed, u - 1)
                nc.tensor.matmul(m.ps[:, u % 2, :], mask(p, "rot"), src[u], start=True, stop=True).then_inc(s.rotated, 1)
            for i in range(2):
                pe.wait_ge(s.added, 5 + i)
                for g in range(2):
                    nc.tensor.matmul(m.ps[:, 2 + 2 * i + g, :], mask(p, f"dup{g}"), dst[4 + i],
                                     start=True, stop=True).then_inc(s.dup, 1)

        @block.scalar
        def _(act):
            for i in range(2):
                for g in range(2):
                    act.wait_ge(s.dup, 2 * i + g + 1)
                    nc.scalar.activation(p.kr[:, i, g, :], m.ps[:, 2 + 2 * i + g, :], ACT.Copy).then_inc(s.moved, 1)

        @block.vector
        def _(dve):
            for u in range(6):
                dve.wait_ge(s.rotated, u + 1)
                nc.vector.tensor_tensor(tmp[:, u % 2, :], m.ps[:, u % 2, :], mask(p, "sin"), ALU.mult).then_inc(s.mixed, 1)
                nc.vector.tensor_tensor(dst[u], src[u], mask(p, "cos"), ALU.mult).then_inc(s.krot, 1)
                dve.wait_ge(s.mixed, u + 1)
                dve.wait_ge(s.krot, u + 1)
                nc.vector.tensor_tensor(dst[u], dst[u], tmp[:, u % 2, :], ALU.add).then_inc(s.added, 1)
                dve.wait_ge(s.added, u + 1)
    st.close()


def attention_stage(m, p, mT):
    nc = m.nc
    st = Stage(m, "attn")
    NB = 3
    pr = st.sb("probs", [P, NB, T])
    pT = st.sb("probsT", [P, 2, NT, P])
    c = st.sb("cols", [P, NB, 4])
    s = st.sem("score top ntop exp total scaled turned t_moved out o_moved masked")
    units = [(c2, t, h, b) for c2 in range(4) for t in range(NT) for h in range(2) for b in range(3)]

    def width(u):
        return NC if units[u][3] == 2 else (units[u][1] + 1) * P

    with st.block() as block:
        @block.tensor
        def _(pe):
            def scores(u):
                c2, t, h, b = units[u]
                g, rows, w = c2 // 2, slice(64 * h, 64 * h + 64), width(u)
                if u >= 3:
                    pe.wait_ge(s.exp, u - 2)
                ps = m.ps[:, u % 3, :]
                if b == 2:
                    nc.tensor.matmul(ps[:, 0:NC], p.nq[rows, c2, t * P:(t + 1) * P], p.kcmp[rows, g, :],
                                     start=True, stop=False)
                    last = nc.tensor.matmul(ps[:, 0:NC], m.ident, mask(p, "cneg")[:, t * NC:(t + 1) * NC],
                                            start=False, stop=True)
                else:
                    nc.tensor.matmul(ps[:, 0:w], p.qr[rows, c2, t * P:(t + 1) * P], p.kr[rows, b, g, 0:w],
                                     start=True, stop=False)
                    last = nc.tensor.matmul(ps[:, w - P:w], m.ident, mask(p, "causal"), start=False, stop=True)
                last.then_inc(s.score, 1)

            def turn(u):
                w = width(u)
                pe.wait_ge(s.scaled, u + 1)
                if u >= 2:
                    pe.wait_ge(s.t_moved, u - 1)
                for j in range(0, w, P):
                    n = min(P, w - j)
                    last = nc.tensor.transpose(m.ps[0:n, 3 + u % 2, j:j + P], pr[:, u % NB, j:j + n], m.ident)
                last.then_inc(s.turned, 1)

            def values(u):
                c2, t, h, b = units[u]
                g, o = c2 // 2, u // 6
                pe.wait_ge(s.t_moved, u + 1)
                first, final = u % 6 == 0, u % 6 == 5
                if first and o >= 2:
                    pe.wait_ge(s.o_moved, o - 1)
                ps = m.ps[:, 6 + o % 2, 0:P]
                lo = 64 if h == 0 else 0
                if b == 2:
                    last = nc.tensor.matmul(ps, p.vpad_c[:, g, lo:lo + P], pT[0:NC, u % 2, 0, :],
                                            start=first, stop=final)
                else:
                    for j in range(t + 1):
                        last = nc.tensor.matmul(ps, p.vpad[:, b, j, g, lo:lo + P], pT[:, u % 2, j, :],
                                                start=(first and j == 0), stop=final)
                last.then_inc(s.out, 1)

            n = len(units)
            for u in range(n + 2):
                if u < n:
                    scores(u)
                if 1 <= u <= n:
                    turn(u - 1)
                if u >= 2:
                    values(u - 2)

        @block.vector
        def _(dve):
            for u, (c2, t, h, b) in enumerate(units):
                w = width(u)
                k = c[:, u % NB, :]
                dve.wait_ge(s.score, u + 1)
                nc.vector.tensor_reduce(k[:, 0:1], m.ps[:, u % 3, 0:w], AX_X, ALU.max).then_inc(s.top, 1)
                dve.wait_ge(s.top, u + 1)
                if u >= NB:
                    dve.wait_ge(s.exp, u - NB + 1)
                nc.vector.tensor_scalar(k[:, 1:2], k[:, 0:1], -0.125, None, ALU.mult).then_inc(s.ntop, 1)
                dve.wait_ge(s.exp, u + 1)
                nc.vector.reciprocal(k[:, 3:4], k[:, 2:3]).then_inc(s.total, 1)
                gate = p.ng[:, t, 3 * (2 * c2 + h) + (1, 2, 0)[b]:3 * (2 * c2 + h) + (1, 2, 0)[b] + 1]
                dve.wait_ge(s.total, u + 1)
                if b == 2:
                    nc.vector.tensor_tensor(pr[:, u % NB, 0:w], pr[:, u % NB, 0:w],
                                            mask(p, "cok")[:, t * NC:(t + 1) * NC], ALU.mult).then_inc(s.masked, 1)
                    dve.wait_ge(s.masked, u // 3 + 1)
                nc.vector.tensor_scalar(pr[:, u % NB, 0:w], pr[:, u % NB, 0:w], k[:, 3:4], gate,
                                        ALU.mult, ALU.mult).then_inc(s.scaled, 1)

        @block.scalar
        def _(act):
            def move(u):
                c2, t, h, b = units[u]
                w = width(u)
                n = min(P, w)
                act.wait_ge(s.turned, u + 1)
                if u >= 2:
                    act.wait_ge(s.out, u - 1)
                src = m.ps[0:n, 3 + u % 2, 0:max(w, P)].rearrange("p (j c) -> p j c", c=P)
                nc.scalar.activation(pT[0:n, u % 2, 0:max(w, P) // P, :], src, ACT.Copy).then_inc(s.t_moved, 1)

            def out(o):
                c2, t = units[6 * o][0:2]
                act.wait_ge(s.out, 6 * o + 6)
                nc.scalar.activation(mT[:, 4 + c2, t * P:(t + 1) * P], m.ps[:, 6 + o % 2, 0:P],
                                     ACT.Copy).then_inc(s.o_moved, 1)

            n = len(units)
            for u in range(n + 2):
                if u < n:
                    w = width(u)
                    act.wait_ge(s.ntop, u + 1)
                    if u >= NB:
                        act.wait_ge(s.turned, u - NB + 1)
                        act.wait_ge(s.total, u - NB + 1)
                    nc.scalar.activation(pr[:, u % NB, 0:w], m.ps[:, u % 3, 0:w], ACT.Exp, bias=c[:, u % NB, 1:2],
                                         scale=0.125, accum_out=c[:, u % NB, 2:3]).then_inc(s.exp, 1)
                if 1 <= u <= n:
                    move(u - 1)
                if u >= 2 and (u - 2) % 6 == 5:
                    out((u - 2) // 6)
    st.close()


def setup_stage(m, a):
    nc = m.nc
    st = Stage(m, "setup")
    s = st.sem("in_ eps")
    with st.block() as block:
        @block.sync
        def _(sp):
            sp.dma_start(m.base[:], a["c_base"][:, 0:2, :]).then_inc(s.in_, 16)
            sp.dma_start(m.before, a["c_before"]).then_inc(s.in_, 16)
            sp.dma_start(m.x[:], a["x"][0].rearrange("(t p) d -> p t d", p=P)).then_inc(s.in_, 16)
            m.ring.stream(sp, SLOTS)
            sp.wait_ge(s.in_, 48)

        @block.gpsimd
        def _(pool):
            nc.gpsimd.memset(m.eps[:], EPS).then_inc(s.eps, 1)
            pool.wait_ge(s.eps, 1)
    st.close()


def simple_load(m, tag, pairs, zero=()):
    nc = m.nc
    st = Stage(m, f"load{tag}")
    s = st.sem("in_ zero")
    with st.block() as block:
        @block.sync
        def _(sp):
            for dst, src in pairs:
                sp.dma_start(dst, src, allow_slow_non_contiguous=True).then_inc(s.in_, 16)
            sp.wait_ge(s.in_, 16 * len(pairs))

        @block.gpsimd
        def _(pool):
            for z in zero:
                nc.gpsimd.memset(z, 0.0).then_inc(s.zero, 1)
            if zero:
                pool.wait_ge(s.zero, len(zero))
    st.close()


def plan_weights(m, a):
    ring, at = m.ring, {}

    def columns(name, w, c0, n=512, k=KD):
        return ring.add([(whole(k, n), rows_of(w, c0, n))])

    def ada(name, w):
        at[name] = [columns(name, w, 512 * i) for i in range(12)][0]

    def experts(name, w1, w3, w2):
        at[name] = len(ring.tiles)
        for e in range(0, E1, 2):
            columns(name, w1[e], 0)
            columns(name, w3[e], 0)
            columns(name, w2[e], 0, D, 4)

    ada("mod0", a["ada_w"][0])
    w = a["w_in_a"][0]
    for hg in range(2):
        at[f"heads{hg}"] = len(ring.tiles)
        for kind in range(3):
            columns("", w, kind * D + hg * 512)
    at["z"] = len(ring.tiles)
    for h in range(2):
        columns("", w, 3 * D + h * 512)
    at["out0"] = len(ring.tiles)
    for h in range(2):
        columns("", a["w_out_a"][0], h * 512)
    experts("moe0", a["w1"][0], a["w3"][0], a["w2"][0])
    ada("mod1", a["ada_w"][1])
    at["conv"] = len(ring.tiles)
    for half in range(2):
        for j in range(3):
            columns("", a["w_in_b"][0], j * D + half * 512)
    at["out1"] = len(ring.tiles)
    for h in range(2):
        columns("", a["w_out_b"][0], h * 512)
    experts("moe1", a["w1"][1], a["w3"][1], a["w2"][1])
    ada("mod2", a["w_ada_2"][0])
    w = a["w_in_2"][0]
    at["mix"] = len(ring.tiles)
    for c in range(5):
        columns("", w, 512 * c)
    at["kv"] = len(ring.tiles)
    columns("", w, 2560)
    columns("", w, 3072, W_IN2 - 3072)
    at["cmp"] = len(ring.tiles)
    for x in "kv":
        w1 = a[f"cmp_w1_{x}_2"][0].rearrange("(l d) n -> d l n", d=64)
        for half in range(2):
            src = w1[:, 16 * half:16 * half + 16, :]
            ring.add([(lambda s, g=g: s[64 * g:64 * g + 64, :].rearrange("p (l n) -> p l n", l=16), src)
                      for g in range(2)])
    at["out2"] = len(ring.tiles)
    for h in range(2):
        columns("", a["w_out_2"][0], h * 512)
    at["moe2"] = len(ring.tiles)
    columns("", a["w_sh_gu_2"][0], 0)
    columns("", a["w_sh_dn_2"][0], 0, D, 2)
    for e in range(0, E2 // 2, 2):
        columns("", a["w_exp_gu_2"][0, 2 * e], 0)
        columns("", a["w_exp_gu_2"][0, 2 * e + 1], 0)
        ring.add([(whole(4, D), a["w_exp_dn_2"][0, 2 * e:2 * e + 2].rearrange("o (k p) n -> p (o k) n", p=P))])
    return at


def build(nc, a, out):
    ctx = ExitStack()
    m = Bag()
    m.nc = nc
    with ctx:
        m.ring = WeightRing(nc, ctx)
        m.x = ctx.enter_context(nc.sbuf_tensor("x_resident", [P, NT, D], F32))
        m.mod = ctx.enter_context(nc.sbuf_tensor("modulation", [P, 6 * D], F32))
        m.base = ctx.enter_context(nc.sbuf_tensor("base", [P, 2, P], F32))
        m.beforeb = ctx.enter_context(nc.sbuf_tensor("before", [P, 64], F32))
        m.rows_blank = ctx.enter_context(nc.semaphore("rows_blank"))
        m.expert_rows = nc.dram_tensor("expert_rows", [UNITS2 * P, D], F32).ap()
        m.eps = ctx.enter_context(nc.sbuf_tensor("eps", [P, 1], F32))
        m.ps = ctx.enter_context(nc.psum_tensor("ps", [P, 8, 512], F32))
        m.ident, m.ones = [m.base[:, i, :] for i in range(2)]
        m.earlier = a["c_base"][:, 2, :]
        m.before, m.ids = m.beforeb[:, :], a["c_ids"]
        at = plan_weights(m, a)
        m.where = mix_masks()[1]
        xt = [m.x[:, t, :] for t in range(NT)]
        mod = [m.mod[:, i * D:(i + 1) * D] for i in range(6)]
        setup_stage(m, a)
        dctx = ExitStack()
        def dsb(name, shape):
            return dctx.enter_context(nc.sbuf_tensor(f"delta_{name}", shape, F32))
        hx = dsb("hx", [P, KD, CT + T])
        p = Bag()
        p.masks, p.conv, p.o = dsb("masks", [P, 20, P]), dsb("conv", [P, 3, 24]), dsb("o", [P, NT, D])
        nt = NCT + NT
        p.cum, p.ncum, p.g, p.egc, p.ekd, p.egl, p.beta, p.bege = [
            dsb(g, [P, nt, 16]) for g in ("cum", "ncum", "g", "egc", "ekd", "egl", "beta", "bege")]
        p.onorm = a["onorm_a"][0]
        with nc.sbuf_tensor("ctx_tiles", [P, NCT, D], F32) as xc, nc.sbuf_tensor("ctx_mod", [P, 2 * D], F32) as mc:
            modulation_stage(m, 0, [(a["c"][0], m.mod, 12), (a["c_ctx"], mc, 4)], at["mod0"],
                             a["ada_b"][0], at["mod0"] + 12 + SLOTS)
            simple_load(m, "ctx", [(xc[:], a["ctx"][0].rearrange("(t p) d -> p t d", p=P)),
                                   (p.masks[:], a["c_delta"])] +
                        [(p.conv[:, j, :], a["conv_a"][0, j, :].rearrange("(k p) -> p k", p=P)) for j in range(3)],
                        [p.o[:]])
            prepare_stage(m, 0, [(xt, mod[0], mod[1], hx, CT, None),
                                 ([xc[:, t, :] for t in range(NCT)], mc[:, 0:D], mc[:, D:2 * D], hx, 0, None)],
                          a["norm_mix"][0], 0)
        delta_gates(m, hx, p, a["w_in_a"][0][:, 4 * D:4 * D + 32],
                    a["a_log_a"][0].rearrange("a b -> (a b)"), a["dt_bias_a"][0].rearrange("a b -> (a b)"))
        for hg in range(2):
            with nc.sbuf_tensor(f"qT{hg}", [P, 4, T], F32) as p.qT, nc.sbuf_tensor(f"kT{hg}", [P, 4, SPAN], F32) as p.kT,                     nc.sbuf_tensor(f"k{hg}", [P, nt, 512], F32) as p.k, nc.sbuf_tensor(f"v{hg}", [P, nt, 512], F32) as p.v:
                delta_heads(m, hg, hx, p, at[f"heads{hg}"], at[f"heads{hg}"] + 6)
                delta_scan(m, hg, p)
        with nc.sbuf_tensor("oT0", [P, KD, T], F32) as oT:
            p.oT = oT
            delta_finish(m, hx, p, at["z"], at["z"] + 5)
            simple_load(m, "x", [(m.x[:], a["x"][0].rearrange("(t p) d -> p t d", p=P))])
            project_stage(m, 0, oT, at["out0"], mod[2], at["out0"] + 5)
        dctx.close()

        def moe(layer, first):
            n_exp, top, units = (E1, TOP1, UNITS1) if layer < 2 else (E2, TOP2, UNITS2)
            with ExitStack() as c:
                def sb(name, shape, dt=F32):
                    return c.enter_context(nc.sbuf_tensor(f"moe_{name}{layer}", shape, dt))
                y, wt, sel = sb("y", [P, NT, D]), sb("wt", [P, NT, n_exp]), sb("sel", [P, NT, n_exp])
                r = Bag()
                r.units = units
                r.start = sb("start", [1, n_exp + 1], mybir.dt.int32)
                r.slot_token = sb("slot_token", [P, units + 2], U32)
                r.dest, r.share = sb("dest", [P, NT, top], U32), sb("share", [P, NT, top])
                hidden = nc.dram_tensor(f"hidden{layer}", [T, D], F32).ap()
                rows = m.expert_rows[0:units * P, :]
                with nc.sbuf_tensor(f"moe_hT{layer}", [P, KD, T], F32) as hT:
                    gain = a["norm_ffn"][layer] if layer < 2 else a["norm2_g_2"][0]
                    prepare_stage(m, f"f{layer}", [(xt, mod[3], mod[4], hT, 0, hidden)], gain, 0)
                    if layer < 2:
                        route_groups_stage(m, layer, hT, a["router_g"][layer], a["router_e"][layer], wt[:], sel[:], 0)
                    else:
                        route_sigmoid_stage(m, layer, hT, a["router_w_2"][0], a["router_bias_2"][0], wt[:], sel[:], 0)
                        shared_expert_stage(m, hT, y, first, first + 5)
                        first += 2
                    dispatch_stage(m, layer, hT, sel[:], wt[:], n_exp, top, units, r, 0)
                if layer < 2:
                    w = (a["w1"][layer], a["w3"][layer], a["w2"][layer])

                    def source(g, j):
                        return w[j][bass.ds(g, 1), :, :].rearrange("o (k p) n -> p (o k) n", p=P)
                    sparse_experts_stage(m, layer, first, E1, 1, F1, hidden, rows, r, source,
                                         first + 3 * (E1 // 2) + SLOTS)
                else:
                    def source(g, j):
                        w = a["w_exp_gu_2"][0] if j < 2 else a["w_exp_dn_2"][0]
                        at_ = bass.ds(2 * g + j, 1) if j < 2 else bass.ds(2 * g, 2)
                        return w[at_, :, :].rearrange("o (k p) n -> p (o k) n", p=P)
                    sparse_experts_stage(m, layer, first, E2 // 2, 2, F2, hidden, rows, r, source, 10 ** 6)
                combine_stage(m, layer, top, rows, r, y, layer < 2, 0)
                residual_stage(m, layer, y, mod[5], 0, *([], [a["final_norm"]], [a["final_g_2"], out[0]])[layer])

        moe(0, at["moe0"])
        modulation_stage(m, 1, [(a["c"][0], m.mod, 12)], at["mod1"], a["ada_b"][1], at["mod1"] + 12 + SLOTS)
        with nc.sbuf_tensor("hT1", [P, KD, T], F32) as hT, nc.sbuf_tensor("yT1", [P, KD, T], F32) as yT:
            prepare_stage(m, 1, [(xt, mod[0], mod[1], hT, 0, None)], a["norm_mix"][1], 0)
            shortconv_stage(m, hT, yT, at["conv"], a["conv_b"][0], at["conv"] + 9)
            project_stage(m, 1, yT, at["out1"], mod[2], at["out1"] + 5)
        moe(1, at["moe1"])
        modulation_stage(m, 2, [(a["c_2"][0], m.mod, 12)], at["mod2"], a["b_ada_2"][0], at["mod2"] + 12 + SLOTS)
        xctx = ExitStack()
        mT = xctx.enter_context(nc.sbuf_tensor("mT", [P, KD, T], F32))
        q = Bag()
        q.where, q.lb_logits, q.hg_norm = m.where, a["hg_lb_logits_2"], a["hg_norm_g_2"][0]
        q.pos, q.b1, q.w2 = [[a[f"cmp_{w}_{x}_2"][0] for x in "kv"] for w in ("pos", "b1", "w2")]

        def xsb(c, name, shape):
            return c.enter_context(nc.sbuf_tensor(f"mix_{name}", shape, F32))
        q.masks = xsb(xctx, "masks", [P, a["c_mix"].shape[1]])
        q.nq = xsb(xctx, "nq", [P, 4, T])
        q.kc, q.vc, q.ks, q.kw = [xsb(xctx, n, [P, T]) for n in ("kc", "vc", "ks", "kw")]
        q.vs, q.vw, q.ng = xsb(xctx, "vs", [P, NT, P]), xsb(xctx, "vw", [P, NT, P]), xsb(xctx, "ng", [P, NT, 24])
        hctx = ExitStack()
        q.q, q.f, q.k, q.gate = [xsb(hctx, n, [P, 4, T]) for n in ("hq", "hf", "hk", "hgate")]
        q.v = xsb(hctx, "v", [P, NT, HW])
        with nc.sbuf_tensor("hT2", [P, KD, T], F32) as hT:
            prepare_stage(m, 2, [(xt, mod[0], mod[1], hT, 0, None)], a["norm1_g_2"][0], 0)
            spill = nc.dram_tensor("x_spill", [P, NT, D], F32).ap()
            simple_load(m, "mix", [(q.masks[:], a["c_mix"]), (spill, m.x[:])])
            mix_columns(m, q, hT, at["mix"], at["kv"], at["kv"] + 2 + SLOTS)
        q.band, q.last = xsb(hctx, "band", [P, 16, SUB]), xsb(hctx, "last", [P, 128])
        q.qd = m.x[:, 0:2, :].rearrange("p a b -> p (a b)").rearrange("p (h t) -> p h t", h=4)
        q.kd = m.x[:, 2:4, :].rearrange("p a b -> p (a b)").rearrange("p (h t) -> p h t", h=4)
        hgrn_prepare(m, q, mT)
        hgrn_scan(m, q, mT)
        hctx.close()
        simple_load(m, "x2", [(m.x[:], spill)])
        q.kcmp, q.vpad_c = xsb(xctx, "kcmp", [P, 2, NC]), xsb(xctx, "vpadc", [NC, 2, 192])
        simple_load(m, "vpadc", [], [q.vpad_c[:]])
        compress_stage(m, q, at["cmp"], at["cmp"] + 7)
        q.qr, q.kr = xsb(xctx, "qr", [P, 4, T]), xsb(xctx, "kr", [P, 2, 2, T])
        q.vpad = xsb(xctx, "vpad", [P, 2, NT, 2, 192])
        rope_stage(m, q)
        attention_stage(m, q, mT)
        project_stage(m, 2, mT, at["out2"], mod[2], at["out2"] + 5)
        xctx.close()
        moe(2, at["moe2"])


INPUTS = ["x", "c", "ctx", "c_ctx", "ada_w", "ada_b", "norm_mix", "norm_ffn", "w_in_a", "conv_a", "a_log_a",
          "dt_bias_a", "onorm_a", "w_out_a", "w_in_b", "conv_b", "w_out_b", "router_g", "router_e", "w1", "w3", "w2",
          "final_norm", "c_2", "w_ada_2", "b_ada_2", "norm1_g_2", "w_in_2", "hg_lb_logits_2", "hg_norm_g_2",
          "cmp_pos_k_2", "cmp_w1_k_2", "cmp_b1_k_2", "cmp_w2_k_2", "cmp_pos_v_2", "cmp_w1_v_2", "cmp_b1_v_2",
          "cmp_w2_v_2", "w_out_2", "norm2_g_2", "router_w_2", "router_bias_2", "w_exp_gu_2", "w_exp_dn_2",
          "w_sh_gu_2", "w_sh_dn_2", "final_g_2"]


def host_constants():
    before = (np.arange(8)[None, :] < np.arange(8)[:, None]).astype(np.float32).reshape(1, 64)
    return {"c_base": base_masks(), "c_before": np.tile(before, (P, 1)), "c_delta": delta_masks(),
            "c_ids": np.arange(T, dtype=np.float32).reshape(NT, P).T.copy(), "c_mix": mix_masks()[0]}


def kernel(**inputs):
    import concourse.bacc as bacc
    from concourse.bass_utils import run_bass_kernel_spmd as run

    nc = bacc.Bacc("TRN2", target_bir_lowering=False, num_devices=1)
    arrays, args = {}, {}
    for name, v in [(n, inputs[n]) for n in INPUTS] + list(host_constants().items()):
        v = np.ascontiguousarray(v)
        arrays[f"in_{name}_dram"] = v
        args[name] = nc.dram_tensor(f"in_{name}_dram", v.shape, mybir.dt.from_np(v.dtype), kind="ExternalInput").ap()
    out = nc.dram_tensor("out_0_dram", (1, T, D), F32, kind="ExternalOutput").ap()
    build(nc, args, out)
    r = run(nc, [arrays], core_ids=[0])
    return r.results[0]["out_0_dram"]
```
